# Optimizing a Trainium2 kernel written in Bass

```python
import math
import jax
import jax.numpy as jnp
from jax import lax
import numpy as np

D_MODEL = 1024
BATCH = 1
SEQ = 256
DEPTH = 2
DEC_BATCH = 8
DEC_SEQ = 1
PAST_LEN = 2048
PAGE_SIZE = 128

MIX_WIDTH = D_MODEL
BRANCH = MIX_WIDTH // 4
S5_CH = 16
S5_GROUPS = BRANCH // S5_CH
S5_STATE = 64
HG_HEADS = 4
HG_DK = BRANCH // HG_HEADS
HG_DV = BRANCH // HG_HEADS
GLA_HEADS = 4
GLA_DK = BRANCH // (2 * GLA_HEADS)
GLA_DV = BRANCH // GLA_HEADS
GLA_LOWRANK = 16
GLA_TAU = 16.0
RET_HEADS = 4
RET_DK = BRANCH // (2 * RET_HEADS)
RET_DV = BRANCH // RET_HEADS
GATED_CHUNK = 16
RET_CHUNK = 64
ROPE_BASE = 10000.0
EPS = 1e-6
SPLIT_WIDTHS = (BRANCH, BRANCH,
                BRANCH, BRANCH, BRANCH, BRANCH,
                GLA_HEADS * GLA_DK, GLA_HEADS * GLA_DK, BRANCH, GLA_LOWRANK, BRANCH,
                RET_HEADS * RET_DK, RET_HEADS * RET_DK, BRANCH, BRANCH)
N_IN = sum(SPLIT_WIDTHS)

kernel_name = 'hybrid_s5_hgrn2_gla_retnet_step'

def rmsnorm(x, w):
    xf = x.astype(jnp.float32)
    y = xf * lax.rsqrt(jnp.mean(xf * xf, axis=-1, keepdims=True) + EPS)
    return (y * w.astype(jnp.float32)).astype(x.dtype)

def split_heads(t, n_heads):
    b, l, w = t.shape
    return t.reshape(b, l, n_heads, w // n_heads).transpose(0, 2, 1, 3)

def merge_heads(t):
    b, h, l, d = t.shape
    return t.transpose(0, 2, 1, 3).reshape(b, l, h * d)

def head_rmsnorm(o, g):
    h, d = o.shape[1], o.shape[3]
    y = o * lax.rsqrt(jnp.mean(o * o, axis=-1, keepdims=True) + EPS)
    return y * g.astype(jnp.float32).reshape(h, 1, d)

def head_layernorm(o, g):
    h, d = o.shape[1], o.shape[3]
    c = o - jnp.mean(o, axis=-1, keepdims=True)
    y = c * lax.rsqrt(jnp.mean(c * c, axis=-1, keepdims=True) + EPS)
    return y * g.astype(jnp.float32).reshape(h, 1, d)

def rotary(t, pos):
    half = t.shape[-1] // 2
    inv = ROPE_BASE ** (-jnp.arange(half, dtype=jnp.float32) / half)
    ang = pos.astype(jnp.float32)[:, None] * inv[None, :]
    cos, sin = jnp.cos(ang), jnp.sin(ang)
    t1, t2 = t[..., :half], t[..., half:]
    return jnp.concatenate([t1 * cos - t2 * sin, t1 * sin + t2 * cos], axis=-1)

def s5_branch(u, s0_re, s0_im, lam_re, lam_im, log_step, b_re, b_im, c_re, c_im, d_skip, w_glu):
    bn, l, _ = u.shape
    uf = u.reshape(bn, l, S5_GROUPS, S5_CH)
    lr = lam_re.astype(jnp.float32)
    li = lam_im.astype(jnp.float32)
    step = jnp.exp(log_step.astype(jnp.float32))[:, None]
    mag = jnp.exp(lr * step)
    ab_re = mag * jnp.cos(li * step)
    ab_im = mag * jnp.sin(li * step)
    den = lr * lr + li * li
    nr = ab_re - 1.0
    f_re = (nr * lr + ab_im * li) / den
    f_im = (ab_im * lr - nr * li) / den
    br = b_re.astype(jnp.float32)
    bi = b_im.astype(jnp.float32)
    bb_re = f_re[..., None] * br - f_im[..., None] * bi
    bb_im = f_re[..., None] * bi + f_im[..., None] * br
    bu_re = jnp.einsum('blgc,gpc->blgp', uf, bb_re)
    bu_im = jnp.einsum('blgc,gpc->blgp', uf, bb_im)
    a_re = jnp.broadcast_to(ab_re, bu_re.shape)
    a_im = jnp.broadcast_to(ab_im, bu_im.shape)

    def combine(e1, e2):
        a1r, a1i, b1r, b1i = e1
        a2r, a2i, b2r, b2i = e2
        return (a2r * a1r - a2i * a1i, a2r * a1i + a2i * a1r,
                a2r * b1r - a2i * b1i + b2r, a2r * b1i + a2i * b1r + b2i)

    _, _, s_re, s_im = lax.associative_scan(combine, (a_re, a_im, bu_re, bu_im), axis=1)
    t1 = jnp.arange(1, l + 1, dtype=jnp.float32)[:, None, None]
    pm = jnp.exp(lr * step * t1)
    pa = li * step * t1
    p_re = pm * jnp.cos(pa)
    p_im = pm * jnp.sin(pa)
    s0r = s0_re[:, None]
    s0i = s0_im[:, None]
    s_re = s_re + p_re * s0r - p_im * s0i
    s_im = s_im + p_re * s0i + p_im * s0r
    y = (jnp.einsum('blgp,gcp->blgc', s_re, c_re.astype(jnp.float32))
         - jnp.einsum('blgp,gcp->blgc', s_im, c_im.astype(jnp.float32))
         + uf * d_skip.astype(jnp.float32).reshape(S5_GROUPS, S5_CH))
    y = jax.nn.gelu(y.reshape(bn, l, BRANCH))
    y = y * jax.nn.sigmoid(jnp.einsum('blc,cn->bln', y, w_glu.astype(jnp.float32)))
    return y, s_re[:, -1], s_im[:, -1]

def gated_chunk_scan(q, k, v, g, s0):
    bn, h, l, dk = q.shape
    dv = v.shape[-1]
    c = math.gcd(l, GATED_CHUNK)
    n = l // c
    causal = jnp.tril(jnp.ones((c, c), dtype=bool))[:, :, None]

    def to_chunks(t):
        return jnp.moveaxis(t.reshape(bn, h, n, c, t.shape[-1]), 2, 0)

    def step(S, inp):
        qc, kc, vc, gc = inp
        b = jnp.cumsum(gc, axis=2)
        diff = b[:, :, :, None, :] - b[:, :, None, :, :]
        w = jnp.where(causal, jnp.exp(jnp.where(causal, diff, 0.0)), 0.0)
        att = jnp.einsum('bhtk,bhsk,bhtsk->bhts', qc, kc, w)
        o = (jnp.einsum('bhtk,bhkv->bhtv', qc * jnp.exp(b), S)
             + jnp.einsum('bhts,bhsv->bhtv', att, vc))
        b_last = b[:, :, -1:, :]
        S = (S * jnp.exp(b_last)[:, :, 0, :, None]
             + jnp.einsum('bhsk,bhsv->bhkv', kc * jnp.exp(b_last - b), vc))
        return S, o

    S, o = lax.scan(step, s0, (to_chunks(q), to_chunks(k), to_chunks(v), to_chunks(g)))
    return jnp.moveaxis(o, 0, 2).reshape(bn, h, l, dv), S

def retention_chunk_scan(q, k, v, s0):
    bn, h, l, dk = q.shape
    dv = v.shape[-1]
    c = math.gcd(l, RET_CHUNK)
    n = l // c
    log_gamma = jnp.log1p(-jnp.exp2(-5.0 - jnp.arange(h, dtype=jnp.float32)))
    idx = jnp.arange(c, dtype=jnp.float32)
    rel = idx[:, None] - idx[None, :]
    causal = rel >= 0
    decay = jnp.where(causal, jnp.exp(jnp.where(causal, rel, 0.0)[None] * log_gamma[:, None, None]), 0.0)
    inner = jnp.exp((idx[None, :] + 1.0) * log_gamma[:, None])
    kdec = jnp.exp((c - 1.0 - idx[None, :]) * log_gamma[:, None])
    cdec = jnp.exp(c * log_gamma)

    def to_chunks(t):
        return jnp.moveaxis(t.reshape(bn, h, n, c, t.shape[-1]), 2, 0)

    def step(S, inp):
        qc, kc, vc = inp
        o_inter = jnp.einsum('bhtk,bhkv->bhtv', qc, S) * inner[None, :, :, None]
        scores = jnp.einsum('bhtk,bhsk->bhts', qc, kc) * decay[None]
        o = o_inter + jnp.einsum('bhts,bhsv->bhtv', scores, vc)
        S = (S * cdec[None, :, None, None]
             + jnp.einsum('bhsk,bhsv->bhkv', kc * kdec[None, :, :, None], vc))
        return S, o

    S, o = lax.scan(step, s0, (to_chunks(q), to_chunks(k), to_chunks(v)))
    return jnp.moveaxis(o, 0, 2).reshape(bn, h, l, dv), S

def mixer_layer(x, pos, s5_re0, s5_im0, hg0, gla0, ret0, lb, p):
    f32 = jnp.float32
    h = rmsnorm(x, p['norm_w'])
    proj = jnp.einsum('bld,dn->bln', h, p['w_in']).astype(f32)
    offs = [int(o) for o in np.cumsum(SPLIT_WIDTHS)[:-1]]
    (s5_u, s5_z, hg_q, hg_f, hg_i, hg_z, gla_q, gla_k, gla_v, gla_lr, gla_z,
     ret_q, ret_k, ret_v, ret_z) = jnp.split(proj, offs, axis=-1)

    y_s5, s5_re, s5_im = s5_branch(s5_u, s5_re0.astype(f32), s5_im0.astype(f32), p['s5_lam_re'], p['s5_lam_im'],
                                   p['s5_log_step'], p['s5_b_re'], p['s5_b_im'], p['s5_c_re'], p['s5_c_im'],
                                   p['s5_d'], p['s5_w_glu'])

    lbh = lb.reshape(HG_HEADS, 1, HG_DK)
    log_f = jnp.logaddexp(jnp.log(lbh), jnp.log1p(-lbh) + jax.nn.log_sigmoid(split_heads(hg_f, HG_HEADS)))
    o_hg, hg_new = gated_chunk_scan(split_heads(hg_q, HG_HEADS), -jnp.expm1(log_f),
                                    split_heads(hg_i, HG_HEADS), log_f, hg0.astype(f32))
    y_hg = merge_heads(head_rmsnorm(o_hg, p['hgrn_norm_w']))

    g_gla = jax.nn.log_sigmoid(jnp.einsum('blr,rn->bln', gla_lr, p['gla_w_gate_up'].astype(f32))
                               + p['gla_b_gate'].astype(f32)) / GLA_TAU
    o_gla, gla_new = gated_chunk_scan(split_heads(gla_q, GLA_HEADS) * GLA_DK ** -0.5,
                                      split_heads(gla_k, GLA_HEADS), split_heads(gla_v, GLA_HEADS),
                                      split_heads(g_gla, GLA_HEADS), gla0.astype(f32))
    y_gla = merge_heads(head_rmsnorm(o_gla, p['gla_norm_w']))

    rq = rotary(split_heads(ret_q, RET_HEADS), pos)
    rk = rotary(split_heads(ret_k, RET_HEADS), pos) * RET_DK ** -0.5
    o_ret, ret_new = retention_chunk_scan(rq, rk, split_heads(ret_v, RET_HEADS), ret0.astype(f32))
    y_ret = merge_heads(head_layernorm(o_ret, p['ret_norm_w']))

    mix = jnp.concatenate([y_s5 * jax.nn.silu(s5_z), y_hg * jax.nn.silu(hg_z),
                           y_gla * jax.nn.silu(gla_z), y_ret * jax.nn.silu(ret_z)], axis=-1)
    out = jnp.einsum('bln,nd->bld', mix, p['w_out'].astype(f32))
    return x + out.astype(x.dtype), (s5_re, s5_im, hg_new, gla_new, ret_new)

def setup_inputs(seed: int = 0) -> dict:
    key = jax.random.key(seed)
    ks = jax.random.split(key, 26)
    f32 = jnp.float32
    nrm = lambda k, s, sc: jax.random.normal(k, s, f32) * sc
    lam_re = -0.5 * jnp.exp(nrm(ks[14], (DEPTH, S5_GROUPS, S5_STATE), 0.05))
    lam_im = math.pi * jnp.arange(S5_STATE, dtype=f32)[None, None, :] + nrm(ks[15], (DEPTH, S5_GROUPS, S5_STATE), 0.05)
    log_step = math.log(1e-3) + jax.random.uniform(ks[16], (DEPTH, S5_GROUPS), f32) * (math.log(1e-1) - math.log(1e-3))
    return {
        'x_prompt': nrm(ks[0], (BATCH, SEQ, D_MODEL), 1.0),
        'x_sample': nrm(ks[1], (DEC_BATCH, DEC_SEQ, D_MODEL), 1.0),
        'state_s5_re': nrm(ks[2], (DEPTH, DEC_BATCH, S5_GROUPS, S5_STATE), 0.5),
        'state_s5_im': nrm(ks[3], (DEPTH, DEC_BATCH, S5_GROUPS, S5_STATE), 0.5),
        'state_hgrn': nrm(ks[4], (DEPTH, DEC_BATCH, HG_HEADS, HG_DK, HG_DV), 0.3),
        'state_gla': nrm(ks[5], (DEPTH, DEC_BATCH, GLA_HEADS, GLA_DK, GLA_DV), 0.3),
        'state_ret': nrm(ks[6], (DEPTH, DEC_BATCH, RET_HEADS, RET_DK, RET_DV), 0.3),
        'norm_w': 1.0 + nrm(ks[7], (DEPTH, D_MODEL), 0.02),
        'final_norm_w': 1.0 + nrm(ks[8], (D_MODEL,), 0.02),
        'w_in': nrm(ks[9], (DEPTH, D_MODEL, N_IN), D_MODEL ** -0.5),
        'w_out': nrm(ks[10], (DEPTH, MIX_WIDTH, D_MODEL), MIX_WIDTH ** -0.5),
        's5_lam_re': lam_re,
        's5_lam_im': lam_im,
        's5_log_step': log_step,
        's5_b_re': nrm(ks[11], (DEPTH, S5_GROUPS, S5_STATE, S5_CH), (2 * S5_CH) ** -0.5),
        's5_b_im': nrm(ks[12], (DEPTH, S5_GROUPS, S5_STATE, S5_CH), (2 * S5_CH) ** -0.5),
        's5_c_re': nrm(ks[13], (DEPTH, S5_GROUPS, S5_CH, S5_STATE), (2 * S5_STATE) ** -0.5),
        's5_c_im': nrm(ks[17], (DEPTH, S5_GROUPS, S5_CH, S5_STATE), (2 * S5_STATE) ** -0.5),
        's5_d': nrm(ks[18], (DEPTH, BRANCH), 1.0),
        's5_w_glu': nrm(ks[19], (DEPTH, BRANCH, BRANCH), BRANCH ** -0.5),
        'hgrn_lb_logits': nrm(ks[20], (DEPTH, HG_HEADS * HG_DK), 1.0),
        'hgrn_norm_w': 1.0 + nrm(ks[21], (DEPTH, BRANCH), 0.02),
        'gla_w_gate_up': nrm(ks[22], (DEPTH, GLA_LOWRANK, GLA_HEADS * GLA_DK), GLA_LOWRANK ** -0.5),
        'gla_b_gate': nrm(ks[23], (DEPTH, GLA_HEADS * GLA_DK), 0.1),
        'gla_norm_w': 1.0 + nrm(ks[24], (DEPTH, BRANCH), 0.02),
        'ret_norm_w': 1.0 + nrm(ks[25], (DEPTH, BRANCH), 0.02),
    }

def reference(x_prompt, x_sample, state_s5_re, state_s5_im, state_hgrn, state_gla, state_ret,
              norm_w, final_norm_w, w_in, w_out, s5_lam_re, s5_lam_im, s5_log_step,
              s5_b_re, s5_b_im, s5_c_re, s5_c_im, s5_d, s5_w_glu, hgrn_lb_logits, hgrn_norm_w,
              gla_w_gate_up, gla_b_gate, gla_norm_w, ret_norm_w):
    f32 = jnp.float32
    bp, lp = x_prompt.shape[0], x_prompt.shape[1]
    ls = x_sample.shape[1]
    pos_p = jnp.arange(lp)
    pos_s = PAST_LEN + jnp.arange(ls)
    lb_all = jnp.cumsum(jax.nn.softmax(hgrn_lb_logits.astype(f32), axis=0), axis=0)
    lb_all = lb_all - lb_all[0:1]

    xp, xs = x_prompt, x_sample
    new_p = ([], [], [], [], [])
    new_s = ([], [], [], [], [])
    for l in range(DEPTH):
        p = {
            'norm_w': norm_w[l], 'w_in': w_in[l], 'w_out': w_out[l],
            's5_lam_re': s5_lam_re[l], 's5_lam_im': s5_lam_im[l], 's5_log_step': s5_log_step[l],
            's5_b_re': s5_b_re[l], 's5_b_im': s5_b_im[l], 's5_c_re': s5_c_re[l], 's5_c_im': s5_c_im[l],
            's5_d': s5_d[l], 's5_w_glu': s5_w_glu[l], 'hgrn_norm_w': hgrn_norm_w[l],
            'gla_w_gate_up': gla_w_gate_up[l], 'gla_b_gate': gla_b_gate[l], 'gla_norm_w': gla_norm_w[l],
            'ret_norm_w': ret_norm_w[l],
        }
        xp, st_p = mixer_layer(xp, pos_p,
                               jnp.zeros((bp, S5_GROUPS, S5_STATE), f32), jnp.zeros((bp, S5_GROUPS, S5_STATE), f32),
                               jnp.zeros((bp, HG_HEADS, HG_DK, HG_DV), f32),
                               jnp.zeros((bp, GLA_HEADS, GLA_DK, GLA_DV), f32),
                               jnp.zeros((bp, RET_HEADS, RET_DK, RET_DV), f32),
                               lb_all[l], p)
        xs, st_s = mixer_layer(xs, pos_s, state_s5_re[l], state_s5_im[l], state_hgrn[l], state_gla[l],
                               state_ret[l], lb_all[l], p)
        for i in range(5):
            new_p[i].append(st_p[i])
            new_s[i].append(st_s[i])
    y_prompt = rmsnorm(xp, final_norm_w)
    y_sample = rmsnorm(xs, final_norm_w)
    return (y_prompt, y_sample,
            jnp.stack(new_p[0]), jnp.stack(new_p[1]), jnp.stack(new_p[2]), jnp.stack(new_p[3]), jnp.stack(new_p[4]),
            jnp.stack(new_s[0]), jnp.stack(new_s[1]), jnp.stack(new_s[2]), jnp.stack(new_s[3]), jnp.stack(new_s[4]))


_drawn_inputs = setup_inputs


def setup_inputs(seed=0):
    import zlib

    import numpy as np

    out = dict(_drawn_inputs(seed))
    spreads = {}
    factors = {'final_norm_w': 8.845,
     'hgrn_norm_w': 20.44,
     'gla_norm_w': 20.112,
     'ret_norm_w': 19.294,
     's5_c_re': 3.41,
     's5_c_im': 3.543,
     's5_w_glu': 3.88}
    for name, (base, spread) in spreads.items():
        noise = np.random.default_rng([zlib.crc32(name.encode()), seed]).standard_normal(out[name].shape)
        drawn = base * np.exp(spread * noise) if base else spread * noise
        out[name] = jnp.asarray(drawn.astype(out[name].dtype))
    for name, factor in factors.items():
        out[name] = (out[name] * factor).astype(out[name].dtype)
    return out
```

```python
from contextlib import ExitStack

import numpy as np

import concourse.bass as bass
from concourse import mybir

F32 = mybir.dt.float32
I32 = mybir.dt.int32
ALU = mybir.AluOpType
ACT = mybir.ActivationFunctionType

P = 128
DEPTH = 2
D = 1024
KT = D // P
TP = 256
NS = 8
TT = TP + NS
NCH = 25
NZ = 8
NP = NCH - NZ
BL = 32
NB = TP // BL
NL = 5
SL = 4
SC = TP // SL
S5T = 8
NPW = SL + 1
RING = 5
EPS = 1e-6
LN2_HI, LN2_LO = 0.693359375, -2.12194440e-4
MAGIC = 12582912.0
TWO_PI = 6.283185
GELU_A, GELU_C = 0.044715, 0.7978845608028654

(C_F0, C_F1, C_LR, C_Q0, C_Q1, C_GQ, C_GK, C_U0, C_U1, C_I0, C_I1, C_GV0, C_GV1,
 C_RQ, C_RK, C_RV0, C_RV1) = range(NP)
CHUNKS = [768, 896, 2048, 512, 640, 1536, 1664, 0, 128, 1024, 1152, 1792, 1920, 2320, 2448, 2576, 2704,
          256, 384, 1280, 1408, 2064, 2192, 2832, 2960]

(Q_NORM, Q_FINAL, Q_LOGIT, Q_GLAB, Q_HEADG, Q_S5D, Q_LR, Q_LI, Q_LS, Q_END) = np.cumsum(
    [0, DEPTH * KT, KT, DEPTH * 2, DEPTH, DEPTH * 6, DEPTH * S5T, DEPTH * S5T, DEPTH * S5T,
     DEPTH * S5T]).tolist()
_CW = [("ident", P), ("mean64", P), ("ones64", P), ("sel_a", P), ("sel_b", P), ("rev", P), ("rot", P),
       ("eye64", 64), ("m64", 2), ("m32", 4), ("m2", 2), ("gamma", 1), ("mult", NPW + SC), ("reset", 3 * TT),
       ("cos", 2 * TT), ("sin", 2 * TT), ("kdec", TP), ("decay", 4 * TP)]
CW = {}
_at = 0
for _n, _w in _CW:
    CW[_n] = (_at, _at + _w)
    _at += _w
CN = _at


def constants():
    p = np.arange(P)
    t = {}
    t["ident"] = np.eye(P)
    same64 = (p[:, None] // 64 == p[None, :] // 64)
    t["mean64"] = same64 / 64.0
    t["ones64"] = same64 * 1.0
    t["sel_a"] = (p[:, None] // 64 == p[None, :] // 32) * 1.0
    t["sel_b"] = (p[:, None] // 64 + 2 == p[None, :] // 32) * 1.0
    t["rev"] = ((p[:, None] % 32 == p[None, :] % 32) & (3 - p[:, None] // 32 == p[None, :] // 32)) * 1.0
    half = 16
    rot = np.zeros((P, P))
    for i in p:
        if i % 32 < half:
            rot[i + half, i] = -1.0
        else:
            rot[i - half, i] = 1.0
    t["rot"] = rot
    t["eye64"] = (p[:, None] % 64 == np.arange(64)[None, :]) * 1.0
    t["m64"] = (p[:, None] // 64 == np.arange(2)[None, :]) * 1.0
    t["m32"] = (p[:, None] // 32 == np.arange(4)[None, :]) * 1.0
    t["m2"] = ((p[:, None] // 32) % 2 == np.arange(2)[None, :]) * 1.0
    log_gamma = np.log1p(-np.exp2(-5.0 - np.arange(4)))
    lg = log_gamma[p // 32]
    t["gamma"] = np.exp(lg)[:, None]
    t["mult"] = np.tile(np.concatenate([np.arange(NPW), np.arange(SC)])[None, :], (P, 1))
    pos = np.arange(TT)
    t["reset"] = np.tile(np.where(pos < TP, pos % BL != 0, 0)[None, :], (P, 3))
    pos = np.where(pos < TP, pos, 2048).astype(np.float32)
    inv = (np.float32(10000.0) ** (-np.arange(half, dtype=np.float32) / np.float32(half))).astype(np.float32)
    ang = (pos[None, :] * inv[p % 32 % half][:, None]).astype(np.float32).astype(np.float64)
    t["cos"] = np.concatenate([np.cos(ang), np.cos(ang) * 32 ** -0.5], 1)
    t["sin"] = np.concatenate([np.sin(ang), np.sin(ang) * 32 ** -0.5], 1)
    t["kdec"] = np.exp((TP - 1 - np.arange(TP))[None, :] * lg[:, None])
    rel = np.arange(TP)[None, :] - p[:, None]
    t["decay"] = np.concatenate([np.where(rel >= 0, np.exp(np.maximum(rel, 0) * g), 0.0) for g in log_gamma], 1)
    big = np.concatenate([t[n] for n, _ in _CW], 1).astype(np.float32)
    mask = np.zeros((P, NL, 64), np.int32)
    for lev in range(NL):
        h = 1 << lev
        right = np.array([x for x in range(P) if (x // h) % 2 == 1])
        mask[:, lev, :] = (p[:, None] // (2 * h) == right[None, :] // (2 * h)) & ((p[:, None] // h) % 2 == 0)
    return big, mask


def build(nc, xt, w_in, w_out, par_d, s5m, w_glu, w_up, s5_in, hg_in, gla_in, ret_in, cst, msk,
          y_out, s5p_out, hgp_out, glap_out, retp_out, s5s_out, hgs_out, glas_out, rets_out):
    with ExitStack() as ctx:
        def sb(name, *shape, dt=F32):
            return ctx.enter_context(nc.sbuf_tensor(name, [P, *shape], dt))

        def sem(name):
            return ctx.enter_context(nc.semaphore(name))

        x = sb("x", KT, TT)
        h = sb("h", KT, TT)
        zs = sb("zs", KT, TT)
        wring = sb("wring", RING, KT, P)
        parm = sb("parm", Q_END)
        cs = sb("cs", CN)
        masks = sb("masks", NL, 64, dt=I32)
        ones_d = sb("ones_d", P)
        rstd = sb("rstd", TT)
        qraw = sb("qraw", TT)
        qv = sb("qv", 4, TT)
        gates = sb("gates", 6, TT)
        x3, tl = gates[:, 0:3, :], gates[:, 3:6, :]
        k3 = sb("k3", 3, TT)
        eb = sb("eb", 3, TT)
        ke = sb("ke", 3, TT)
        u = sb("u", 2, TT)
        lr_t = sb("lr_t", TT)
        v = sb("v", 6, TT)
        o = v
        r2 = sb("r2", 2, TT)
        rqm = sb("rqm", 2, TT)
        kd = sb("kd", TP)
        qm = sb("qm", 8, TP)
        rs = qm[:, :, :].rearrange("p a t -> p (a t)")[:, 0:6 * TT].rearrange("p (a t) -> p a t", a=6)
        lev = sb("lev", 4224)
        dl = [lev[:, 768 * i:768 * i + 768].rearrange("p (g t) -> p g t", g=3) for i in range(2)]
        kl = [lev[:, 1536 + 768 * i:2304 + 768 * i].rearrange("p (g t) -> p g t", g=3) for i in range(2)]
        ql = [lev[:, 3072 + 512 * i:3584 + 512 * i].rearrange("p (g t) -> p g t", g=4) for i in range(2)]
        kvb = lev[:, 0:2048]
        vd = lev[:, 2048:3072].rearrange("p (g n) -> p g n", g=2)
        osq = lev[:, 2048:2048 + 6 * TT].rearrange("p (g t) -> p g t", g=6)
        att = sb("att", 2, 4, 2, P)
        attr = gates[:, :, :].rearrange("p a t -> p (a t)")[:, 0:4 * 384].rearrange("p (a t) -> p a t", a=4)
        rt1, rt2 = gates[:, 0:2, :], gates[:, 2:4, :]
        tok = sb("tok", 18 * P)
        vt = tok[:, 0:12 * P].rearrange("p (b t c) -> p b t c", b=2, t=6)
        ket = tok[:, 12 * P:18 * P].rearrange("p (b t c) -> p b t c", b=2, t=3)
        krt = sb("krt", 2, P)
        s3 = sb("s3", 3, NB + 1, 64)
        retf = sb("retf", 64)
        ss = sb("ss", 4, NS, 64)
        f4 = sb("f4", 4, NS)
        k4 = sb("k4", 4, NS)
        q4 = sb("q4", 4, NS)
        qs_hg = sb("qs_hg", 2, NS, 2)
        qs_gr = sb("qs_gr", 2, NS, 4)
        lbc = sb("lbc", 2, 2, 3)
        lbt = sb("lbt", 2, 4)
        s5m_t = sb("s5m_t", 4, S5T, 32)
        LS = DEPTH * S5T
        sw = sb("sw", 12, LS)
        turns, turnr = (lev[:, i * LS * (NPW + SC):(i + 1) * LS * (NPW + SC)].rearrange("p (s m) -> p s m", s=LS) for i in range(2))
        sinm = sb("sinm", LS, NPW + SC)
        cosm = sb("cosm", LS, NPW + SC)
        mag = sb("mag", LS, NPW)
        are = sb("are", LS, NPW)
        aim = sb("aim", LS, NPW)
        mtmp = sb("mtmp", LS, NPW)
        gre = sb("gre", LS, SL)
        gim = sb("gim", LS, SL)
        gt1 = sb("gt1", LS, SL)
        gt2 = sb("gt2", LS, SL)
        m4 = sb("m4", S5T, SC)
        bb_re, bb_im = (tok[:, i * 1024:i * 1024 + 1024].rearrange("p (s j c) -> p s j c", s=S5T, j=SL) for i in range(2))
        ca_re = sb("ca_re", S5T, NPW, 32)
        ca_im = sb("ca_im", S5T, NPW, 32)
        gtr = qm[:, :, :].rearrange("p a t -> p (a t)").rearrange("p (n s m) -> p n s m", n=2, s=S5T)
        tmat = sb("tmat", S5T, P)
        ub = sb("ub", S5T, NS + SC)
        us0 = sb("us0", S5T, NS)
        sr = sb("sr", S5T, NS + SC + 1)
        si = sb("si", S5T, NS + SC + 1)
        s5i = sb("s5i", DEPTH, 2, S5T, NS)
        s5n = sb("s5n", 2, S5T, NS)
        s5t = sb("s5t", 4, S5T, NS)
        s5f = sb("s5f", 2, S5T)
        flat_att = att[:, :, :, :, :].rearrange("p g i b t -> p (g i b t)")
        sv = [flat_att[:, 512 * i:512 * i + 512] for i in range(4)]
        NY = S5T * (NS + SC)
        yb, yt2 = lev[:, 3072:3072 + NY], lev[:, 3072 + NY:3072 + 2 * NY]
        yg = u
        wg = sb("wg", DEPTH, 2, 2, P)
        wup = sb("wup", DEPTH, P)
        glu = rqm
        ptmp = sb("ptmp", S5T // 2, NPW, 32)

        pr = [ctx.enter_context(nc.psum_tensor(f"pr{i}", [P, 512], F32)) for i in range(3)]
        wk = ctx.enter_context(nc.psum_tensor("wk", [P, 5, 512], F32))

        def c(name):
            return cs[:, CW[name][0]:CW[name][1]]

        x_in, par_in, cst_in, small_in = sem("x_in"), sem("par_in"), sem("cst_in"), sem("small_in")
        w_in_sem = [sem(f"w_slot{i}") for i in range(RING)]
        s5m_in, state_out = sem("s5m_in"), sem("state_out")
        s5s_used, s5f_ready, r2_used = (sem(n) for n in ("s5s_used", "s5f_ready", "r2_used"))
        ss_in = sem("ss_in")
        out_sem = sem("out_sem")
        stored = sem("stored")
        ms_done, proj_done, lrup_done, s5v_done, diag_done, lvl_done, tr_done, kv_done = (
            sem(n) for n in ("ms_done", "proj_done", "lrup_done", "s5v_done", "diag_done", "lvl_done", "tr_done", "kv_done"))
        rot_done, rsc_done, y_done, vb_done, o_done, rst_done, so_done, glu_done = (
            sem(n) for n in ("rot_done", "rsc_done", "y_done", "vb_done", "o_done", "rst_done", "so_done", "glu_done"))
        mean_done, var_done, out_done, gtr_done, kt_done = (
            sem(n) for n in ("mean_done", "var_done", "out_done", "gtr_done", "kt_done"))
        act_step, sq_ready, rstd_ready, chunk_evac, l_ready, k3_ready, eb_ready, lexp_ready, tr_evac = (
            sem(n) for n in ("act_step", "sq_ready", "rstd_ready", "chunk_evac", "l_ready", "k3_ready", "eb_ready", "lexp_ready", "tr_evac"))
        gtr_evac, sin_ready, y_evac, tanh_ready, glu_tanh, osq_ready, ors_ready, lb_act, lb2_act = (
            sem(n) for n in ("gtr_evac", "sin_ready", "y_evac", "tanh_ready", "glu_tanh", "osq_ready", "ors_ready", "lb_act", "lb2_act"))
        dve_step, h_ready, t_ready, ls_ready, b_ready, de_ready, ld_ready, ql_ready, att_ready, lvl_used = (
            sem(n) for n in ("dve_step", "h_ready", "t_ready", "ls_ready", "b_ready", "de_ready", "ld_ready", "ql_ready", "att_ready", "lvl_used"))
        lb_ready, ph_ready, tab_ready, tmat_ready, u_ready, s5v_used, s_ready, ke_ready, qv_ready = (
            sem(n) for n in ("lb_ready", "ph_ready", "tab_ready", "tmat_ready", "u_ready", "s5v_used", "s_ready", "ke_ready", "qv_ready"))
        s3_ready, rqm_ready, attr_ready, kvb_ready, ss_ready, tin_ready, yg_ready, qm_ready, vb_used, ym_ready = (
            sem(n) for n in ("s3_ready", "rqm_ready", "attr_ready", "kvb_ready", "ss_ready", "tin_ready", "yg_ready", "qm_ready", "vb_used", "ym_ready"))
        o_ready, mean_used, mix_ready, out_used, fin_ready, st_ready, lm_ready, zero_ready = (
            sem(n) for n in ("o_ready", "mean_used", "mix_ready", "out_used", "fin_ready", "st_ready", "lm_ready", "zero_ready"))
        pool_step, bb_ready, ca_ready, fs_ready, vd_ready, q4_ready, s5s_part, set_ready = (
            sem(n) for n in ("pool_step", "bb_ready", "ca_ready", "fs_ready", "vd_ready", "q4_ready", "s5s_part", "set_ready"))

        def chain(eng, steps):
            last = [None, {}]

            def step(ins, signal=None):
                s = signal if signal is not None else steps
                n = last[1].get(s.name, 0) + 1
                last[1][s.name] = n
                ins.then_inc(s, 1)
                last[0] = (s, n)

            def settle():
                eng.wait_ge(*last[0])
            return step, settle

        def par(col, n=1):
            return parm[:, col:col + n]

        def qrt(ap, q):
            return ap[32 * q:32 * q + 32]

        USES = NCH + 2 + 6 + KT

        def ring_free(eng, layer, i):
            i -= 3
            if i < 0:
                layer, i = layer - 1, i + USES
            if layer < 0:
                return
            if i < NCH:
                eng.wait_ge(chunk_evac, layer * NCH + i + 1)
            elif i < NCH + 2:
                eng.wait_ge(mean_used, layer * 2 + i - NCH + 1)
            elif i < NCH + 8:
                eng.wait_ge(ors_ready, layer * 7 + i - NCH - 2 + 1)
            else:
                eng.wait_ge(out_used, layer * KT + i - NCH - 8 + 1)

        def ring_bank(layer, i):
            return pr[(layer * USES + i) % 3]

        block = ctx.enter_context(nc.Block())

        @block.sync
        def _(sp):
            sp.dma_start(x[:, :, :], xt).then_inc(x_in, 16)
            sp.dma_start(parm[:, :], par_d).then_inc(par_in, 16)
            use = 0

            def chunk(src):
                nonlocal use
                if use >= RING:
                    before, i = divmod(use - RING, NCH + KT)
                    if i < NCH:
                        sp.wait_ge(proj_done, before * NCH + i + 1)
                    else:
                        sp.wait_ge(out_done, before * KT + i - NCH + 1)
                sp.dma_start(wring[:, use % RING, :, :], src).then_inc(w_in_sem[use % RING], 16)
                use += 1

            for layer in range(DEPTH):
                for i in range(NCH):
                    chunk(w_in[layer, i])
                    if layer == 0 and i == 1:
                        sp.dma_start(cs[:, :], cst).then_inc(cst_in, 16)
                        sp.dma_start(s5m_t[:, :, :, :], s5m[0]).then_inc(s5m_in, 16)
                    if layer == 0 and i == 3:
                        sp.dma_start(wup[0:16, :, :], w_up).then_inc(small_in, 16)
                        sp.dma_start(s5i[:, :, :, :, :], s5_in).then_inc(small_in, 16)
                        sp.dma_start(masks[:, :, :], msk).then_inc(small_in, 16)
                        sp.dma_start(wg[:, :, :, :, :], w_glu).then_inc(small_in, 16)
                    if i == 5:
                        if layer:
                            sp.wait_ge(stored, layer)
                        sp.dma_start(ss[:, 0:2, :, :], hg_in[layer]).then_inc(ss_in, 16)
                        sp.dma_start(ss[:, 2, :, :], gla_in[layer]).then_inc(ss_in, 16)
                        sp.dma_start(ss[:, 3, :, :], ret_in[layer]).then_inc(ss_in, 16)
                for i in range(KT):
                    chunk(w_out[layer, i])
                    if i == 0 and layer + 1 < DEPTH:
                        sp.wait_ge(bb_ready, layer + 1)
                        sp.wait_ge(ca_ready, layer + 1)
                        sp.dma_start(s5m_t[:, :, :, :], s5m[layer + 1]).then_inc(s5m_in, 16)
            sp.wait_ge(fin_ready, KT)
            sp.dma_start(y_out, h[:, :, :]).then_inc(out_sem, 16)
            sp.wait_ge(out_sem, 16)

        @block.tensor
        def _(pe):
            use = [0]

            def weight():
                i = use[0]
                pe.wait_ge(w_in_sem[i % RING], 16 * (i // RING + 1))
                use[0] += 1
                return wring[:, i % RING, :, :]

            def mean_square(n):
                for k in range(KT):
                    pe.wait_ge(sq_ready, n * KT + k + 1)
                    mm = nc.tensor.matmul(wk[:, 0, 0:TT], ones_d[:, :], h[:, k, :], start=(k == 0), stop=(k == KT - 1))
                mm.then_inc(ms_done, 1)

            def project(layer, i):
                w = weight()
                ring_free(pe, layer, i)
                for k in range(KT):
                    if i == 0:
                        pe.wait_ge(h_ready, layer * KT + k + 1)
                    mm = nc.tensor.matmul(ring_bank(layer, i)[:, 0:TT], w[:, k, :], h[:, k, :],
                                          start=(k == 0), stop=(k == KT - 1))
                mm.then_inc(proj_done, 1)

            def low_rank(layer):
                pe.wait_ge(chunk_evac, layer * NCH + C_LR + 1)
                if layer == 0:
                    pe.wait_ge(small_in, 64)
                nc.tensor.matmul(wk[:, 1, 0:TT], wup[0:16, layer, :], lr_t[0:16, :], start=True, stop=True)\
                    .then_inc(lrup_done, 1)

            def s5_tables(layer):
                pe.wait_ge(bb_ready, layer + 1)
                for r in range(4):
                    if r:
                        pe.wait_ge(gtr_evac, layer * 4 + r)
                    elif layer:
                        pe.wait_ge(o_ready, layer * 4)
                    for n in range(4):
                        src = (bb_re, bb_im)[r // 2][:, 4 * (r % 2) + n, :, :]
                        mm = nc.tensor.transpose(wk[:, 4, P * n:P * n + P], src.rearrange("p j c -> p (j c)"), c("ident"))
                    mm.then_inc(gtr_done, 1)
                pe.wait_ge(ca_ready, layer + 1)
                for s in range(S5T):
                    for n, (b, ca) in enumerate(((bb_re, ca_re), (bb_im, ca_im))):
                        mm = nc.tensor.matmul(wk[0:32, 2 + s // 4, P * (s % 4):P * (s % 4) + P], b[:, s, 0, :],
                                              ca[:, s, 0:SL, :].rearrange("p j c -> p (j c)"),
                                              start=(n == 0), stop=(n == 1))
                mm.then_inc(kt_done, 1)

            def s5_inputs(layer):
                pe.wait_ge(u_ready, layer + 1)
                pe.wait_ge(gtr_evac, layer * 4 + 4)
                pe.wait_ge(tmat_ready, layer + 1)
                for n in range(2):
                    for s in range(S5T):
                        nc.tensor.matmul(wk[:, 2 + n, SC * s:SC * s + SC], gtr[:, n, s, :], ub[:, s, NS:],
                                         start=True, stop=True)
                for n in range(2):
                    for s in range(S5T):
                        mm = nc.tensor.matmul(wk[:, 4, 64 * n + NS * s:64 * n + NS * s + NS], gtr[:, n, s, :], us0[:, s, :],
                                              start=True, stop=True)
                mm.then_inc(s5v_done, 1)

            def s5_outputs(layer, n):
                if n == 0:
                    pe.wait_ge(s_ready, layer + 1)
                pe.wait_ge(tr_evac, layer * 6 + 6)
                if n:
                    pe.wait_ge(y_evac, layer * 2 + 1)
                for s in range(4 * n, 4 * n + 4):
                    dst = wk[:, 4, 72 * (s - 4 * n):72 * (s - 4 * n) + 72]
                    nc.tensor.matmul(dst, tmat[:, s, :], ub[:, s, :], start=True, stop=False)
                    nc.tensor.matmul(dst, ca_re[:, s, 1:NPW, :].rearrange("p j c -> p (j c)"), sr[:, s, 0:72],
                                     start=False, stop=False)
                    mm = nc.tensor.matmul(dst, ca_im[:, s, 1:NPW, :].rearrange("p j c -> p (j c)"), si[:, s, 0:72],
                                          start=False, stop=True)
                mm.then_inc(y_done, 1)

            def diagonal(layer):
                pe.wait_ge(qv_ready, layer + 1)
                pe.wait_ge(k3_ready, layer + 1)
                pe.wait_ge(s5v_used, layer + 1)
                for blk in range(2):
                    for g in range(2):
                        rows = slice(64 * g, 64 * g + 64)
                        for i in range(4):
                            mm = nc.tensor.matmul(wk[:, 2 * blk + g, P * i:P * i + P],
                                                  k3[rows, min(i, 2), P * blk:P * blk + P],
                                                  qv[rows, i, P * blk:P * blk + P], start=True, stop=True)
                mm.then_inc(diag_done, 1)

            def level(layer, n):
                pe.wait_ge(ql_ready, layer * NL + n + 1)
                if n < 2:
                    pe.wait_ge(att_ready, layer * 4 + (2 if n == 0 else 4))
                else:
                    pe.wait_ge(lvl_used, layer * NL + n - 1)
                for g in range(2):
                    rows = slice(64 * g, 64 * g + 64)
                    for i in range(4):
                        for blk in range(2):
                            a = (2 * i + blk) * 64
                            mm = nc.tensor.matmul(wk[:, 2 * (n % 2) + g, a:a + 64],
                                                  kl[n % 2][rows, min(i, 2), P * blk:P * blk + P],
                                                  ql[n % 2][rows, i, 64 * blk:64 * blk + 64], start=True, stop=True)
                mm.then_inc(lvl_done, 1)

            def turn(layer, r, tiles):
                if r:
                    pe.wait_ge(tr_evac, layer * 6 + r)
                else:
                    pe.wait_ge(s5s_used, layer + 1)
                for n, t in enumerate(tiles):
                    mm = nc.tensor.transpose(wk[:, 4, P * n:P * n + P], t, c("ident"))
                mm.then_inc(tr_done, 1)

            def block_states(layer):
                pe.wait_ge(tr_evac, layer * 6 + 4)
                pe.wait_ge(r2_used, layer + 1)
                pe.wait_ge(lvl_used, layer * NL + NL)
                for blk in range(2):
                    for j in range(4):
                        rows = slice(32 * j, 32 * j + 32)
                        for hd in range(4):
                            t, hh = hd // 2, hd % 2
                            nc.tensor.matmul(wk[64 * hh:64 * hh + 64, j, (3 * blk + t) * 64:(3 * blk + t) * 64 + 64],
                                             ket[rows, blk, t, 64 * hh:64 * hh + 64],
                                             vt[rows, blk, t, 64 * hh:64 * hh + 64], start=True, stop=True)
                        for hd in range(4):
                            mm = nc.tensor.matmul(wk[32 * hd:32 * hd + 32, j, (3 * blk + 2) * 64:(3 * blk + 2) * 64 + 64],
                                                  ket[rows, blk, 2, 32 * hd:32 * hd + 32],
                                                  vt[rows, blk, 2 + hd // 2, 64 * (hd % 2):64 * (hd % 2) + 64],
                                                  start=True, stop=True)
                mm.then_inc(kv_done, 1)

            def rotate(layer):
                pe.wait_ge(chunk_evac, layer * NCH + C_RK + 1)
                pe.wait_ge(lvl_used, layer * NL + 4)
                for n in range(2):
                    mm = nc.tensor.matmul(wk[:, 2 + n, 0:TT], c("rot"), r2[:, n, :], start=True, stop=True)
                mm.then_inc(rot_done, 1)

            def ret_scores(layer):
                pe.wait_ge(rqm_ready, layer + 1)
                pe.wait_ge(s3_ready, layer + 1)
                for hd in range(4):
                    rows = slice(64 * (hd // 2), 64 * (hd // 2) + 64)
                    nc.tensor.matmul(wk[:, hd, 0:TP], r2[rows, 1, 0:P], rqm[rows, hd % 2, 0:TP], start=True, stop=True)
                    mm = nc.tensor.matmul(wk[:, hd, TP:384], r2[rows, 1, P:TP], rqm[rows, hd % 2, P:TP], start=True, stop=True)
                mm.then_inc(rsc_done, 1)

            def sample_v(layer, n):
                pe.wait_ge(vd_ready, layer * 3 + n + 1)
                if n == 0:
                    pe.wait_ge(attr_ready, layer + 1)
                    for t in range(2):
                        mm = nc.tensor.matmul(wk[:, t, :], c("ones64"), vd[:, t, :], start=True, stop=True)
                else:
                    for t in range(2):
                        mm = nc.tensor.matmul(wk[:, 1 + n, :], c(("sel_a", "sel_b")[t]), vd[:, t, :],
                                              start=(t == 0), stop=(t == 1))
                mm.then_inc(vb_done, 1)

            def outputs(layer):
                pe.wait_ge(vb_used, layer + 1)
                pe.wait_ge(lvl_used, layer * NL + NL)
                pe.wait_ge(qm_ready, layer + 1)
                pe.wait_ge(tr_evac, layer * 6 + 6)
                for kind in range(2):
                    for t in range(2):
                        for hh in range(2):
                            rows = slice(64 * hh, 64 * hh + 64)
                            g, i = (hh, t) if kind == 0 else (t, 2 + hh)
                            vtile = 2 * kind + t
                            for blk in range(2):
                                nc.tensor.matmul(wk[rows, kind, TP * t + P * blk:TP * t + P * blk + P],
                                                 vt[:, blk, vtile, rows], att[:, g, i, blk, :],
                                                 start=(t == 0 and blk == 0), stop=False, skip_group_check=True)
                            for b in range(1, NB):
                                st = s3[:, t if kind == 0 else 2, b, :]
                                q = qm[:, 4 * kind + 2 * t + hh, BL * b:BL * b + BL]
                                mm = nc.tensor.matmul(wk[rows, kind, TP * t + BL * b:TP * t + BL * b + BL], st, q,
                                                      start=False, stop=(t == 1 and b == NB - 1), skip_group_check=True)
                    mm.then_inc(o_done, 1)
                for t in range(2):
                    for hh in range(2):
                        rows = slice(64 * hh, 64 * hh + 64)
                        nc.tensor.matmul(wk[rows, 2, TP * t:TP * t + TP], vt[:, 0, 4 + t, rows], attr[:, 2 * t + hh, 0:TP],
                                         start=(t == 0), stop=False, skip_group_check=True)
                        mm = nc.tensor.matmul(wk[rows, 2, TP * t + P:TP * t + TP], vt[:, 1, 4 + t, rows],
                                              attr[:, 2 * t + hh, TP:384], start=False, stop=(t == 1), skip_group_check=True)
                mm.then_inc(o_done, 1)
                for blk in range(2):
                    mm = nc.tensor.matmul(wk[:, 3, 0:TP], krt[:, blk, :],
                                          vt[:, blk, 4:6, :].rearrange("p a c -> p (a c)"), start=(blk == 0), stop=(blk == 1))
                mm.then_inc(rst_done, 1)

            def sample_outputs(layer):
                pe.wait_ge(ss_ready, layer + 1)
                pe.wait_ge(q4_ready, layer + 1)
                pe.wait_ge(y_evac, layer * 2 + 2)
                for t in range(2):
                    for b in range(NS):
                        a = 2 * (NS * t + b)
                        nc.tensor.matmul(wk[0:64, 4, a:a + 2], ss[:, t, b, :], qs_hg[:, t, b, :], start=True, stop=True)
                for n in range(2):
                    for b in range(NS):
                        a = 32 + 4 * (NS * n + b)
                        mm = nc.tensor.matmul(wk[0:64, 4, a:a + 4], ss[:, 2 + n, b, :], qs_gr[:, n, b, :], start=True, stop=True)
                mm.then_inc(so_done, 1)

            def glu_gate(layer):
                pe.wait_ge(yg_ready, layer + 1)
                pe.wait_ge(st_ready, layer + 1)
                pe.wait_ge(o_ready, layer * 4 + 4)
                for m in range(2):
                    for k in range(2):
                        mm = nc.tensor.matmul(wk[:, 2 + m, 0:TT], wg[:, layer, k, m, :], yg[:, k, :],
                                              start=(k == 0), stop=(k == 1))
                mm.then_inc(glu_done, 1)

            def head_norms(layer):
                pe.wait_ge(o_ready, layer * 4 + 4)
                for t in range(2):
                    i = NCH + t
                    ring_free(pe, layer, i)
                    nc.tensor.matmul(ring_bank(layer, i)[:, 0:TT], c("mean64"), o[:, 4 + t, :], start=True, stop=True)\
                        .then_inc(mean_done, 1)
                for t in range(6):
                    i = NCH + 2 + t
                    ring_free(pe, layer, i)
                    pe.wait_ge(osq_ready, layer * 2 + (1 if t < 4 else 2))
                    nc.tensor.matmul(ring_bank(layer, i)[:, 0:TT], c("mean64"), osq[:, t, :], start=True, stop=True)\
                        .then_inc(var_done, 1)

            def project_out(layer, m):
                w = weight()
                i = NCH + 8 + m
                ring_free(pe, layer, i)
                for k in range(KT):
                    if m == 0:
                        pe.wait_ge(mix_ready, layer * 2 + (1 if k < 2 else 2))
                    mm = nc.tensor.matmul(ring_bank(layer, i)[:, 0:TT], w[:, k, :], zs[:, k, :],
                                          start=(k == 0), stop=(k == KT - 1))
                mm.then_inc(out_done, 1)

            pe.wait_ge(zero_ready, 1)
            for layer in range(DEPTH):
                mean_square(layer)
                for i in range(NCH):
                    project(layer, i)
                    if i == C_Q0:
                        low_rank(layer)
                    if i == C_GK:
                        if layer == 0:
                            pe.wait_ge(cst_in, 16)
                        s5_tables(layer)
                    if i == C_I0:
                        s5_inputs(layer)
                    if i == C_I1:
                        diagonal(layer)
                    if C_GV0 <= i < C_GV0 + NL:
                        level(layer, i - C_GV0)
                    if i == C_GV1:
                        pe.wait_ge(ke_ready, layer + 1)
                        turn(layer, 0, [ke[:, t, 0:P] for t in range(3)])
                    if i == C_RQ:
                        turn(layer, 1, [ke[:, t, P:TP] for t in range(3)])
                    if i == C_RK:
                        turn(layer, 2, [v[:, t, P * b:P * b + P] for b in range(2) for t in range(2)])
                    if i == C_RV0:
                        turn(layer, 3, [v[:, 2 + t, P * b:P * b + P] for b in range(2) for t in range(2)])
                    if i == C_RV1:
                        rotate(layer)
                    if i == NP:
                        pe.wait_ge(chunk_evac, layer * NCH + C_RV1 + 1)
                        turn(layer, 4, [v[:, 4 + t, P * b:P * b + P] for b in range(2) for t in range(2)])
                    if i == NP + 1:
                        block_states(layer)
                    if i == NP + 2:
                        pe.wait_ge(rqm_ready, layer + 1)
                        turn(layer, 5, [kd[:, P * b:P * b + P] for b in range(2)])
                    if i == NP + 3:
                        ret_scores(layer)
                    if i == NP + 4:
                        s5_outputs(layer, 0)
                        sample_v(layer, 0)
                    if i == NP + 5:
                        s5_outputs(layer, 1)
                        sample_v(layer, 1)
                    if i == NP + 6:
                        sample_v(layer, 2)
                outputs(layer)
                sample_outputs(layer)
                glu_gate(layer)
                head_norms(layer)
                for m in range(KT):
                    project_out(layer, m)
            mean_square(DEPTH)

        @block.scalar
        def _(act):
            step, settle = chain(act, act_step)
            fn = nc.scalar.activation

            def use_logs():
                nc.scalar.preload_act_table_set("natural_log_exp_and_others")

            def use_silu():
                nc.scalar.preload_act_table_set("silu_and_others")

            def rsqrt_of(src, dst, signal):
                step(fn(dst, src, ACT.Ln, bias=EPS))
                settle()
                step(fn(dst, dst, ACT.Exp, scale=-0.5), signal)

            def norm(n):
                for k in range(KT):
                    if n:
                        act.wait_ge(out_used, (n - 1) * KT + k + 1)
                        if k == 0:
                            act.wait_ge(proj_done, n * NCH)
                    step(fn(h[:, k, :], x[:, k, :], ACT.Square), sq_ready)
                act.wait_ge(ms_done, n + 1)
                if n:
                    act.wait_ge(h_ready, n * KT)
                rsqrt_of(wk[:, 0, 0:TT], rstd[:, :], rstd_ready)

            def evac(layer, i, dst):
                act.wait_ge(proj_done, layer * NCH + i + 1)
                m = dst.shape[0]
                step(fn(dst, ring_bank(layer, i)[0:m, 0:TT], ACT.Copy), chunk_evac)

            def lower_bounds():
                act.wait_ge(lb_ready, 1)
                step(fn(lbt[:, :, 1], lbt[:, :, 0], ACT.Abs))
                settle()
                step(fn(lbt[:, :, 1], lbt[:, :, 1], ACT.Exp, scale=-1.0))
                settle()
                step(fn(lbt[:, :, 1], lbt[:, :, 1], ACT.Ln, bias=1.0), lb_act)

            def gate_logs(layer):
                act.wait_ge(lrup_done, layer + 1)
                if layer:
                    act.wait_ge(b_ready, layer)
                step(fn(x3[:, 2, :], wk[:, 1, 0:TT], ACT.Identity, bias=par(Q_GLAB + layer)))
                settle()
                step(fn(tl, x3, ACT.Abs))
                settle()
                step(fn(tl, tl, ACT.Exp, scale=-1.0))
                settle()
                step(fn(tl, tl, ACT.Ln, bias=1.0), l_ready)

            def keys(layer):
                act.wait_ge(t_ready, layer + 1)
                for t in range(2):
                    step(fn(k3[:, t, :], k3[:, t, :], ACT.Exp, scale=-1.0, bias=lbc[:, layer, t, 1:2]),
                         k3_ready if t == 1 else None)
                if layer:
                    act.wait_ge(ls_ready, layer + 1)
                    for t in range(2):
                        step(fn(eb[:, t, :], x3[:, t, :], ACT.Abs, bias=lbc[:, layer, t, 2:3]))
                    settle()
                    step(fn(eb[:, 0:2, :], eb[:, 0:2, :], ACT.Exp, scale=-1.0))
                    settle()
                    step(fn(eb[:, 0:2, :], eb[:, 0:2, :], ACT.Ln, bias=1.0), lb2_act)

            def decays(layer):
                act.wait_ge(b_ready, layer + 1)
                step(fn(eb[:, :, :], tl, ACT.Exp), eb_ready)
                act.wait_ge(de_ready, layer + 1)
                step(fn(ke[:, :, 0:TP], ke[:, :, 0:TP], ACT.Exp), eb_ready)

            def level_exp(layer, n):
                act.wait_ge(ld_ready, layer * NL + n + 1)
                step(fn(dl[n % 2], dl[n % 2], ACT.Exp), lexp_ready)

            def turned(layer, r, dst):
                act.wait_ge(tr_done, layer * 6 + r + 1)
                n = dst.free_size()
                step(fn(dst, wk[:, 4, 0:n] if len(dst.shape) == 2 else
                        wk[:, 4, 0:n].rearrange("p (a b) -> p a b", a=dst.shape[1]) if len(dst.shape) == 3 else
                        wk[:, 4, 0:n].rearrange("p (a b c) -> p a b c", a=dst.shape[1], b=dst.shape[2]), ACT.Copy), tr_evac)

            def s5_turned(layer):
                for r in range(4):
                    act.wait_ge(gtr_done, layer * 4 + r + 1)
                    step(fn(gtr[:, r // 2, 4 * (r % 2):4 * (r % 2) + 4, :].rearrange("p s m -> p (s m)"),
                            wk[:, 4, :], ACT.Copy), gtr_evac)

            def silu(layer, i):
                act.wait_ge(proj_done, layer * NCH + i + 1)
                if layer and i == NP:
                    act.wait_ge(out_done, layer * KT)
                step(fn(zs[:, i - NP, :], ring_bank(layer, i)[:, 0:TT], ACT.Silu), chunk_evac)

            def s5_evac(layer, n):
                act.wait_ge(y_done, layer * 2 + n + 1)
                step(fn(yb[:, NY // 2 * n:NY // 2 * n + NY // 2], wk[:, 4, 0:NY // 2], ACT.Copy), y_evac)

            use_logs()
            act.wait_ge(x_in, 16)
            act.wait_ge(par_in, 16)
            for layer in range(DEPTH):
                norm(layer)
                if layer == 0:
                    lower_bounds()
                    use_silu()
                    act.wait_ge(ph_ready, 2)
                    step(fn(sinm[:, :, :], sinm[:, :, :], ACT.Sin, scale=TWO_PI))
                    step(fn(cosm[:, :, :], cosm[:, :, :], ACT.Sin, scale=TWO_PI), sin_ready)
                    use_logs()
                evac(layer, C_F0, x3[:, 0, :])
                evac(layer, C_F1, x3[:, 1, :])
                evac(layer, C_LR, lr_t[0:16, :])
                evac(layer, C_Q0, qv[:, 0, :])
                evac(layer, C_Q1, qv[:, 1, :])
                gate_logs(layer)
                evac(layer, C_GQ, qraw[:, :])
                evac(layer, C_GK, k3[:, 2, :])
                keys(layer)
                s5_turned(layer)
                evac(layer, C_U0, u[:, 0, :])
                decays(layer)
                evac(layer, C_U1, u[:, 1, :])
                level_exp(layer, 0)
                evac(layer, C_I0, v[:, 0, :])
                level_exp(layer, 1)
                evac(layer, C_I1, v[:, 1, :])
                level_exp(layer, 2)
                evac(layer, C_GV0, v[:, 2, :])
                level_exp(layer, 3)
                evac(layer, C_GV1, v[:, 3, :])
                turned(layer, 0, ket[:, 0, :, :])
                level_exp(layer, 4)
                evac(layer, C_RQ, r2[:, 0, :])
                turned(layer, 1, ket[:, 1, :, :])
                evac(layer, C_RK, r2[:, 1, :])
                turned(layer, 2, vt[:, :, 0:2, :])
                evac(layer, C_RV0, v[:, 4, :])
                turned(layer, 3, vt[:, :, 2:4, :])
                evac(layer, C_RV1, v[:, 5, :])
                use_silu()
                for i in range(NP, NCH):
                    silu(layer, i)
                    if i == NP:
                        turned(layer, 4, vt[:, :, 4:6, :])
                    if i == NP + 2:
                        turned(layer, 5, krt[:, :, :])
                    if i == NP + 4:
                        s5_evac(layer, 0)
                    if i == NP + 5:
                        s5_evac(layer, 1)
                act.wait_ge(tin_ready, layer + 1)
                step(fn(yt2, yt2, ACT.Tanh, scale=GELU_C), tanh_ready)
                act.wait_ge(glu_done, layer + 1)
                step(fn(glu[:, :, :], wk[:, 2:4, 0:TT], ACT.Tanh, scale=0.5), glu_tanh)
                use_logs()
                act.wait_ge(o_ready, layer * 4 + 4)
                step(fn(osq[:, 0:4, :], o[:, 0:4, :], ACT.Square), osq_ready)
                act.wait_ge(mean_used, layer * 2 + 2)
                step(fn(osq[:, 4:6, :], o[:, 4:6, :], ACT.Square), osq_ready)
                for t in range(6):
                    act.wait_ge(var_done, layer * 6 + t + 1)
                    step(fn(rs[:, t, :], ring_bank(layer, NCH + 2 + t)[:, 0:TT], ACT.Ln, bias=EPS), ors_ready)
                settle()
                step(fn(rs[:, :, :], rs[:, :, :], ACT.Exp, scale=-0.5), ors_ready)
            norm(DEPTH)

        @block.vector
        def _(dve):
            step, settle = chain(dve, dve_step)
            tt, ts, stt, cp = (nc.vector.tensor_tensor, nc.vector.tensor_scalar,
                               nc.vector.scalar_tensor_tensor, nc.vector.tensor_copy)

            def scale_x(n, weights, signal):
                dve.wait_ge(rstd_ready, n + 1)
                for k in range(KT):
                    step(stt(out=h[:, k, :], in0=x[:, k, :], scalar=par(weights + k), in1=rstd[:, :],
                             op0=ALU.mult, op1=ALU.mult), signal)

            def lower_bounds():
                step(tt(lbt[:, :, 0], par(Q_LOGIT + 2, 2), par(Q_LOGIT, 2), ALU.subtract), lb_ready)
                step(nc.vector.memset(lbc[:, 0, :, :], 0.0))
                dve.wait_ge(lb_act, 1)
                step(ts(lbt[:, :, 2], lbt[:, :, 0], 0.0, None, ALU.min))
                step(ts(lbt[:, :, 3], lbt[:, :, 0], 0.0, None, ALU.max))
                settle()
                step(tt(lbc[:, 1, :, 0], lbt[:, :, 2], lbt[:, :, 1], ALU.subtract))
                step(stt(out=lbc[:, 1, :, 1], in0=lbt[:, :, 3], scalar=-1.0, in1=lbt[:, :, 1], op0=ALU.mult, op1=ALU.subtract))
                settle()
                step(tt(lbc[:, 1, :, 2], lbc[:, 1, :, 1], lbc[:, 1, :, 0], ALU.subtract))
                settle()

            def accurate_exp(dst, src, tmp):
                r, k, q = tmp
                step(ts(r, src, -87.0, 88.0, ALU.max, ALU.min))
                settle()
                step(ts(k, r, 1.4426950408889634, MAGIC, ALU.mult, ALU.add))
                settle()
                step(ts(k, k, MAGIC, None, ALU.subtract))
                settle()
                for part in (LN2_HI, LN2_LO):
                    step(stt(out=r, in0=k, scalar=-part, in1=r, op0=ALU.mult, op1=ALU.add))
                    settle()
                step(ts(q, r, 1.0 / 5040, None, ALU.mult))
                for n in (720, 120, 24, 6, 2, 1):
                    settle()
                    step(stt(out=q, in0=q, scalar=1.0 / n, in1=r, op0=ALU.add, op1=ALU.mult))
                step(ts(k.bitcast(I32), k, 127.0, None, ALU.add))
                settle()
                step(ts(k.bitcast(I32), k.bitcast(I32), 23, None, ALU.logical_shift_left))
                settle()
                step(stt(out=dst, in0=q, scalar=1.0, in1=k, op0=ALU.add, op1=ALU.mult))
                settle()

            def s5_phases():
                lr, li = par(Q_LR, LS), par(Q_LI, LS)
                accurate_exp(sw[:, 0, :], par(Q_LS, LS), [sw[:, n, :] for n in (1, 2, 3)])
                step(tt(sw[:, 1, :], lr, sw[:, 0, :], ALU.mult))
                step(tt(sw[:, 2, :], li, sw[:, 0, :], ALU.mult))
                settle()
                step(tt(mag[:, :, :], sw[:, 1, :].unsqueeze(2).to_broadcast([P, LS, NPW]),
                        c("mult")[:, 0:NPW].unsqueeze(1).to_broadcast([P, LS, NPW]), ALU.mult))
                settle()
                flat = mag[:, :, :].rearrange("p s m -> p (s m)")
                accurate_exp(flat, flat, [z[:, :, :].rearrange("p s m -> p (s m)") for z in (are, aim, mtmp)])
                step(ts(sw[:, 2, :], sw[:, 2, :], 1.0 / (2 * np.pi), None, ALU.mult))
                settle()
                step(ts(sw[:, 3, :], sw[:, 2, :], MAGIC, MAGIC, ALU.add, ALU.subtract))
                settle()
                step(tt(sw[:, 2, :], sw[:, 2, :], sw[:, 3, :], ALU.subtract))
                settle()
                step(ts(sw[:, 3, :], sw[:, 2, :], float(SL), None, ALU.mult))
                settle()
                step(ts(sw[:, 4, :], sw[:, 3, :], MAGIC, MAGIC, ALU.add, ALU.subtract))
                settle()
                step(tt(sw[:, 3, :], sw[:, 3, :], sw[:, 4, :], ALU.subtract))
                settle()
                for a, b, src in ((0, NPW, 2), (NPW, NPW + SC, 3)):
                    step(tt(turns[:, :, a:b], sw[:, src, :].unsqueeze(2).to_broadcast([P, LS, b - a]),
                            c("mult")[:, a:b].unsqueeze(1).to_broadcast([P, LS, b - a]), ALU.mult))
                settle()
                step(ts(turnr[:, :, :], turns[:, :, :], MAGIC, MAGIC, ALU.add, ALU.subtract))
                settle()
                step(tt(sinm[:, :, :], turns[:, :, :], turnr[:, :, :], ALU.subtract), ph_ready)
                step(ts(turns[:, :, :], turns[:, :, :], 0.25, None, ALU.add))
                settle()
                step(ts(turnr[:, :, :], turns[:, :, :], MAGIC, MAGIC, ALU.add, ALU.subtract))
                settle()
                step(tt(cosm[:, :, :], turns[:, :, :], turnr[:, :, :], ALU.subtract), ph_ready)

            def s5_coefficients():
                lr, li = par(Q_LR, LS), par(Q_LI, LS)
                dve.wait_ge(sin_ready, 1)
                step(tt(are[:, :, :], mag[:, :, :], cosm[:, :, 0:NPW], ALU.mult))
                step(tt(aim[:, :, :], mag[:, :, :], sinm[:, :, 0:NPW], ALU.mult))
                step(tt(sw[:, 3, :], lr, lr, ALU.mult))
                step(tt(sw[:, 4, :], li, li, ALU.mult))
                settle()
                step(tt(sw[:, 3, :], sw[:, 3, :], sw[:, 4, :], ALU.add))
                step(ts(sw[:, 5, :], are[:, :, 1], -1.0, None, ALU.add))
                settle()
                step(nc.vector.reciprocal(sw[:, 4, :], sw[:, 3, :]))
                step(tt(sw[:, 6, :], sw[:, 5, :], lr, ALU.mult))
                step(tt(sw[:, 7, :], aim[:, :, 1], li, ALU.mult))
                step(tt(sw[:, 8, :], aim[:, :, 1], lr, ALU.mult))
                step(tt(sw[:, 9, :], sw[:, 5, :], li, ALU.mult))
                settle()
                step(tt(sw[:, 6, :], sw[:, 6, :], sw[:, 7, :], ALU.add))
                step(tt(sw[:, 8, :], sw[:, 8, :], sw[:, 9, :], ALU.subtract))
                settle()
                step(tt(sw[:, 10, :], sw[:, 6, :], sw[:, 4, :], ALU.mult))
                step(tt(sw[:, 11, :], sw[:, 8, :], sw[:, 4, :], ALU.mult))
                settle()
                fr = sw[:, 10, :].unsqueeze(2).to_broadcast([P, LS, SL])
                fi = sw[:, 11, :].unsqueeze(2).to_broadcast([P, LS, SL])
                step(tt(gre[:, :, :], are[:, :, 0:SL], fr, ALU.mult))
                step(tt(gt1[:, :, :], aim[:, :, 0:SL], fi, ALU.mult))
                step(tt(gim[:, :, :], are[:, :, 0:SL], fi, ALU.mult))
                step(tt(gt2[:, :, :], aim[:, :, 0:SL], fr, ALU.mult))
                settle()
                step(tt(gre[:, :, :], gre[:, :, :], gt1[:, :, :], ALU.subtract))
                step(tt(gim[:, :, :], gim[:, :, :], gt2[:, :, :], ALU.add), tab_ready)

            def s5_within(layer):
                if layer:
                    dve.wait_ge(y_done, layer * 2)
                step(cp(m4[:, :, :], mag[:, S5T * layer:S5T * layer + S5T, SL:SL + 1].to_broadcast([P, S5T, SC])))
                settle()
                step(nc.vector.memset(m4[:, :, 0:1], 0.0))
                dve.wait_ge(kt_done, layer + 1)
                for q in range(4):
                    for half in range(2):
                        src = wk[0:32, 2 + half, :].rearrange("p (s m) -> p s m", s=4)[:, :, 0:32 * (q + 1)]
                        step(cp(qrt(tmat, q)[:, 4 * half:4 * half + 4, 32 * (3 - q):P], src))
                settle()
                for s in range(S5T):
                    step(stt(out=tmat[:, s, :], in0=c("rev"), scalar=par(Q_S5D + layer * S5T + s), in1=tmat[:, s, :],
                             op0=ALU.mult, op1=ALU.add), tmat_ready if s == S5T - 1 else None)

            def s5_relay(layer):
                dve.wait_ge(chunk_evac, layer * NCH + C_U1 + 1)
                if layer:
                    dve.wait_ge(y_done, layer * 2)
                for a in range(4):
                    src = qrt(u, a)[:, :, 0:TP].rearrange("p t (k j) -> p t k j", j=SL)
                    for q in range(4):
                        dst = qrt(ub, q)[:, :, NS:].rearrange("p (t s) k -> p t s k", t=2)[:, :, a, :]
                        step(cp(dst, src[:, :, :, 3 - q]))
                    for n, dst in enumerate((qrt(ub, 3)[:, :, 0:NS], qrt(us0, 0)[:, :, :])):
                        step(cp(dst.rearrange("p (t s) k -> p t s k", t=2)[:, :, a, :], qrt(u, a)[:, :, TP:TT]),
                             u_ready if a == 3 and n == 1 else None)

            def s5_scan(layer):
                L = slice(S5T * layer, S5T * layer + S5T)
                co, sn = cosm[:, L, NPW:], sinm[:, L, NPW:]
                vr, vi = (wk[:, 2 + n, :].rearrange("p (s k) -> p s k", s=S5T) for n in range(2))
                t = [z.rearrange("p (s k) -> p s k", s=S5T) for z in sv]
                dve.wait_ge(s5v_done, layer + 1)
                if layer:
                    dve.wait_ge(stored, layer)
                if layer:
                    dve.wait_ge(tanh_ready, layer)
                step(tt(t[0], vr, co, ALU.mult))
                step(tt(t[1], vi, sn, ALU.mult))
                step(tt(t[2], vi, co, ALU.mult))
                step(tt(t[3], vr, sn, ALU.mult), s5v_used)
                settle()
                step(tt(t[0], t[0], t[1], ALU.add))
                step(tt(t[2], t[2], t[3], ALU.subtract))
                settle()
                m = m4[:, :, :].rearrange("p s k -> p (s k)")
                step(nc.vector.tensor_tensor_scan(sv[1], m, sv[0], 0.0, ALU.mult, ALU.add))
                step(nc.vector.tensor_tensor_scan(sv[3], m, sv[2], 0.0, ALU.mult, ALU.add))
                settle()
                step(tt(t[0], t[1], co, ALU.mult))
                step(tt(t[2], t[3], sn, ALU.mult))
                settle()
                step(tt(sr[:, :, NS + 1:], t[0], t[2], ALU.subtract))
                settle()
                step(tt(t[0], t[1], sn, ALU.mult))
                step(tt(t[2], t[3], co, ALU.mult))
                dve.wait_ge(s5s_part, layer + 1)
                for n in range(2):
                    step(tt(s5n[:, n, :, :], s5t[:, 2 * n, :, :],
                            wk[:, 4, 64 * n:64 * n + 64].rearrange("p (s b) -> p s b", s=S5T), ALU.add),
                         s5s_used if n else None)
                settle()
                step(tt(si[:, :, NS + 1:], t[0], t[2], ALU.add), s_ready)
                settle()
                for n, s in enumerate((sr, si)):
                    step(cp(s5f[:, n, :], s[:, :, NS + SC]), s5f_ready if n else None)

            def gate(layer):
                dve.wait_ge(l_ready, layer + 1)
                step(stt(out=k3[:, 0:2, :], in0=x3[:, 0:2, :], scalar=0.0, in1=tl[:, 0:2, :], op0=ALU.max, op1=ALU.add), t_ready)
                settle()
                step(stt(out=x3, in0=x3, scalar=0.0, in1=tl, op0=ALU.min, op1=ALU.subtract), ls_ready)
                settle()
                step(ts(x3[:, 2, :], x3[:, 2, :], 1.0 / 16.0, None, ALU.mult))
                if layer:
                    for t in range(2):
                        step(ts(tl[:, t, :], x3[:, t, :], lbc[:, layer, t, 1:2], lbc[:, layer, t, 0:1], ALU.add, ALU.max))
                    dve.wait_ge(lb2_act, layer)
                    settle()
                    step(tt(x3[:, 0:2, :], tl[:, 0:2, :], eb[:, 0:2, :], ALU.add))
                settle()
                step(nc.vector.tensor_tensor_scan(tl.rearrange("p a t -> p (a t)"), c("reset"),
                                                  x3.rearrange("p a t -> p (a t)"), 0.0, ALU.mult, ALU.add), b_ready)
                settle()
                bb = tl[:, :, 0:TP].rearrange("p a (b t) -> p a b t", t=BL)
                step(tt(ke[:, :, 0:TP].rearrange("p a (b t) -> p a b t", t=BL),
                        bb[:, :, :, BL - 1:BL].to_broadcast([P, 3, NB, BL]), bb, ALU.subtract), de_ready)

            def halves(ap, n):
                return ap.rearrange("p g (n w h) -> p g n w h", w=2, h=1 << n)

            def level_diff(layer, n):
                b = halves(tl[:, :, 0:TP], n)
                d = halves(dl[n % 2], n)
                hh = 1 << n
                mid = b[:, :, :, 0, hh - 1:hh].to_broadcast([P, 3, TP // (2 * hh), hh])
                step(tt(d[:, :, :, 1, :], b[:, :, :, 1, :], mid, ALU.subtract))
                step(tt(d[:, :, :, 0, :], mid, b[:, :, :, 0, :], ALU.subtract), ld_ready)

            def level_operands(layer, n):
                dve.wait_ge(lexp_ready, layer * NL + n + 1)
                if n >= 2:
                    dve.wait_ge(lvl_done, layer * NL + n - 1)
                d, kk = halves(dl[n % 2], n), halves(k3[:, :, 0:TP], n)
                qq = halves(qv[:, :, 0:TP], n)
                dst = ql[n % 2].rearrange("p g (n h) -> p g n h", h=1 << n)
                step(tt(halves(kl[n % 2], n)[:, :, :, 0, :], kk[:, :, :, 0, :], d[:, :, :, 0, :], ALU.mult))
                step(tt(dst[:, 0:2], qq[:, 0:2, :, 1, :], d[:, 0:2, :, 1, :], ALU.mult))
                step(tt(dst[:, 2:4], qq[:, 2:4, :, 1, :],
                        d[:, 2:3, :, 1, :].to_broadcast([P, 2, TP >> (n + 1), 1 << n]), ALU.mult), ql_ready)

            def level_scores(layer, n):
                dve.wait_ge(lvl_done, layer * NL + n + 1)
                settle()
                for g in range(2):
                    out = att[:, g].rearrange("p i b t -> p (i b) t")
                    out = halves(out, n)[:, :, :, 1, :]
                    data = wk[:, 2 * (n % 2) + g, :].rearrange("p (g n h) -> p g n h", g=8, h=1 << n)
                    mk = masks[:, n, :].rearrange("p (n h) -> p n h", h=1 << n).unsqueeze(1).to_broadcast([P, 8, 64 >> n, 1 << n])
                    step(nc.vector.copy_predicated(out, mk, data), lvl_used if g else None)

            def decayed_q(layer):
                dve.wait_ge(eb_ready, layer * 2 + 1)
                if layer:
                    dve.wait_ge(ors_ready, layer * 7)
                for hh in range(2):
                    step(stt(out=qm[:, hh:4:2, :], in0=eb[:, 0:2, 0:TP], scalar=c("m64")[:, hh:hh + 1], in1=qv[:, 0:2, 0:TP],
                             op0=ALU.mult, op1=ALU.mult))
                for hd in range(4):
                    step(stt(out=qm[:, 4 + hd, :], in0=eb[:, 2, 0:TP], scalar=c("m32")[:, hd:hd + 1], in1=qv[:, 2 + hd % 2, 0:TP],
                             op0=ALU.mult, op1=ALU.mult), qm_ready if hd == 3 else None)

            def diagonal_scores(layer):
                dve.wait_ge(diag_done, layer + 1)
                if layer:
                    dve.wait_ge(o_done, layer * 3)
                for blk in range(2):
                    for g in range(2):
                        step(tt(att[:, g, :, blk, :], wk[:, 2 * blk + g, :].rearrange("p (i t) -> p i t", i=4),
                                c("ident").unsqueeze(1).to_broadcast([P, 4, P]), ALU.mult), att_ready)
                settle()

            def carry(layer):
                dve.wait_ge(kv_done, layer + 1)
                if layer:
                    dve.wait_ge(stored, layer)
                dve.wait_ge(tr_evac, layer * 6 + 4)
                dec = eb[:, :, 0:TP].rearrange("p a (b t) -> p a b t", t=BL)
                for b in range(NB):
                    kv = wk[:, b % 4, 192 * (b // 4):192 * (b // 4) + 192].rearrange("p (a c) -> p a c", a=3)
                    if b:
                        settle()
                        for t in range(3):
                            step(stt(out=s3[:, t, b + 1, :], in0=s3[:, t, b, :], scalar=dec[:, t, b, BL - 1:BL],
                                     in1=kv[:, t, :], op0=ALU.mult, op1=ALU.add), s3_ready if b == NB - 1 and t == 2 else None)
                    else:
                        step(cp(s3[:, :, 1, :], kv))

            def rotary(layer):
                dve.wait_ge(rot_done, layer + 1)
                step(tt(rt1, r2[:, :, :], c("cos").rearrange("p (a t) -> p a t", a=2), ALU.mult))
                step(tt(rt2, wk[:, 2:4, 0:TT], c("sin").rearrange("p (a t) -> p a t", a=2), ALU.mult), r2_used)
                settle()
                step(tt(r2[:, :, :], rt1, rt2, ALU.add))
                settle()
                for n in range(2):
                    step(ts(rqm[:, n, :], r2[:, 0, :], c("m2")[:, n:n + 1], None, ALU.mult))
                step(tt(kd[:, :], r2[:, 1, 0:TP], c("kdec"), ALU.mult), rqm_ready)

            def ret_decay(layer):
                dve.wait_ge(rsc_done, layer + 1)
                dec = c("decay").rearrange("p (a t) -> p a t", a=4)
                step(tt(attr[:, :, 0:TP], wk[:, 0:4, 0:TP], dec, ALU.mult))
                step(tt(attr[:, :, TP:384], wk[:, 0:4, TP:384], dec[:, :, 0:P], ALU.mult), attr_ready)

            def sample_states(layer):
                dve.wait_ge(q4_ready, layer + 1)
                for n in range(3):
                    dve.wait_ge(vb_done, layer * 3 + n + 1)
                    if n == 0:
                        a, m = 0, 2
                    else:
                        a, m = 1 + n, 1
                    for t in range(a, a + m):
                        step(tt(kvb[:, 512 * t:512 * t + 512].rearrange("p (b c) -> p b c", b=NS),
                                wk[:, t, :].rearrange("p (b c) -> p b c", b=NS),
                                k4[:, t, :].unsqueeze(2).to_broadcast([P, NS, 64]), ALU.mult),
                             vb_used if n == 2 else None)
                settle()
                dve.wait_ge(fs_ready, layer + 1)
                fl = ss[:, :, :, :].rearrange("p a b c -> p (a b c)")
                step(tt(fl, fl, kvb, ALU.add), ss_ready)

            def gather_outputs(layer):
                dve.wait_ge(vd_ready, layer * 3 + 3)
                for kind in range(3):
                    dve.wait_ge(o_done, layer * 3 + kind + 1)
                    step(cp(o[:, 2 * kind:2 * kind + 2, 0:TP], wk[:, kind, :].rearrange("p (t n) -> p t n", t=2)), o_ready)
                dve.wait_ge(rst_done, layer + 1)
                if layer:
                    dve.wait_ge(stored, layer)
                for hd in range(4):
                    step(cp(qrt(retf, hd), qrt(wk, hd)[:, 3, 64 * hd:64 * hd + 64]), st_ready if hd == 3 else None)
                dve.wait_ge(so_done, layer + 1)
                for hh in range(2):
                    rows = slice(64 * hh, 64 * hh + 64)
                    step(cp(o[rows, 0:2, TP:TT], wk[0:64, 4, 0:32].rearrange("p (t b h) -> p t b h", t=2, h=2)[:, :, :, hh]))
                    for n in range(2):
                        src = wk[0:64, 4, 32 + 32 * n:64 + 32 * n].rearrange("p (b t h) -> p t b h", t=2, h=2)[:, :, :, hh]
                        step(cp(o[rows, 2 + 2 * n:4 + 2 * n, TP:TT], src), o_ready if hh and n else None)

            def s5_gelu(layer):
                dve.wait_ge(y_evac, layer * 2 + 2)
                step(tt(yt2, yb, yb, ALU.mult))
                settle()
                step(ts(yt2, yt2, GELU_A, 1.0, ALU.mult, ALU.add))
                settle()
                step(tt(yt2, yt2, yb, ALU.mult), tin_ready)

            def s5_back(layer):
                dve.wait_ge(tanh_ready, layer + 1)
                step(stt(out=yb, in0=yt2, scalar=1.0, in1=yb, op0=ALU.add, op1=ALU.mult))
                settle()
                yv = yb.rearrange("p (t s k) -> p t s k", t=2, s=4)
                for a in range(4):
                    for j in range(4):
                        dst = qrt(yg, a)[:, :, 0:TP].rearrange("p t (k j) -> p t k j", j=SL)[:, :, :, j]
                        step(ts(dst, qrt(yv, j)[:, :, a, NS:], 0.5, None, ALU.mult))
                    step(ts(qrt(yg, a)[:, :, TP:TT], qrt(yv, 0)[:, :, a, 0:NS], 0.5, None, ALU.mult),
                         yg_ready if a == 3 else None)

            def s5_mix(layer):
                dve.wait_ge(glu_tanh, layer + 1)
                step(stt(out=glu[:, :, :], in0=glu[:, :, :], scalar=1.0, in1=yg[:, :, :], op0=ALU.add, op1=ALU.mult))
                settle()
                step(stt(out=zs[:, 0:2, :], in0=glu[:, :, :], scalar=0.5, in1=zs[:, 0:2, :], op0=ALU.mult, op1=ALU.mult), mix_ready)

            def center(layer):
                for t in range(2):
                    dve.wait_ge(mean_done, layer * 2 + t + 1)
                    step(tt(o[:, 4 + t, :], o[:, 4 + t, :], ring_bank(layer, NCH + t)[:, 0:TT], ALU.subtract), mean_used)

            def head_mix(layer):
                dve.wait_ge(ors_ready, layer * 7 + 7)
                for t in range(6):
                    step(stt(out=o[:, t, :], in0=o[:, t, :], scalar=par(Q_HEADG + layer * 6 + t), in1=rs[:, t, :],
                             op0=ALU.mult, op1=ALU.mult))
                settle()
                step(tt(zs[:, 2:8, :], zs[:, 2:8, :], o[:, :, :], ALU.mult), mix_ready)

            def residual(layer, m):
                dve.wait_ge(out_done, layer * KT + m + 1)
                step(tt(x[:, m, :], x[:, m, :], ring_bank(layer, NCH + 8 + m)[:, 0:TT], ALU.add), out_used)

            step(nc.vector.memset(ones_d[:, :], 1.0 / D), zero_ready)
            step(nc.vector.memset(lev[:, :], 0.0))
            step(nc.vector.memset(ub[:, :, :], 0.0))
            step(nc.vector.memset(us0[:, :, :], 0.0))
            step(nc.vector.memset(tmat[:, :, :], 0.0))
            step(nc.vector.memset(sr[:, :, NS:NS + 1], 0.0))
            step(nc.vector.memset(si[:, :, NS:NS + 1], 0.0))
            settle()
            dve.wait_ge(par_in, 16)
            dve.wait_ge(x_in, 16)
            for layer in range(DEPTH):
                scale_x(layer, Q_NORM + layer * KT, h_ready)
                if layer == 0:
                    dve.wait_ge(cst_in, 16)
                    lower_bounds()
                    s5_phases()
                    s5_coefficients()
                gate(layer)
                level_diff(layer, 0)
                dve.wait_ge(chunk_evac, layer * NCH + C_GQ + 1)
                for n in range(2):
                    step(ts(qv[:, 2 + n, :], qraw[:, :], c("m2")[:, n:n + 1], 32 ** -0.5, ALU.mult, ALU.mult),
                         qv_ready if n else None)
                s5_within(layer)
                s5_relay(layer)
                level_diff(layer, 1)
                settle()
                level_operands(layer, 0)
                dve.wait_ge(eb_ready, layer * 2 + 2)
                step(tt(ke[:, :, 0:TP], ke[:, :, 0:TP], k3[:, :, 0:TP], ALU.mult), ke_ready)
                level_operands(layer, 1)
                settle()
                level_diff(layer, 2)
                level_diff(layer, 3)
                s5_scan(layer)
                decayed_q(layer)
                if layer == 0:
                    dve.wait_ge(small_in, 64)
                diagonal_scores(layer)
                for n in range(NL):
                    level_scores(layer, n)
                    if n + 2 < NL:
                        level_operands(layer, n + 2)
                        settle()
                    if n == 0:
                        level_diff(layer, 4)
                rotary(layer)
                carry(layer)
                ret_decay(layer)
                s5_gelu(layer)
                sample_states(layer)
                s5_back(layer)
                gather_outputs(layer)
                center(layer)
                s5_mix(layer)
                head_mix(layer)
                for m in range(KT):
                    residual(layer, m)
            scale_x(DEPTH, Q_FINAL, fin_ready)

        @block.gpsimd
        def _(pool):
            step, settle = chain(pool, pool_step)
            tt, cp = nc.gpsimd.tensor_tensor, nc.gpsimd.tensor_copy

            def s5_matrices(layer):
                L = slice(S5T * layer, S5T * layer + S5T)
                pool.wait_ge(s5m_in, 16 * (layer + 1))
                if layer:
                    pool.wait_ge(y_done, layer * 2)
                    pool.wait_ge(rst_done, layer)
                else:
                    pool.wait_ge(tab_ready, 1)

                for (cr, ci, m, n, re, im, done) in ((gre, gim, 0, SL, bb_re, bb_im, bb_ready),
                                                     (are, aim, 2, NPW, ca_re, ca_im, ca_ready)):
                    for half in range(2):
                        H = slice(4 * half, 4 * half + 4)
                        LH = slice(S5T * layer + 4 * half, S5T * layer + 4 * half + 4)
                        a_r, a_i = (z[:, LH, 0:n].unsqueeze(3).to_broadcast([P, 4, n, 32]) for z in (cr, ci))
                        m_r, m_i = (s5m_t[:, m + i, H, :].unsqueeze(2).to_broadcast([P, 4, n, 32]) for i in range(2))
                        tmp = ptmp[:, :, 0:n, :]
                        step(tt(re[:, H], a_r, m_r, ALU.mult))
                        step(tt(tmp, a_i, m_i, ALU.mult))
                        settle()
                        step(tt(re[:, H], re[:, H], tmp, ALU.subtract))
                        step(tt(im[:, H], a_r, m_i, ALU.mult))
                        settle()
                        step(tt(tmp, a_i, m_r, ALU.mult))
                        settle()
                        step(tt(im[:, H], im[:, H], tmp, ALU.add), done if half and m == 0 else None)
                        settle()
                        if m:
                            step(nc.gpsimd.tensor_scalar(im[:, H], im[:, H], -1.0, None, ALU.mult), done if half else None)

            def s5_samples(layer):
                L = slice(S5T * layer, S5T * layer + S5T)
                a_r = are[:, L, 1:2].to_broadcast([P, S5T, NS])
                a_i = aim[:, L, 1:2].to_broadcast([P, S5T, NS])
                s_r, s_i = s5i[:, layer, 0, :, :], s5i[:, layer, 1, :, :]
                if layer == 0:
                    pool.wait_ge(small_in, 64)
                step(tt(s5t[:, 0, :, :], s_r, a_r, ALU.mult))
                step(tt(s5t[:, 1, :, :], s_i, a_i, ALU.mult))
                step(tt(s5t[:, 2, :, :], s_r, a_i, ALU.mult))
                step(tt(s5t[:, 3, :, :], s_i, a_r, ALU.mult))
                step(cp(sr[:, :, 0:NS], s_r))
                step(cp(si[:, :, 0:NS], s_i))
                settle()
                step(tt(s5t[:, 0, :, :], s5t[:, 0, :, :], s5t[:, 1, :, :], ALU.subtract))
                step(tt(s5t[:, 2, :, :], s5t[:, 2, :, :], s5t[:, 3, :, :], ALU.add), s5s_part)

            def sample_v(layer, n):
                pool.wait_ge(chunk_evac, layer * NCH + (C_I1, C_GV1, C_RV1)[n] + 1)
                if n == 0:
                    pool.wait_ge(lvl_done, layer * NL + NL)
                    pool.wait_ge(lvl_used, layer * NL + NL)
                else:
                    pool.wait_ge(vb_done, layer * 3 + n)
                for t in range(2):
                    step(tt(vd[:, t, :].rearrange("p (b c) -> p b c", b=NS),
                            v[:, 2 * n + t, TP:TT].unsqueeze(2).to_broadcast([P, NS, 64]),
                            c("eye64").unsqueeze(1).to_broadcast([P, NS, 64]), ALU.mult), vd_ready if t else None)

            def sample_gates(layer):
                pool.wait_ge(eb_ready, layer * 2 + 1)
                pool.wait_ge(rqm_ready, layer + 1)
                pool.wait_ge(ss_in, 48 * (layer + 1))
                step(cp(f4[:, 0:3, :], eb[:, :, TP:TT]))
                step(cp(f4[:, 3, :], c("gamma").to_broadcast([P, NS])))
                step(cp(k4[:, 0:3, :], k3[:, :, TP:TT]))
                step(cp(k4[:, 3, :], r2[:, 1, TP:TT]))
                step(cp(q4[:, 0:2, :], qv[:, 0:2, TP:TT]))
                step(tt(q4[:, 2, :], qv[:, 2, TP:TT], qv[:, 3, TP:TT], ALU.add))
                step(cp(q4[:, 3, :], r2[:, 0, TP:TT]))
                settle()
                for t in range(2):
                    step(tt(qs_hg[:, t, :, :], q4[:, t, :].unsqueeze(2).to_broadcast([P, NS, 2]),
                            c("m64").unsqueeze(1).to_broadcast([P, NS, 2]), ALU.mult))
                for n in range(2):
                    step(tt(qs_gr[:, n, :, :], q4[:, 2 + n, :].unsqueeze(2).to_broadcast([P, NS, 4]),
                            c("m32").unsqueeze(1).to_broadcast([P, NS, 4]), ALU.mult), q4_ready if n else None)
                for n in range(4):
                    step(tt(ss[:, n, :, :], ss[:, n, :, :], f4[:, n, :].unsqueeze(2).to_broadcast([P, NS, 64]), ALU.mult),
                         fs_ready if n == 3 else None)

            pool.wait_ge(cst_in, 16)
            s5_matrices(0)
            for layer in range(DEPTH):
                if layer:
                    pool.wait_ge(s_ready, layer)
                s5_samples(layer)
                sample_v(layer, 0)
                sample_gates(layer)
                sample_v(layer, 1)
                sample_v(layer, 2)
                if layer + 1 < DEPTH:
                    s5_matrices(layer + 1)
                pool.wait_ge(s5f_ready, layer + 1)
                pool.wait_ge(s3_ready, layer + 1)
                pool.wait_ge(ss_ready, layer + 1)
                pool.wait_ge(st_ready, layer + 1)
                for dst, src in ((s5p_out[layer], s5f[:, :, :]), (s5s_out[layer], s5n[:, :, :, :]),
                                 (hgp_out[layer], s3[:, 0:2, NB, :]), (glap_out[layer], s3[:, 2, NB, :]),
                                 (retp_out[layer], retf[:, :]), (hgs_out[layer], ss[:, 0:2, :, :]),
                                 (glas_out[layer], ss[:, 2, :, :]), (rets_out[layer], ss[:, 3, :, :])):
                    pool.dma_start(dst, src).then_inc(state_out, 16)
                pool.wait_ge(state_out, 16 * 8 * (layer + 1))
                step(cp(f4[:, 3, 0:1], c("gamma")), stored)


_OUTS = [("y", (P, KT, TT)), ("s5p", (DEPTH, P, 2, S5T)), ("hgp", (DEPTH, P, 2, 64)), ("glap", (DEPTH, P, 64)),
         ("retp", (DEPTH, P, 64)), ("s5s", (DEPTH, P, 2, S5T, NS)), ("hgs", (DEPTH, P, 2, NS, 64)),
         ("glas", (DEPTH, P, NS, 64)), ("rets", (DEPTH, P, NS, 64))]


def layouts(d):
    f = {k: np.ascontiguousarray(a) for k, a in d.items()}
    L = DEPTH
    out = {}
    xa = np.concatenate([f["x_prompt"][0], f["x_sample"][:, 0]], 0)
    out["xt"] = xa.reshape(TT, KT, P).transpose(2, 1, 0)
    w = f["w_in"]
    wi = np.zeros((L, NCH, P, KT, P), np.float32)
    for i, col in enumerate(CHUNKS):
        n = 16 if i == C_LR else P
        wi[:, i, :, :, 0:n] = w[:, :, col:col + n].reshape(L, KT, P, n).transpose(0, 2, 1, 3)
    out["w_in"] = wi
    out["w_out"] = f["w_out"].reshape(L, KT, P, KT, P).transpose(0, 3, 2, 1, 4)

    def tiles(a, n):
        return a.reshape(-1, P).T

    def s5(a):
        return a.reshape(L * S5T, P).T

    heads = np.stack([f["hgrn_norm_w"].reshape(L, 2, P), f["gla_norm_w"].reshape(L, 2, P),
                      f["ret_norm_w"].reshape(L, 2, P)], 1)
    skip = np.tile(f["s5_d"].reshape(L, S5T, 1, 32), (1, 1, 4, 1))
    step = np.repeat(f["s5_log_step"][:, :, None], 64, 2)
    out["par"] = np.concatenate([
        tiles(f["norm_w"], KT), tiles(f["final_norm_w"], KT), tiles(f["hgrn_lb_logits"], 2), tiles(f["gla_b_gate"], 1),
        tiles(heads, 6), tiles(skip, 8), s5(f["s5_lam_re"]), s5(f["s5_lam_im"]), s5(step)], 1)
    m = np.zeros((L, P, 4, S5T, 32), np.float32)
    for i, name in enumerate(("s5_b_re", "s5_b_im", "s5_c_re", "s5_c_im")):
        a = f[name] if i < 2 else f[name].transpose(0, 1, 3, 2)
        a = a.reshape(L, S5T, 2, 64, 16)
        for g in range(2):
            m[:, 64 * g:64 * g + 64, i, :, 16 * g:16 * g + 16] = a[:, :, g].transpose(0, 2, 1, 3)
    out["s5m"] = m
    out["w_glu"] = f["s5_w_glu"].reshape(L, 2, P, 2, P).transpose(2, 0, 1, 3, 4)
    out["w_up"] = f["gla_w_gate_up"].transpose(1, 0, 2)
    s5s = np.stack([f["state_s5_re"], f["state_s5_im"]], 1).reshape(L, 2, NS, S5T, P)
    out["s5_in"] = s5s.transpose(4, 0, 1, 3, 2)
    out["hg_in"] = f["state_hgrn"].reshape(L, NS, 2, P, 64).transpose(0, 3, 2, 1, 4)
    out["gla_in"] = f["state_gla"].reshape(L, NS, P, 64).transpose(0, 2, 1, 3)
    out["ret_in"] = f["state_ret"].reshape(L, NS, P, 64).transpose(0, 2, 1, 3)
    out["cst"], out["msk"] = constants()
    return {k: np.ascontiguousarray(a) for k, a in out.items()}


def kernel(**inputs):
    import concourse.bacc as bacc
    from concourse.bass_utils import run_bass_kernel_spmd

    nc = bacc.Bacc("TRN2", target_bir_lowering=False, num_devices=1)
    arrays = {"in_" + k: a for k, a in layouts(inputs).items()}
    args = [nc.dram_tensor(k, a.shape, mybir.dt.from_np(a.dtype), kind="ExternalInput").ap() for k, a in arrays.items()]
    args += [nc.dram_tensor("out_" + k, shape, F32, kind="ExternalOutput").ap() for k, shape in _OUTS]
    build(nc, *args)
    r = run_bass_kernel_spmd(nc, [arrays], core_ids=[0]).results[0]
    r = {k: np.asarray(r["out_" + k]) for k, _ in _OUTS}
    L = DEPTH
    y = r["y"].transpose(2, 1, 0).reshape(TT, D)
    s5p = r["s5p"].transpose(0, 2, 3, 1).reshape(L, 2, 1, 16, 64)
    s5s = r["s5s"].transpose(0, 2, 4, 3, 1).reshape(L, 2, NS, 16, 64)
    return (y[0:TP].reshape(1, TP, D), y[TP:].reshape(NS, 1, D),
            s5p[:, 0], s5p[:, 1],
            r["hgp"].transpose(0, 2, 1, 3).reshape(L, 1, 4, 64, 64),
            r["glap"].reshape(L, 1, 4, 32, 64), r["retp"].reshape(L, 1, 4, 32, 64),
            s5s[:, 0], s5s[:, 1],
            r["hgs"].transpose(0, 3, 2, 1, 4).reshape(L, NS, 4, 64, 64),
            r["glas"].transpose(0, 2, 1, 3).reshape(L, NS, 4, 32, 64),
            r["rets"].transpose(0, 2, 1, 3).reshape(L, NS, 4, 32, 64))
```

```python
from contextlib import ExitStack

import numpy as np

import concourse.bass as bass
from concourse import mybir

F32 = mybir.dt.float32
I32 = mybir.dt.int32
F32R = mybir.dt.float32r
ALU = mybir.AluOpType
ACT = mybir.ActivationFunctionType

P = 128
DEPTH = 2
D = 1024
KT = D // P
TP = 256
NS = 8
TT = TP + NS
NCH = 25
NZ = 8
NP = NCH - NZ
BL = 32
NB = TP // BL
NL = 5
SL = 4
SC = TP // SL
S5T = 8
NPW = SL + 1
KH = KT // 2
RING = 4
WSLOTS = 4
A_LO_POOL = (0, 1, 2, 4)
A_LO_DVE = (3, 5, 6, 7)
EPS = 1e-6
LN2_HI, LN2_LO = 0.693359375, -2.12194440e-4
MAGIC = 12582912.0
TWO_PI = 6.283185
GELU_A, GELU_C = 0.044715, 0.7978845608028654

(C_F0, C_F1, C_LR, C_Q0, C_Q1, C_GQ, C_GK, C_I0, C_I1, C_GV0, C_GV1,
 C_RQ, C_RK, C_RV0, C_RV1, C_U0, C_U1) = range(NP)
CHUNKS = [768, 896, 2048, 512, 640, 1536, 1664, 1024, 1152, 1792, 1920, 2320, 2448, 2576, 2704, 0, 128,
          256, 384, 1280, 1408, 2064, 2192, 2832, 2960]

(Q_NORM, Q_FINAL, Q_LOGIT, Q_GLAB, Q_HEADG, Q_S5D, Q_LR, Q_LI, Q_LS, Q_END) = np.cumsum(
    [0, DEPTH * KT, KT, DEPTH * 2, DEPTH, DEPTH * 6, DEPTH * S5T, DEPTH * S5T, DEPTH * S5T,
     DEPTH * S5T]).tolist()
_CW = [("m64", 2), ("m32", 4), ("m2", 2), ("gamma", 1), ("mult", NPW + SC),
       ("reset", 3 * TT), ("ident", P), ("rot", P),
       ("cos", TT), ("sin", TT), ("kdec", TP), ("decay", 4 * TP),
       ("mean64", P), ("ones64", P), ("sel_a", P), ("sel_b", P), ("rev", P), ("eye64", 64)]
CST_PARTS = ("m64", "reset", "cos")
CW = {}
_at = 0
for _n, _w in _CW:
    CW[_n] = (_at, _at + _w)
    _at += _w
CN = _at
CST_AT = [CW[_n][0] for _n in CST_PARTS] + [CN]


def constants():
    p = np.arange(P)
    t = {}
    t["ident"] = np.eye(P)
    same64 = (p[:, None] // 64 == p[None, :] // 64)
    t["mean64"] = same64 / 64.0
    t["ones64"] = same64 * 1.0
    t["sel_a"] = (p[:, None] // 64 == p[None, :] // 32) * 1.0
    t["sel_b"] = (p[:, None] // 64 + 2 == p[None, :] // 32) * 1.0
    t["rev"] = ((p[:, None] % 32 == p[None, :] % 32) & (3 - p[:, None] // 32 == p[None, :] // 32)) * 1.0
    half = 16
    rot = np.zeros((P, P))
    for i in p:
        if i % 32 < half:
            rot[i + half, i] = -1.0
        else:
            rot[i - half, i] = 1.0
    t["rot"] = rot
    t["eye64"] = (p[:, None] % 64 == np.arange(64)[None, :]) * 1.0
    t["m64"] = (p[:, None] // 64 == np.arange(2)[None, :]) * 1.0
    t["m32"] = (p[:, None] // 32 == np.arange(4)[None, :]) * 1.0
    t["m2"] = ((p[:, None] // 32) % 2 == np.arange(2)[None, :]) * 1.0
    log_gamma = np.log1p(-np.exp2(-5.0 - np.arange(4)))
    lg = log_gamma[p // 32]
    t["gamma"] = np.exp(lg)[:, None]
    t["mult"] = np.tile(np.concatenate([np.arange(NPW), np.arange(SC)])[None, :], (P, 1))
    pos = np.arange(TT)
    t["reset"] = np.tile(np.where(pos < TP, pos % BL != 0, 0)[None, :], (P, 3))
    pos = np.where(pos < TP, pos, 2048).astype(np.float32)
    inv = (np.float32(10000.0) ** (-np.arange(half, dtype=np.float32) / np.float32(half))).astype(np.float32)
    ang = (pos[None, :] * inv[p % 32 % half][:, None]).astype(np.float32).astype(np.float64)
    t["cos"] = np.cos(ang)
    t["sin"] = np.sin(ang)
    t["kdec"] = np.exp((TP - 1 - np.arange(TP))[None, :] * lg[:, None]) * 32 ** -0.5
    rel = np.arange(TP)[None, :] - p[:, None]
    t["decay"] = np.concatenate([np.where(rel >= 0, np.exp(np.maximum(rel, 0) * g) * 32 ** -0.5, 0.0)
                                 for g in log_gamma], 1)
    big = np.concatenate([t[n] for n, _ in _CW], 1).astype(np.float32)
    mask = np.zeros((P, NL, 64), np.int32)
    for lev in range(NL):
        h = 1 << lev
        right = np.array([x for x in range(P) if (x // h) % 2 == 1])
        mask[:, lev, :] = (p[:, None] // (2 * h) == right[None, :] // (2 * h)) & ((p[:, None] // h) % 2 == 0)
    return big, mask


def build(nc, xt, w_in, w_out, par_d, s5m, w_glu, w_up, s5_in, hg_in, gla_in, ret_in, cst, msk,
          y_out, s5p_out, hgp_out, glap_out, retp_out, s5s_out, hgs_out, glas_out, rets_out):
    with ExitStack() as ctx:
        def sb(name, *shape, dt=F32):
            return ctx.enter_context(nc.sbuf_tensor(name, [P, *shape], dt))

        def sem(name):
            return ctx.enter_context(nc.semaphore(name))

        x = sb("x", KT, TT)
        a_hi, a_lo = sb("a_hi", KT, TT, dt=F32R), sb("a_lo", KT, TT, dt=F32R)
        w_hi, w_lo = sb("w_hi", WSLOTS, KH, P, dt=F32R), sb("w_lo", WSLOTS, KH, P, dt=F32R)
        wring = sb("wring", RING, KH, P)
        zs = sb("zs", KT, TT)
        h = zs
        parm = sb("parm", Q_END)
        cs = sb("cs", CN)
        masks = sb("masks", NL, 64, dt=I32)
        ones_d = sb("ones_d", P)
        qraw = sb("qraw", TT)
        qv = sb("qv", 4, TT)
        gates = sb("gates", 6, TT)
        x3, tl = gates[:, 0:3, :], gates[:, 3:6, :]
        k3 = sb("k3", 3, TT)
        eb = sb("eb", 3, TT)
        ke = sb("ke", 3, TT)
        u = sb("u", 2, TT)
        lr_t, rstd = u[:, 0, :], u[:, 1, :]
        v = sb("v", 6, TT)
        o = v
        r2 = ke[:, 0:2, :]
        rqm = sb("rqm", 2, TT)
        kdr = sb("kdr", 2 * TP)
        kd = kdr[:, 0:TP]
        krt = kdr[:, TP:].rearrange("p (b c) -> p b c", b=2)
        ptmp = kdr[:, 0:S5T // 4 * NPW * 32].rearrange("p (s n c) -> p s n c", s=S5T // 4, n=NPW)
        qm = sb("qm", 8, TP)
        rs = qm[:, :, :].rearrange("p a t -> p (a t)")[:, 0:6 * TT].rearrange("p (a t) -> p a t", a=6)
        lev = sb("lev", 4224)
        dl = [lev[:, 768 * i:768 * i + 768].rearrange("p (g t) -> p g t", g=3) for i in range(2)]
        kl = [lev[:, 1536 + 768 * i:2304 + 768 * i].rearrange("p (g t) -> p g t", g=3) for i in range(2)]
        ql = [lev[:, 3072 + 512 * i:3584 + 512 * i].rearrange("p (g t) -> p g t", g=4) for i in range(2)]
        kvb = lev[:, 0:2048]
        vd = lev[:, 2048:3072].rearrange("p (g n) -> p g n", g=2)
        osq = lev[:, 2048:2048 + 6 * TT].rearrange("p (g t) -> p g t", g=6)
        att = sb("att", 2, 4, 2, P)
        attr = gates[:, :, :].rearrange("p a t -> p (a t)")[:, 0:4 * 384].rearrange("p (a t) -> p a t", a=4)
        rt1, rt2 = gates[:, 0:2, :], gates[:, 2:4, :]
        tok = sb("tok", 18 * P)
        vt = tok[:, 0:12 * P].rearrange("p (b t c) -> p b t c", b=2, t=6)
        ket = tok[:, 12 * P:18 * P].rearrange("p (b t c) -> p b t c", b=2, t=3)
        s3 = sb("s3", 3, NB + 1, 64)
        retf = sb("retf", 64)
        ss = sb("ss", 4, NS, 64)
        f4 = sb("f4", 4, NS)
        k4 = sb("k4", 4, NS)
        q4 = sb("q4", 4, NS)
        qs_hg = sb("qs_hg", 2, NS, 2)
        qs_gr = sb("qs_gr", 2, NS, 4)
        lbc = sb("lbc", 2, 2, 3)
        lbt = sb("lbt", 2, 4)
        s5m_t = sb("s5m_t", 4, S5T, 32)
        LS = DEPTH * S5T
        sw = sb("sw", 12, LS)
        turn4 = sb("turn4", LS)
        sinp, cosp = sb("sinp", LS, NPW), sb("cosp", LS, NPW)
        sinc, cosc = sb("sinc", S5T, SC), sb("cosc", S5T, SC)
        turns, turnr = (lev[:, 3072 + i * S5T * SC:3072 + (i + 1) * S5T * SC] for i in range(2))
        mag = sb("mag", LS, NPW)
        are = sb("are", LS, NPW)
        aim = sb("aim", LS, NPW)
        mtmp = sb("mtmp", LS, NPW)
        gre = sb("gre", LS, SL)
        gim = sb("gim", LS, SL)
        gt1 = sb("gt1", LS, SL)
        gt2 = sb("gt2", LS, SL)
        m4 = sb("m4", S5T, SC)
        bb_re, bb_im, bb_t = (lev[:, i * 1024:i * 1024 + 1024].rearrange("p (s j c) -> p s j c", s=S5T, j=SL) for i in range(3))
        ca_re = sb("ca_re", S5T, NPW, 32)
        ca_im = sb("ca_im", S5T, NPW, 32)
        gtr = qm[:, :, :].rearrange("p a t -> p (a t)").rearrange("p (n s m) -> p n s m", n=2, s=S5T)
        tmat = sb("tmat", S5T, P)
        ub = sb("ub", S5T, NS + SC)
        us0 = sb("us0", S5T, NS)
        sr = sb("sr", S5T, NS + SC + 1)
        si = sb("si", S5T, NS + SC + 1)
        s5i = sb("s5i", DEPTH, 2, S5T, NS)
        s5n = sb("s5n", 2, S5T, NS)
        s5t = sb("s5t", 4, S5T, NS)
        s5f = sb("s5f", 2, S5T)
        sv = [lev[:, 512 * i:512 * i + 512] for i in range(4)]
        NY = S5T * (NS + SC)
        yb, yt2 = lev[:, 3072:3072 + NY], lev[:, 3072 + NY:3072 + 2 * NY]
        yg = u
        wg = sb("wg", 2, 2, P)
        wup = sb("wup", DEPTH, P)
        glu = rqm

        pr = [ctx.enter_context(nc.psum_tensor(f"pr{i}", [P, 512], F32)) for i in range(3)]
        wk = ctx.enter_context(nc.psum_tensor("wk", [P, 5, 512], F32))

        def c(name):
            return cs[:, CW[name][0]:CW[name][1]]

        x_in = [sem(f"x_in{i}") for i in range(2)]
        par_in, small_in = sem("par_in"), sem("small_in")
        cst_in = [sem(f"cst_in{i}") for i in range(3)]
        w_in_sem = [sem(f"w_slot{i}") for i in range(RING)]
        wup_in, angles_ready = sem("wup_in"), sem("angles_ready")
        wg_in = sem("wg_in")
        s5m_in = [sem(f"s5m_in{i}") for i in range(DEPTH)]
        state_out = sem("state_out")
        s5s_used, s5f_ready, r2_used = (sem(n) for n in ("s5s_used", "s5f_ready", "r2_used"))
        ss_in = [sem(f"ss_in{i}") for i in range(DEPTH)]
        out_sem = sem("out_sem")
        whi_ready, wlo_ready, half_done = sem("whi_ready"), sem("wlo_ready"), sem("half_done")
        ahi_ready, alo_pool, alo_dve = sem("ahi_ready"), sem("alo_pool"), sem("alo_dve")
        stored = sem("stored")
        ms_done, proj_done, lrup_done, s5v_done, diag_done, lvl_done, tr_done, kv_done = (
            sem(n) for n in ("ms_done", "proj_done", "lrup_done", "s5v_done", "diag_done", "lvl_done", "tr_done", "kv_done"))
        rot_done, rsc_done, y_done, vb_done, o_done, rst_done, so_done, glu_done = (
            sem(n) for n in ("rot_done", "rsc_done", "y_done", "vb_done", "o_done", "rst_done", "so_done", "glu_done"))
        mean_done, var_done, out_done, gtr_done, kt_done = (
            sem(n) for n in ("mean_done", "var_done", "out_done", "gtr_done", "kt_done"))
        act_step, sq_ready, rstd_ready, chunk_evac, l_ready, k3_ready, eb_ready, lexp_ready, tr_evac = (
            sem(n) for n in ("act_step", "sq_ready", "rstd_ready", "chunk_evac", "l_ready", "k3_ready", "eb_ready", "lexp_ready", "tr_evac"))
        gtr_evac, sin_ready, y_evac, tanh_ready, glu_tanh, osq_ready, ors_ready, lb_act, lb2_act = (
            sem(n) for n in ("gtr_evac", "sin_ready", "y_evac", "tanh_ready", "glu_tanh", "osq_ready", "ors_ready", "lb_act", "lb2_act"))
        dve_step, h_ready, t_ready, ls_ready, b_ready, de_ready, ld_ready, ql_ready, att_ready, lvl_used = (
            sem(n) for n in ("dve_step", "h_ready", "t_ready", "ls_ready", "b_ready", "de_ready", "ld_ready", "ql_ready", "att_ready", "lvl_used"))
        lb_ready, ph_ready, tab_ready, tmat_ready, u_ready, s5v_used, s_ready, ke_ready, qv_ready = (
            sem(n) for n in ("lb_ready", "ph_ready", "tab_ready", "tmat_ready", "u_ready", "s5v_used", "s_ready", "ke_ready", "qv_ready"))
        s3_ready, rqm_ready, attr_ready, kvb_ready, ss_ready, tin_ready, yg_ready, qm_ready, vb_used, ym_ready = (
            sem(n) for n in ("s3_ready", "rqm_ready", "attr_ready", "kvb_ready", "ss_ready", "tin_ready", "yg_ready", "qm_ready", "vb_used", "ym_ready"))
        o_ready, mean_used, mix_ready, out_used, fin_ready, st_ready, lm_ready, zero_ready = (
            sem(n) for n in ("o_ready", "mean_used", "mix_ready", "out_used", "fin_ready", "st_ready", "lm_ready", "zero_ready"))
        pool_step, bb_ready, ca_ready, fs_ready, vd_ready, q4_ready, s5s_part, set_ready = (
            sem(n) for n in ("pool_step", "bb_ready", "ca_ready", "fs_ready", "vd_ready", "q4_ready", "s5s_part", "set_ready"))

        def chain(eng, steps):
            last = [None, {}]

            def step(ins, signal=None):
                s = signal if signal is not None else steps
                n = last[1].get(s.name, 0) + 1
                last[1][s.name] = n
                ins.then_inc(s, 1)
                last[0] = (s, n)

            def settle():
                eng.wait_ge(*last[0])
            return step, settle

        def par(col, n=1):
            return parm[:, col:col + n]

        def qrt(ap, q):
            return ap[32 * q:32 * q + 32]

        USES = NCH + 2 + 6 + KT

        def ring_free(eng, layer, i):
            i -= 3
            if i < 0:
                layer, i = layer - 1, i + USES
            if layer < 0:
                return
            if i < NCH:
                eng.wait_ge(chunk_evac, layer * NCH + i + 1)
            elif i < NCH + 2:
                eng.wait_ge(mean_used, layer * 2 + i - NCH + 1)
            elif i < NCH + 8:
                eng.wait_ge(ors_ready, layer * 7 + i - NCH - 2 + 1)
            else:
                eng.wait_ge(out_used, layer * KT + i - NCH - 8 + 1)

        def half_used(eng, j):
            if j < 0:
                return
            before, i = divmod(j // 2, NCH + KT)
            if j % 2 == 0:
                eng.wait_ge(half_done, j // 2 + 1)
            elif i < NCH:
                eng.wait_ge(proj_done, before * NCH + i + 1)
            else:
                eng.wait_ge(out_done, before * KT + i - NCH + 1)

        def part_ready(eng, n, k):
            if k in A_LO_DVE:
                eng.wait_ge(alo_dve, n * len(A_LO_DVE) + A_LO_DVE.index(k) + 1)
            else:
                eng.wait_ge(alo_pool, n * len(A_LO_POOL) + A_LO_POOL.index(k) + 1)

        def ring_bank(layer, i):
            return pr[(layer * USES + i) % 3]

        block = ctx.enter_context(nc.Block())

        @block.sync
        def _(sp):
            def const(i):
                part = slice(CST_AT[i], CST_AT[i + 1])
                sp.dma_start(cs[:, part], cst[:, part]).then_inc(cst_in[i], 16)

            sp.dma_start(parm[:, :], par_d).then_inc(par_in, 16)
            const(0)
            for i in range(2):
                half = slice(KT // 2 * i, KT // 2 * (i + 1))
                sp.dma_start(x[:, half, :], xt[:, half, :]).then_inc(x_in[i], 16)
            use = 0

            def chunk(src):
                nonlocal use
                for half in (slice(0, KH), slice(KH, KT)):
                    if use >= RING:
                        sp.wait_ge(wlo_ready, use - RING + 1)
                    sp.dma_start(wring[:, use % RING, :, :], src[:, half]).then_inc(w_in_sem[use % RING], 16)
                    use += 1

            for layer in range(DEPTH):
                for i in range(NCH):
                    chunk(w_in[layer, i])
                    if layer == 0 and i == 1:
                        sp.dma_start(wup[0:16, :, :], w_up).then_inc(wup_in, 16)
                    if layer == 0 and i == 2:
                        const(1)
                        sp.dma_start(s5m_t[:, :, :, :], s5m[0]).then_inc(s5m_in[0], 16)
                    if layer == 0 and i == 6:
                        const(2)
                    if layer == 0 and i == 5:
                        sp.dma_start(s5i[:, :, :, :, :], s5_in).then_inc(small_in, 16)
                        sp.dma_start(masks[:, :, :], msk).then_inc(small_in, 16)
                        sp.dma_start(wg[:, :, :, :], w_glu[0]).then_inc(small_in, 16)
                    if layer == 0 and i == 8:
                        sp.dma_start(ss[:, 0:2, :, :], hg_in[0]).then_inc(ss_in[0], 16)
                        sp.dma_start(ss[:, 2, :, :], gla_in[0]).then_inc(ss_in[0], 16)
                        sp.dma_start(ss[:, 3, :, :], ret_in[0]).then_inc(ss_in[0], 16)
                for i in range(KT):
                    chunk(w_out[layer, i])
            sp.wait_ge(fin_ready, KT)
            sp.dma_start(y_out, h[:, :, :]).then_inc(out_sem, 16)
            sp.wait_ge(out_sem, 16)

        @block.tensor
        def _(pe):
            use = [0]

            def product(dst, done, operand_ready=None):
                for half in range(2):
                    slot = use[0] % WSLOTS
                    use[0] += 1
                    pe.wait_ge(wlo_ready, use[0])
                    for n in range(KH):
                        k = KH * half + n
                        if operand_ready:
                            operand_ready(k)
                        for p, (w, a) in enumerate(((w_hi, a_hi), (w_hi, a_lo), (w_lo, a_hi))):
                            mm = nc.tensor.matmul(dst, w[:, slot, n, :], a[:, k, :],
                                                  start=(k == 0 and p == 0), stop=(k == KT - 1 and p == 2))
                    mm.then_inc(done if half else half_done, 1)

            def mean_square(n):
                for k in range(KT):
                    pe.wait_ge(sq_ready, n * KT + k + 1)
                    mm = nc.tensor.matmul(wk[:, 0, 0:TT], ones_d[:, :], h[:, k, :], start=(k == 0), stop=(k == KT - 1))
                mm.then_inc(ms_done, 1)

            def project(layer, i):
                ring_free(pe, layer, i)
                product(ring_bank(layer, i)[:, 0:TT], proj_done,
                        (lambda k: part_ready(pe, 2 * layer, k)) if i == 0 else None)

            def low_rank(layer):
                pe.wait_ge(chunk_evac, layer * NCH + C_LR + 1)
                if layer == 0:
                    pe.wait_ge(wup_in, 16)
                nc.tensor.matmul(wk[:, 1, 0:TT], wup[0:16, layer, :], lr_t[0:16, :], start=True, stop=True)\
                    .then_inc(lrup_done, 1)

            def s5_turn(layer):
                pe.wait_ge(bb_ready, layer + 1)
                pe.wait_ge(attr_ready, layer + 1)
                for r in range(4):
                    for n in range(4):
                        src = (bb_re, bb_im)[r // 2][:, 4 * (r % 2) + n, :, :]
                        mm = nc.tensor.transpose(wk[:, r, P * n:P * n + P], src.rearrange("p j c -> p (j c)"), c("ident"))
                    mm.then_inc(gtr_done, 1)

            def s5_response(layer):
                pe.wait_ge(ca_ready, layer + 1)
                pe.wait_ge(gtr_evac, layer * 4 + 4)
                for s in range(S5T):
                    for n, (b, ca) in enumerate(((bb_re, ca_re), (bb_im, ca_im))):
                        mm = nc.tensor.matmul(wk[0:32, 2 + s // 4, P * (s % 4):P * (s % 4) + P], b[:, s, 0, :],
                                              ca[:, s, 0:SL, :].rearrange("p j c -> p (j c)"),
                                              start=(n == 0), stop=(n == 1))
                mm.then_inc(kt_done, 1)

            def s5_inputs(layer):
                pe.wait_ge(u_ready, layer + 1)
                pe.wait_ge(tr_evac, layer * 6 + 6)
                for n in range(2):
                    for s in range(S5T):
                        nc.tensor.matmul(wk[:, n, SC * s:SC * s + SC], gtr[:, n, s, :], ub[:, s, NS:],
                                         start=True, stop=True)
                for n in range(2):
                    for s in range(S5T):
                        mm = nc.tensor.matmul(wk[:, 4, 64 * n + NS * s:64 * n + NS * s + NS], gtr[:, n, s, :], us0[:, s, :],
                                              start=True, stop=True)
                mm.then_inc(s5v_done, 1)

            def s5_outputs(layer, n):
                if n == 0:
                    pe.wait_ge(s_ready, layer + 1)
                if n == 0:
                    pe.wait_ge(s5s_used, layer + 1)
                if n:
                    pe.wait_ge(y_evac, layer * 2 + 1)
                for s in range(4 * n, 4 * n + 4):
                    dst = wk[:, 4, 72 * (s - 4 * n):72 * (s - 4 * n) + 72]
                    nc.tensor.matmul(dst, tmat[:, s, :], ub[:, s, :], start=True, stop=False)
                    nc.tensor.matmul(dst, ca_re[:, s, 1:NPW, :].rearrange("p j c -> p (j c)"), sr[:, s, 0:72],
                                     start=False, stop=False)
                    mm = nc.tensor.matmul(dst, ca_im[:, s, 1:NPW, :].rearrange("p j c -> p (j c)"), si[:, s, 0:72],
                                          start=False, stop=True)
                mm.then_inc(y_done, 1)

            def diagonal(layer):
                pe.wait_ge(qv_ready, layer + 1)
                if layer == 0:
                    pe.wait_ge(cst_in[1], 16)
                    pe.wait_ge(cst_in[2], 16)
                    pe.wait_ge(small_in, 48)
                pe.wait_ge(k3_ready, layer + 1)
                for blk in range(2):
                    for g in range(2):
                        rows = slice(64 * g, 64 * g + 64)
                        for i in range(4):
                            mm = nc.tensor.matmul(wk[:, 2 * blk + g, P * i:P * i + P],
                                                  k3[rows, min(i, 2), P * blk:P * blk + P],
                                                  qv[rows, i, P * blk:P * blk + P], start=True, stop=True)
                mm.then_inc(diag_done, 1)

            def level(layer, n):
                pe.wait_ge(ql_ready, layer * NL + n + 1)
                if n < 2:
                    pe.wait_ge(att_ready, layer * 4 + (2 if n == 0 else 4))
                else:
                    pe.wait_ge(lvl_used, layer * NL + n - 1)
                for g in range(2):
                    rows = slice(64 * g, 64 * g + 64)
                    for i in range(4):
                        for blk in range(2):
                            a = (2 * i + blk) * 64
                            mm = nc.tensor.matmul(wk[:, 2 * (n % 2) + g, a:a + 64],
                                                  kl[n % 2][rows, min(i, 2), P * blk:P * blk + P],
                                                  ql[n % 2][rows, i, 64 * blk:64 * blk + 64], start=True, stop=True)
                mm.then_inc(lvl_done, 1)

            def turn(layer, r, tiles):
                if r:
                    pe.wait_ge(tr_evac, layer * 6 + r)
                else:
                    if layer:
                        pe.wait_ge(o_ready, layer * 4)
                for n, t in enumerate(tiles):
                    mm = nc.tensor.transpose(wk[:, 4, P * n:P * n + P], t, c("ident"))
                mm.then_inc(tr_done, 1)

            def block_states(layer):
                pe.wait_ge(tr_evac, layer * 6 + 4)
                pe.wait_ge(r2_used, layer + 1)
                pe.wait_ge(lvl_used, layer * NL + NL)
                for blk in range(2):
                    for j in range(4):
                        rows = slice(32 * j, 32 * j + 32)
                        for hd in range(4):
                            t, hh = hd // 2, hd % 2
                            nc.tensor.matmul(wk[64 * hh:64 * hh + 64, j, (3 * blk + t) * 64:(3 * blk + t) * 64 + 64],
                                             ket[rows, blk, t, 64 * hh:64 * hh + 64],
                                             vt[rows, blk, t, 64 * hh:64 * hh + 64], start=True, stop=True)
                        for hd in range(4):
                            mm = nc.tensor.matmul(wk[32 * hd:32 * hd + 32, j, (3 * blk + 2) * 64:(3 * blk + 2) * 64 + 64],
                                                  ket[rows, blk, 2, 32 * hd:32 * hd + 32],
                                                  vt[rows, blk, 2 + hd // 2, 64 * (hd % 2):64 * (hd % 2) + 64],
                                                  start=True, stop=True)
                mm.then_inc(kv_done, 1)

            def rotate(layer):
                pe.wait_ge(chunk_evac, layer * NCH + C_RK + 1)
                pe.wait_ge(lvl_used, layer * NL + 4)
                for n in range(2):
                    mm = nc.tensor.matmul(wk[:, 2 + n, 0:TT], c("rot"), r2[:, n, :], start=True, stop=True)
                mm.then_inc(rot_done, 1)

            def ret_scores(layer):
                pe.wait_ge(rqm_ready, layer + 1)
                pe.wait_ge(s3_ready, layer + 1)
                for hd in range(4):
                    rows = slice(64 * (hd // 2), 64 * (hd // 2) + 64)
                    nc.tensor.matmul(wk[:, hd, 0:TP], r2[rows, 1, 0:P], rqm[rows, hd % 2, 0:TP], start=True, stop=True)
                    mm = nc.tensor.matmul(wk[:, hd, TP:384], r2[rows, 1, P:TP], rqm[rows, hd % 2, P:TP], start=True, stop=True)
                mm.then_inc(rsc_done, 1)

            def sample_v(layer, n):
                pe.wait_ge(vd_ready, layer * 3 + n + 1)
                if n == 0:
                    pe.wait_ge(s5v_used, layer + 1)
                    pe.wait_ge(tmat_ready, layer + 1)
                    for t in range(2):
                        mm = nc.tensor.matmul(wk[:, t, :], c("ones64"), vd[:, t, :], start=True, stop=True)
                else:
                    for t in range(2):
                        mm = nc.tensor.matmul(wk[:, 1 + n, :], c(("sel_a", "sel_b")[t]), vd[:, t, :],
                                              start=(t == 0), stop=(t == 1))
                mm.then_inc(vb_done, 1)

            def outputs(layer):
                pe.wait_ge(vb_used, layer + 1)
                pe.wait_ge(lvl_used, layer * NL + NL)
                pe.wait_ge(qm_ready, layer + 1)
                pe.wait_ge(tr_evac, layer * 6 + 6)
                for kind in range(2):
                    for t in range(2):
                        for hh in range(2):
                            rows = slice(64 * hh, 64 * hh + 64)
                            g, i = (hh, t) if kind == 0 else (t, 2 + hh)
                            vtile = 2 * kind + t
                            for blk in range(2):
                                nc.tensor.matmul(wk[rows, kind, TP * t + P * blk:TP * t + P * blk + P],
                                                 vt[:, blk, vtile, rows], att[:, g, i, blk, :],
                                                 start=(t == 0 and blk == 0), stop=False, skip_group_check=True)
                            for b in range(1, NB):
                                st = s3[:, t if kind == 0 else 2, b, :]
                                q = qm[:, 4 * kind + 2 * t + hh, BL * b:BL * b + BL]
                                mm = nc.tensor.matmul(wk[rows, kind, TP * t + BL * b:TP * t + BL * b + BL], st, q,
                                                      start=False, stop=(t == 1 and b == NB - 1), skip_group_check=True)
                    mm.then_inc(o_done, 1)
                for t in range(2):
                    for hh in range(2):
                        rows = slice(64 * hh, 64 * hh + 64)
                        nc.tensor.matmul(wk[rows, 2, TP * t:TP * t + TP], vt[:, 0, 4 + t, rows], attr[:, 2 * t + hh, 0:TP],
                                         start=(t == 0), stop=False, skip_group_check=True)
                        mm = nc.tensor.matmul(wk[rows, 2, TP * t + P:TP * t + TP], vt[:, 1, 4 + t, rows],
                                              attr[:, 2 * t + hh, TP:384], start=False, stop=(t == 1), skip_group_check=True)
                mm.then_inc(o_done, 1)
                for blk in range(2):
                    mm = nc.tensor.matmul(wk[:, 3, 0:TP], krt[:, blk, :],
                                          vt[:, blk, 4:6, :].rearrange("p a c -> p (a c)"), start=(blk == 0), stop=(blk == 1))
                mm.then_inc(rst_done, 1)

            def sample_outputs(layer):
                pe.wait_ge(ss_ready, layer + 1)
                pe.wait_ge(q4_ready, layer + 1)
                pe.wait_ge(y_evac, layer * 2 + 2)
                for t in range(2):
                    for b in range(NS):
                        a = 2 * (NS * t + b)
                        nc.tensor.matmul(wk[0:64, 4, a:a + 2], ss[:, t, b, :], qs_hg[:, t, b, :], start=True, stop=True)
                for n in range(2):
                    for b in range(NS):
                        a = 32 + 4 * (NS * n + b)
                        mm = nc.tensor.matmul(wk[0:64, 4, a:a + 4], ss[:, 2 + n, b, :], qs_gr[:, n, b, :], start=True, stop=True)
                mm.then_inc(so_done, 1)

            def glu_gate(layer):
                pe.wait_ge(yg_ready, layer + 1)
                if layer:
                    pe.wait_ge(wg_in, 16 * layer)
                pe.wait_ge(st_ready, layer + 1)
                pe.wait_ge(o_ready, layer * 4 + 4)
                for m in range(2):
                    for k in range(2):
                        mm = nc.tensor.matmul(wk[:, 2 + m, 0:TT], wg[:, k, m, :], yg[:, k, :],
                                              start=(k == 0), stop=(k == 1))
                mm.then_inc(glu_done, 1)

            def head_norms(layer):
                pe.wait_ge(o_ready, layer * 4 + 4)
                for t in range(2):
                    i = NCH + t
                    ring_free(pe, layer, i)
                    nc.tensor.matmul(ring_bank(layer, i)[:, 0:TT], c("mean64"), o[:, 4 + t, :], start=True, stop=True)\
                        .then_inc(mean_done, 1)
                for t in range(6):
                    i = NCH + 2 + t
                    ring_free(pe, layer, i)
                    pe.wait_ge(osq_ready, layer * 2 + (1 if t < 4 else 2))
                    nc.tensor.matmul(ring_bank(layer, i)[:, 0:TT], c("mean64"), osq[:, t, :], start=True, stop=True)\
                        .then_inc(var_done, 1)

            def project_out(layer, m):
                i = NCH + 8 + m
                ring_free(pe, layer, i)
                product(ring_bank(layer, i)[:, 0:TT], out_done,
                        (lambda k: part_ready(pe, 2 * layer + 1, k)) if m == 0 else None)

            pe.wait_ge(zero_ready, 1)
            for layer in range(DEPTH):
                mean_square(layer)
                for i in range(NCH):
                    project(layer, i)
                    if i == C_Q0:
                        low_rank(layer)
                    if i == C_I0:
                        diagonal(layer)
                    if C_I1 <= i < C_I1 + NL:
                        level(layer, i - C_I1)
                    if i == C_GV0:
                        pe.wait_ge(ke_ready, layer + 1)
                        turn(layer, 0, [ke[:, t, 0:P] for t in range(3)])
                    if i == C_GV1:
                        turn(layer, 1, [ke[:, t, P:TP] for t in range(3)])
                    if i == C_RQ:
                        turn(layer, 2, [v[:, t, P * b:P * b + P] for b in range(2) for t in range(2)])
                    if i == C_RK:
                        turn(layer, 3, [v[:, 2 + t, P * b:P * b + P] for b in range(2) for t in range(2)])
                    if i == C_RV0:
                        rotate(layer)
                    if i == C_RV1:
                        block_states(layer)
                    if i == C_U0:
                        pe.wait_ge(chunk_evac, layer * NCH + C_RV1 + 1)
                        turn(layer, 4, [v[:, 4 + t, P * b:P * b + P] for b in range(2) for t in range(2)])
                    if i == C_U1:
                        pe.wait_ge(rqm_ready, layer + 1)
                        turn(layer, 5, [kd[:, P * b:P * b + P] for b in range(2)])
                    if i == NP:
                        ret_scores(layer)
                    if i == NP + 1:
                        s5_turn(layer)
                    if i == NP + 2:
                        s5_response(layer)
                        s5_inputs(layer)
                    if i == NP + 4:
                        sample_v(layer, 0)
                    if i == NP + 5:
                        sample_v(layer, 1)
                    if i == NP + 6:
                        sample_v(layer, 2)
                        s5_outputs(layer, 0)
                    if i == NP + 7:
                        s5_outputs(layer, 1)
                outputs(layer)
                sample_outputs(layer)
                glu_gate(layer)
                head_norms(layer)
                for m in range(KT):
                    project_out(layer, m)
            mean_square(DEPTH)

        @block.scalar
        def _(act):
            step, settle = chain(act, act_step)
            fn = nc.scalar.activation

            def use_logs():
                nc.scalar.preload_act_table_set("natural_log_exp_and_others")

            def use_silu():
                nc.scalar.preload_act_table_set("silu_and_others")

            def rsqrt_of(src, dst, signal):
                step(fn(dst, src, ACT.Ln, bias=EPS))
                settle()
                step(fn(dst, dst, ACT.Exp, scale=-0.5), signal)

            def norm(n):
                for k in range(KT):
                    if n == 0 and k % (KT // 2) == 0:
                        act.wait_ge(x_in[2 * k // KT], 16)
                    if n:
                        act.wait_ge(out_used, (n - 1) * KT + k + 1)
                    step(fn(h[:, k, :], x[:, k, :], ACT.Square), sq_ready)
                    if n and k < KT - 1:
                        split_weights((n - 1) * (NCH + KT) + NCH + k + 2)
                act.wait_ge(ms_done, n + 1)
                if n:
                    act.wait_ge(h_ready, n * KT)
                rsqrt_of(wk[:, 0, 0:TT], rstd, rstd_ready)
                if n:
                    split_weights(n * (NCH + KT) + 1)

            def split_weights(chunk):
                if chunk >= DEPTH * (NCH + KT):
                    return
                for j in (2 * chunk, 2 * chunk + 1):
                    act.wait_ge(w_in_sem[j % RING], 16 * (j // RING + 1))
                    half_used(act, j - WSLOTS)
                    step(fn(w_hi[:, j % WSLOTS, :, :], wring[:, j % RING, :, :], ACT.Copy), whi_ready)

            def split_operand(n):
                for k in range(KT):
                    if n % 2 == 0:
                        act.wait_ge(h_ready, n // 2 * KT + k + 1)
                        if n and k == 0:
                            act.wait_ge(out_done, n // 2 * KT)
                    else:
                        act.wait_ge(mix_ready, n // 2 * KT + k + 1)
                        if k == 0:
                            act.wait_ge(proj_done, (n // 2 + 1) * NCH)
                    step(fn(a_hi[:, k, :], zs[:, k, :], ACT.Copy), ahi_ready)

            def evac(layer, i, dst):
                act.wait_ge(proj_done, layer * NCH + i + 1)
                m = dst.shape[0]
                step(fn(dst, ring_bank(layer, i)[0:m, 0:TT], ACT.Copy), chunk_evac)
                split_weights(layer * (NCH + KT) + i + 2)

            def sines(s, c):
                step(fn(s[:, :, :], s[:, :, :], ACT.Sin, scale=TWO_PI))
                step(fn(c[:, :, :], c[:, :, :], ACT.Sin, scale=TWO_PI), sin_ready)

            def lower_bounds():
                act.wait_ge(lb_ready, 1)
                step(fn(lbt[:, :, 1], lbt[:, :, 0], ACT.Abs))
                settle()
                step(fn(lbt[:, :, 1], lbt[:, :, 1], ACT.Exp, scale=-1.0))
                settle()
                step(fn(lbt[:, :, 1], lbt[:, :, 1], ACT.Ln, bias=1.0), lb_act)

            def gate_logs(layer):
                act.wait_ge(lrup_done, layer + 1)
                if layer:
                    act.wait_ge(b_ready, layer)
                step(fn(x3[:, 2, :], wk[:, 1, 0:TT], ACT.Identity, bias=par(Q_GLAB + layer)))
                settle()
                step(fn(tl, x3, ACT.Abs))
                settle()
                step(fn(tl, tl, ACT.Exp, scale=-1.0))
                settle()
                step(fn(tl, tl, ACT.Ln, bias=1.0), l_ready)

            def keys(layer):
                act.wait_ge(t_ready, layer + 1)
                for t in range(2):
                    step(fn(k3[:, t, :], k3[:, t, :], ACT.Exp, scale=-1.0, bias=lbc[:, layer, t, 1:2]),
                         k3_ready if t == 1 else None)
                if layer:
                    act.wait_ge(ls_ready, layer + 1)
                    for t in range(2):
                        step(fn(eb[:, t, :], x3[:, t, :], ACT.Abs, bias=lbc[:, layer, t, 2:3]))
                    settle()
                    step(fn(eb[:, 0:2, :], eb[:, 0:2, :], ACT.Exp, scale=-1.0))
                    settle()
                    step(fn(eb[:, 0:2, :], eb[:, 0:2, :], ACT.Ln, bias=1.0), lb2_act)

            def decays(layer):
                act.wait_ge(b_ready, layer + 1)
                step(fn(eb[:, :, :], tl, ACT.Exp), eb_ready)
                act.wait_ge(de_ready, layer + 1)
                step(fn(ke[:, :, 0:TP], ke[:, :, 0:TP], ACT.Exp), eb_ready)

            def level_exp(layer, n):
                act.wait_ge(ld_ready, layer * NL + n + 1)
                step(fn(dl[n % 2], dl[n % 2], ACT.Exp), lexp_ready)

            def turned(layer, r, dst):
                act.wait_ge(tr_done, layer * 6 + r + 1)
                n = dst.free_size()
                step(fn(dst, wk[:, 4, 0:n] if len(dst.shape) == 2 else
                        wk[:, 4, 0:n].rearrange("p (a b) -> p a b", a=dst.shape[1]) if len(dst.shape) == 3 else
                        wk[:, 4, 0:n].rearrange("p (a b c) -> p a b c", a=dst.shape[1], b=dst.shape[2]), ACT.Copy), tr_evac)

            def s5_turned(layer, rounds):
                for r in rounds:
                    act.wait_ge(gtr_done, layer * 4 + r + 1)
                    step(fn(gtr[:, r // 2, 4 * (r % 2):4 * (r % 2) + 4, :].rearrange("p s m -> p (s m)"),
                            wk[:, r, :], ACT.Copy), gtr_evac)

            def silu(layer, i):
                act.wait_ge(proj_done, layer * NCH + i + 1)
                step(fn(zs[:, i - NP, :], ring_bank(layer, i)[:, 0:TT], ACT.Silu), chunk_evac)
                split_weights(layer * (NCH + KT) + i + 2)

            def s5_evac(layer, n):
                act.wait_ge(y_done, layer * 2 + n + 1)
                step(fn(yb[:, NY // 2 * n:NY // 2 * n + NY // 2], wk[:, 4, 0:NY // 2], ACT.Copy), y_evac)

            use_logs()
            act.wait_ge(par_in, 16)
            for layer in range(DEPTH):
                if layer == 0:
                    split_weights(0)
                norm(layer)
                split_operand(2 * layer)
                if layer == 0:
                    split_weights(1)
                if layer == 0:
                    lower_bounds()
                    use_silu()
                    act.wait_ge(ph_ready, 1)
                    sines(sinp, cosp)
                    use_logs()
                evac(layer, C_F0, x3[:, 0, :])
                evac(layer, C_F1, x3[:, 1, :])
                evac(layer, C_LR, lr_t[0:16, :])
                evac(layer, C_Q0, qv[:, 0, :])
                evac(layer, C_Q1, qv[:, 1, :])
                gate_logs(layer)
                evac(layer, C_GQ, qraw[:, :])
                evac(layer, C_GK, k3[:, 2, :])
                keys(layer)
                decays(layer)
                level_exp(layer, 0)
                evac(layer, C_I0, v[:, 0, :])
                level_exp(layer, 1)
                evac(layer, C_I1, v[:, 1, :])
                level_exp(layer, 2)
                evac(layer, C_GV0, v[:, 2, :])
                turned(layer, 0, ket[:, 0, :, :])
                level_exp(layer, 3)
                evac(layer, C_GV1, v[:, 3, :])
                turned(layer, 1, ket[:, 1, :, :])
                evac(layer, C_RQ, r2[:, 0, :])
                turned(layer, 2, vt[:, :, 0:2, :])
                level_exp(layer, 4)
                evac(layer, C_RK, r2[:, 1, :])
                turned(layer, 3, vt[:, :, 2:4, :])
                evac(layer, C_RV0, v[:, 4, :])
                evac(layer, C_RV1, v[:, 5, :])
                evac(layer, C_U0, u[:, 0, :])
                use_silu()
                turned(layer, 4, vt[:, :, 4:6, :])
                evac(layer, C_U1, u[:, 1, :])
                turned(layer, 5, krt[:, :, :])
                for i in range(NP, NCH):
                    silu(layer, i)
                    if i == NP + 1:
                        act.wait_ge(angles_ready, layer + 1)
                        sines(sinc, cosc)
                        s5_turned(layer, range(4))
                    if i == NP + 6:
                        s5_evac(layer, 0)
                    if i == NP + 7:
                        s5_evac(layer, 1)
                act.wait_ge(tin_ready, layer + 1)
                step(fn(yt2, yt2, ACT.Tanh, scale=GELU_C), tanh_ready)
                act.wait_ge(glu_done, layer + 1)
                step(fn(glu[:, :, :], wk[:, 2:4, 0:TT], ACT.Tanh, scale=0.5), glu_tanh)
                use_logs()
                act.wait_ge(o_ready, layer * 4 + 4)
                step(fn(osq[:, 0:4, :], o[:, 0:4, :], ACT.Square), osq_ready)
                act.wait_ge(mean_used, layer * 2 + 2)
                step(fn(osq[:, 4:6, :], o[:, 4:6, :], ACT.Square), osq_ready)
                for t in range(6):
                    act.wait_ge(var_done, layer * 6 + t + 1)
                    step(fn(rs[:, t, :], ring_bank(layer, NCH + 2 + t)[:, 0:TT], ACT.Ln, bias=EPS), ors_ready)
                settle()
                step(fn(rs[:, :, :], rs[:, :, :], ACT.Exp, scale=-0.5), ors_ready)
                split_operand(2 * layer + 1)
            norm(DEPTH)

        @block.vector
        def _(dve):
            step, settle = chain(dve, dve_step)
            tt, ts, stt, cp = (nc.vector.tensor_tensor, nc.vector.tensor_scalar,
                               nc.vector.scalar_tensor_tensor, nc.vector.tensor_copy)

            def scale_x(n, weights, signal):
                dve.wait_ge(rstd_ready, n + 1)
                for k in range(KT):
                    step(stt(out=h[:, k, :], in0=x[:, k, :], scalar=par(weights + k), in1=rstd,
                             op0=ALU.mult, op1=ALU.mult), signal)
                if n < DEPTH:
                    lower_parts(2 * n)

            def lower_parts(n):
                for k in A_LO_DVE:
                    dve.wait_ge(ahi_ready, n * KT + k + 1)
                    step(tt(a_lo[:, k, :], zs[:, k, :], a_hi[:, k, :].bitcast(F32), ALU.subtract), alo_dve)

            def lower_bounds():
                step(tt(lbt[:, :, 0], par(Q_LOGIT + 2, 2), par(Q_LOGIT, 2), ALU.subtract), lb_ready)
                step(nc.vector.memset(lbc[:, 0, :, :], 0.0))
                dve.wait_ge(lb_act, 1)
                step(ts(lbt[:, :, 2], lbt[:, :, 0], 0.0, None, ALU.min))
                step(ts(lbt[:, :, 3], lbt[:, :, 0], 0.0, None, ALU.max))
                settle()
                step(tt(lbc[:, 1, :, 0], lbt[:, :, 2], lbt[:, :, 1], ALU.subtract))
                step(stt(out=lbc[:, 1, :, 1], in0=lbt[:, :, 3], scalar=-1.0, in1=lbt[:, :, 1], op0=ALU.mult, op1=ALU.subtract))
                settle()
                step(tt(lbc[:, 1, :, 2], lbc[:, 1, :, 1], lbc[:, 1, :, 0], ALU.subtract))
                settle()

            def accurate_exp(dst, src, tmp):
                r, k, q = tmp
                step(ts(r, src, -87.0, 88.0, ALU.max, ALU.min))
                settle()
                step(ts(k, r, 1.4426950408889634, MAGIC, ALU.mult, ALU.add))
                settle()
                step(ts(k, k, MAGIC, None, ALU.subtract))
                settle()
                for part in (LN2_HI, LN2_LO):
                    step(stt(out=r, in0=k, scalar=-part, in1=r, op0=ALU.mult, op1=ALU.add))
                    settle()
                step(ts(q, r, 1.0 / 5040, None, ALU.mult))
                for n in (720, 120, 24, 6, 2, 1):
                    settle()
                    step(stt(out=q, in0=q, scalar=1.0 / n, in1=r, op0=ALU.add, op1=ALU.mult))
                step(ts(k.bitcast(I32), k, 127.0, None, ALU.add))
                settle()
                step(ts(k.bitcast(I32), k.bitcast(I32), 23, None, ALU.logical_shift_left))
                settle()
                step(stt(out=dst, in0=q, scalar=1.0, in1=k, op0=ALU.add, op1=ALU.mult))
                settle()

            def s5_phases():
                lr, li = par(Q_LR, LS), par(Q_LI, LS)
                accurate_exp(sw[:, 0, :], par(Q_LS, LS), [sw[:, n, :] for n in (1, 2, 3)])
                step(tt(sw[:, 1, :], lr, sw[:, 0, :], ALU.mult))
                step(tt(sw[:, 2, :], li, sw[:, 0, :], ALU.mult))
                settle()
                step(tt(mag[:, :, :], sw[:, 1, :].unsqueeze(2).to_broadcast([P, LS, NPW]),
                        c("mult")[:, 0:NPW].unsqueeze(1).to_broadcast([P, LS, NPW]), ALU.mult))
                settle()
                flat = mag[:, :, :].rearrange("p s m -> p (s m)")
                accurate_exp(flat, flat, [z[:, :, :].rearrange("p s m -> p (s m)") for z in (are, aim, mtmp)])
                step(ts(sw[:, 2, :], sw[:, 2, :], 1.0 / (2 * np.pi), None, ALU.mult))
                settle()
                step(ts(sw[:, 3, :], sw[:, 2, :], MAGIC, MAGIC, ALU.add, ALU.subtract))
                settle()
                step(tt(sw[:, 2, :], sw[:, 2, :], sw[:, 3, :], ALU.subtract))
                settle()
                step(ts(sw[:, 3, :], sw[:, 2, :], float(SL), None, ALU.mult))
                settle()
                step(ts(sw[:, 4, :], sw[:, 3, :], MAGIC, MAGIC, ALU.add, ALU.subtract))
                settle()
                step(tt(turn4[:, :], sw[:, 3, :], sw[:, 4, :], ALU.subtract))
                settle()
                s5_turns(sw[:, 2, :], c("mult")[:, 0:NPW], sinp, cosp, ph_ready)

            def s5_turns(turn, mult, dst_sin, dst_cos, signal):
                n, m = turn.free_size(), mult.free_size()
                t, r = (z[:, 0:n * m].rearrange("p (s m) -> p s m", s=n) for z in (turns, turnr))
                step(tt(t, turn.unsqueeze(2).to_broadcast([P, n, m]), mult.unsqueeze(1).to_broadcast([P, n, m]), ALU.mult))
                settle()
                step(ts(r, t, MAGIC, MAGIC, ALU.add, ALU.subtract))
                settle()
                step(tt(dst_sin[:, :, :], t, r, ALU.subtract))
                step(ts(t, t, 0.25, None, ALU.add))
                settle()
                step(ts(r, t, MAGIC, MAGIC, ALU.add, ALU.subtract))
                settle()
                step(tt(dst_cos[:, :, :], t, r, ALU.subtract), signal)

            def s5_chunk_angles(layer):
                if layer:
                    settle()
                s5_turns(turn4[:, S5T * layer:S5T * layer + S5T], c("mult")[:, NPW:], sinc, cosc, angles_ready)

            def s5_coefficients():
                lr, li = par(Q_LR, LS), par(Q_LI, LS)
                dve.wait_ge(sin_ready, 1)
                step(tt(are[:, :, :], mag[:, :, :], cosp[:, :, :], ALU.mult))
                step(tt(aim[:, :, :], mag[:, :, :], sinp[:, :, :], ALU.mult))
                step(tt(sw[:, 3, :], lr, lr, ALU.mult))
                step(tt(sw[:, 4, :], li, li, ALU.mult))
                settle()
                step(tt(sw[:, 3, :], sw[:, 3, :], sw[:, 4, :], ALU.add))
                step(ts(sw[:, 5, :], are[:, :, 1], -1.0, None, ALU.add))
                settle()
                step(nc.vector.reciprocal(sw[:, 4, :], sw[:, 3, :]))
                step(tt(sw[:, 6, :], sw[:, 5, :], lr, ALU.mult))
                step(tt(sw[:, 7, :], aim[:, :, 1], li, ALU.mult))
                step(tt(sw[:, 8, :], aim[:, :, 1], lr, ALU.mult))
                step(tt(sw[:, 9, :], sw[:, 5, :], li, ALU.mult))
                settle()
                step(tt(sw[:, 6, :], sw[:, 6, :], sw[:, 7, :], ALU.add))
                step(tt(sw[:, 8, :], sw[:, 8, :], sw[:, 9, :], ALU.subtract))
                settle()
                step(tt(sw[:, 10, :], sw[:, 6, :], sw[:, 4, :], ALU.mult))
                step(tt(sw[:, 11, :], sw[:, 8, :], sw[:, 4, :], ALU.mult))
                settle()
                fr = sw[:, 10, :].unsqueeze(2).to_broadcast([P, LS, SL])
                fi = sw[:, 11, :].unsqueeze(2).to_broadcast([P, LS, SL])
                step(tt(gre[:, :, :], are[:, :, 0:SL], fr, ALU.mult))
                step(tt(gt1[:, :, :], aim[:, :, 0:SL], fi, ALU.mult))
                step(tt(gim[:, :, :], are[:, :, 0:SL], fi, ALU.mult))
                step(tt(gt2[:, :, :], aim[:, :, 0:SL], fr, ALU.mult))
                settle()
                step(tt(gre[:, :, :], gre[:, :, :], gt1[:, :, :], ALU.subtract))
                step(tt(gim[:, :, :], gim[:, :, :], gt2[:, :, :], ALU.add), tab_ready)

            def s5_b(layer):
                L = slice(S5T * layer, S5T * layer + S5T)
                dve.wait_ge(s5m_in[layer], 16)
                dve.wait_ge(lvl_done, layer * NL + NL)
                settle()
                g_r, g_i = (z[:, L, :].unsqueeze(3).to_broadcast([P, S5T, SL, 32]) for z in (gre, gim))
                b_r, b_i = (s5m_t[:, n, :, :].unsqueeze(2).to_broadcast([P, S5T, SL, 32]) for n in range(2))
                step(tt(bb_re, g_r, b_r, ALU.mult))
                step(tt(bb_t, g_i, b_i, ALU.mult))
                step(tt(bb_im, g_r, b_i, ALU.mult))
                settle()
                step(tt(bb_re, bb_re, bb_t, ALU.subtract))
                settle()
                step(tt(bb_t, g_i, b_r, ALU.mult))
                settle()
                step(tt(bb_im, bb_im, bb_t, ALU.add), bb_ready)

            def s5_within(layer):
                if layer:
                    dve.wait_ge(y_done, layer * 2)
                step(cp(m4[:, :, :], mag[:, S5T * layer:S5T * layer + S5T, SL:SL + 1].to_broadcast([P, S5T, SC])))
                settle()
                step(nc.vector.memset(m4[:, :, 0:1], 0.0))
                dve.wait_ge(kt_done, layer + 1)
                for q in range(4):
                    for half in range(2):
                        src = wk[0:32, 2 + half, :].rearrange("p (s m) -> p s m", s=4)[:, :, 0:32 * (q + 1)]
                        step(cp(qrt(tmat, q)[:, 4 * half:4 * half + 4, 32 * (3 - q):P], src))
                settle()
                for s in range(S5T):
                    step(stt(out=tmat[:, s, :], in0=c("rev"), scalar=par(Q_S5D + layer * S5T + s), in1=tmat[:, s, :],
                             op0=ALU.mult, op1=ALU.add), tmat_ready if s == S5T - 1 else None)

            def s5_relay(layer):
                dve.wait_ge(chunk_evac, layer * NCH + C_U1 + 1)
                if layer:
                    dve.wait_ge(y_done, layer * 2)
                for a in range(4):
                    src = qrt(u, a)[:, :, 0:TP].rearrange("p t (k j) -> p t k j", j=SL)
                    for q in range(4):
                        dst = qrt(ub, q)[:, :, NS:].rearrange("p (t s) k -> p t s k", t=2)[:, :, a, :]
                        step(cp(dst, src[:, :, :, 3 - q]))
                    for n, dst in enumerate((qrt(ub, 3)[:, :, 0:NS], qrt(us0, 0)[:, :, :])):
                        step(cp(dst.rearrange("p (t s) k -> p t s k", t=2)[:, :, a, :], qrt(u, a)[:, :, TP:TT]),
                             u_ready if a == 3 and n == 1 else None)

            def s5_scan(layer):
                co, sn = cosc[:, :, :], sinc[:, :, :]
                vr, vi = (wk[:, n, :].rearrange("p (s k) -> p s k", s=S5T) for n in range(2))
                t = [z.rearrange("p (s k) -> p s k", s=S5T) for z in sv]
                dve.wait_ge(s5v_done, layer + 1)
                dve.wait_ge(sin_ready, layer + 2)
                if layer:
                    dve.wait_ge(stored, layer)
                step(tt(t[0], vr, co, ALU.mult))
                step(tt(t[1], vi, sn, ALU.mult))
                step(tt(t[2], vi, co, ALU.mult))
                step(tt(t[3], vr, sn, ALU.mult), s5v_used)
                settle()
                step(tt(t[0], t[0], t[1], ALU.add))
                step(tt(t[2], t[2], t[3], ALU.subtract))
                settle()
                m = m4[:, :, :].rearrange("p s k -> p (s k)")
                step(nc.vector.tensor_tensor_scan(sv[1], m, sv[0], 0.0, ALU.mult, ALU.add))
                step(nc.vector.tensor_tensor_scan(sv[3], m, sv[2], 0.0, ALU.mult, ALU.add))
                settle()
                step(tt(t[0], t[1], co, ALU.mult))
                step(tt(t[2], t[3], sn, ALU.mult))
                settle()
                step(tt(sr[:, :, NS + 1:], t[0], t[2], ALU.subtract))
                settle()
                step(tt(t[0], t[1], sn, ALU.mult))
                step(tt(t[2], t[3], co, ALU.mult))
                dve.wait_ge(s5s_part, layer + 1)
                for n in range(2):
                    step(tt(s5n[:, n, :, :], s5t[:, 2 * n, :, :],
                            wk[:, 4, 64 * n:64 * n + 64].rearrange("p (s b) -> p s b", s=S5T), ALU.add),
                         s5s_used if n else None)
                settle()
                step(tt(si[:, :, NS + 1:], t[0], t[2], ALU.add), s_ready)
                settle()
                for n, s in enumerate((sr, si)):
                    step(cp(s5f[:, n, :], s[:, :, NS + SC]), s5f_ready if n else None)

            def gate(layer):
                dve.wait_ge(l_ready, layer + 1)
                step(stt(out=k3[:, 0:2, :], in0=x3[:, 0:2, :], scalar=0.0, in1=tl[:, 0:2, :], op0=ALU.max, op1=ALU.add), t_ready)
                settle()
                step(stt(out=x3, in0=x3, scalar=0.0, in1=tl, op0=ALU.min, op1=ALU.subtract), ls_ready)
                settle()
                step(ts(x3[:, 2, :], x3[:, 2, :], 1.0 / 16.0, None, ALU.mult))
                if layer:
                    for t in range(2):
                        step(ts(tl[:, t, :], x3[:, t, :], lbc[:, layer, t, 1:2], lbc[:, layer, t, 0:1], ALU.add, ALU.max))
                    dve.wait_ge(lb2_act, layer)
                    settle()
                    step(tt(x3[:, 0:2, :], tl[:, 0:2, :], eb[:, 0:2, :], ALU.add))
                settle()
                step(nc.vector.tensor_tensor_scan(tl.rearrange("p a t -> p (a t)"), c("reset"),
                                                  x3.rearrange("p a t -> p (a t)"), 0.0, ALU.mult, ALU.add), b_ready)
                settle()
                bb = tl[:, :, 0:TP].rearrange("p a (b t) -> p a b t", t=BL)
                step(tt(ke[:, :, 0:TP].rearrange("p a (b t) -> p a b t", t=BL),
                        bb[:, :, :, BL - 1:BL].to_broadcast([P, 3, NB, BL]), bb, ALU.subtract), de_ready)

            def halves(ap, n):
                return ap.rearrange("p g (n w h) -> p g n w h", w=2, h=1 << n)

            def level_diff(layer, n):
                b = halves(tl[:, :, 0:TP], n)
                d = halves(dl[n % 2], n)
                hh = 1 << n
                mid = b[:, :, :, 0, hh - 1:hh].to_broadcast([P, 3, TP // (2 * hh), hh])
                step(tt(d[:, :, :, 1, :], b[:, :, :, 1, :], mid, ALU.subtract))
                step(tt(d[:, :, :, 0, :], mid, b[:, :, :, 0, :], ALU.subtract), ld_ready)

            def level_operands(layer, n):
                dve.wait_ge(lexp_ready, layer * NL + n + 1)
                if n >= 2:
                    dve.wait_ge(lvl_done, layer * NL + n - 1)
                d, kk = halves(dl[n % 2], n), halves(k3[:, :, 0:TP], n)
                qq = halves(qv[:, :, 0:TP], n)
                dst = ql[n % 2].rearrange("p g (n h) -> p g n h", h=1 << n)
                step(tt(halves(kl[n % 2], n)[:, :, :, 0, :], kk[:, :, :, 0, :], d[:, :, :, 0, :], ALU.mult))
                step(tt(dst[:, 0:2], qq[:, 0:2, :, 1, :], d[:, 0:2, :, 1, :], ALU.mult))
                step(tt(dst[:, 2:4], qq[:, 2:4, :, 1, :],
                        d[:, 2:3, :, 1, :].to_broadcast([P, 2, TP >> (n + 1), 1 << n]), ALU.mult), ql_ready)

            def level_scores(layer, n):
                dve.wait_ge(lvl_done, layer * NL + n + 1)
                settle()
                for g in range(2):
                    out = att[:, g].rearrange("p i b t -> p (i b) t")
                    out = halves(out, n)[:, :, :, 1, :]
                    data = wk[:, 2 * (n % 2) + g, :].rearrange("p (g n h) -> p g n h", g=8, h=1 << n)
                    mk = masks[:, n, :].rearrange("p (n h) -> p n h", h=1 << n).unsqueeze(1).to_broadcast([P, 8, 64 >> n, 1 << n])
                    step(nc.vector.copy_predicated(out, mk, data), lvl_used if g else None)

            def decayed_q(layer):
                dve.wait_ge(eb_ready, layer * 2 + 1)
                if layer:
                    dve.wait_ge(ors_ready, layer * 7)
                for hh in range(2):
                    step(stt(out=qm[:, hh:4:2, :], in0=eb[:, 0:2, 0:TP], scalar=c("m64")[:, hh:hh + 1], in1=qv[:, 0:2, 0:TP],
                             op0=ALU.mult, op1=ALU.mult))
                for hd in range(4):
                    step(stt(out=qm[:, 4 + hd, :], in0=eb[:, 2, 0:TP], scalar=c("m32")[:, hd:hd + 1], in1=qv[:, 2 + hd % 2, 0:TP],
                             op0=ALU.mult, op1=ALU.mult), qm_ready if hd == 3 else None)

            def diagonal_scores(layer):
                dve.wait_ge(diag_done, layer + 1)
                if layer:
                    dve.wait_ge(o_done, layer * 3)
                for blk in range(2):
                    for g in range(2):
                        step(tt(att[:, g, :, blk, :], wk[:, 2 * blk + g, :].rearrange("p (i t) -> p i t", i=4),
                                c("ident").unsqueeze(1).to_broadcast([P, 4, P]), ALU.mult), att_ready)
                settle()

            def carry(layer):
                dve.wait_ge(kv_done, layer + 1)
                if layer:
                    dve.wait_ge(stored, layer)
                dve.wait_ge(tr_evac, layer * 6 + 4)
                dec = eb[:, :, 0:TP].rearrange("p a (b t) -> p a b t", t=BL)
                for b in range(NB):
                    kv = wk[:, b % 4, 192 * (b // 4):192 * (b // 4) + 192].rearrange("p (a c) -> p a c", a=3)
                    if b:
                        settle()
                        for t in range(3):
                            step(stt(out=s3[:, t, b + 1, :], in0=s3[:, t, b, :], scalar=dec[:, t, b, BL - 1:BL],
                                     in1=kv[:, t, :], op0=ALU.mult, op1=ALU.add), s3_ready if b == NB - 1 and t == 2 else None)
                    else:
                        step(cp(s3[:, :, 1, :], kv))

            def rotary(layer):
                dve.wait_ge(rot_done, layer + 1)
                step(tt(rt1, r2[:, :, :], c("cos").unsqueeze(1).to_broadcast([P, 2, TT]), ALU.mult))
                step(tt(rt2, wk[:, 2:4, 0:TT], c("sin").unsqueeze(1).to_broadcast([P, 2, TT]), ALU.mult), r2_used)
                settle()
                step(tt(r2[:, :, :], rt1, rt2, ALU.add))
                settle()
                for n in range(2):
                    step(ts(rqm[:, n, :], r2[:, 0, :], c("m2")[:, n:n + 1], None, ALU.mult))
                dve.wait_ge(ca_ready, layer + 1)
                step(tt(kd, r2[:, 1, 0:TP], c("kdec"), ALU.mult), rqm_ready)

            def ret_decay(layer):
                dve.wait_ge(rsc_done, layer + 1)
                dec = c("decay").rearrange("p (a t) -> p a t", a=4)
                step(tt(attr[:, :, 0:TP], wk[:, 0:4, 0:TP], dec, ALU.mult))
                step(tt(attr[:, :, TP:384], wk[:, 0:4, TP:384], dec[:, :, 0:P], ALU.mult), attr_ready)

            def sample_states(layer):
                dve.wait_ge(q4_ready, layer + 1)
                for n in range(3):
                    dve.wait_ge(vb_done, layer * 3 + n + 1)
                    if n == 0:
                        a, m = 0, 2
                    else:
                        a, m = 1 + n, 1
                    for t in range(a, a + m):
                        step(tt(kvb[:, 512 * t:512 * t + 512].rearrange("p (b c) -> p b c", b=NS),
                                wk[:, t, :].rearrange("p (b c) -> p b c", b=NS),
                                k4[:, t, :].unsqueeze(2).to_broadcast([P, NS, 64]), ALU.mult),
                             vb_used if n == 2 else None)
                settle()
                dve.wait_ge(fs_ready, layer + 1)
                fl = ss[:, :, :, :].rearrange("p a b c -> p (a b c)")
                step(tt(fl, fl, kvb, ALU.add), ss_ready)

            def gather_outputs(layer):
                dve.wait_ge(vd_ready, layer * 3 + 3)
                for kind in range(3):
                    dve.wait_ge(o_done, layer * 3 + kind + 1)
                    step(cp(o[:, 2 * kind:2 * kind + 2, 0:TP], wk[:, kind, :].rearrange("p (t n) -> p t n", t=2)), o_ready)
                dve.wait_ge(rst_done, layer + 1)
                if layer:
                    dve.wait_ge(stored, layer)
                for hd in range(4):
                    step(cp(qrt(retf, hd), qrt(wk, hd)[:, 3, 64 * hd:64 * hd + 64]), st_ready if hd == 3 else None)
                dve.wait_ge(so_done, layer + 1)
                for hh in range(2):
                    rows = slice(64 * hh, 64 * hh + 64)
                    step(cp(o[rows, 0:2, TP:TT], wk[0:64, 4, 0:32].rearrange("p (t b h) -> p t b h", t=2, h=2)[:, :, :, hh]))
                    for n in range(2):
                        src = wk[0:64, 4, 32 + 32 * n:64 + 32 * n].rearrange("p (b t h) -> p t b h", t=2, h=2)[:, :, :, hh]
                        step(cp(o[rows, 2 + 2 * n:4 + 2 * n, TP:TT], src), o_ready if hh and n else None)

            def s5_gelu(layer):
                dve.wait_ge(y_evac, layer * 2 + 2)
                step(tt(yt2, yb, yb, ALU.mult))
                settle()
                step(ts(yt2, yt2, GELU_A, 1.0, ALU.mult, ALU.add))
                settle()
                step(tt(yt2, yt2, yb, ALU.mult), tin_ready)

            def s5_back(layer):
                dve.wait_ge(tanh_ready, layer + 1)
                step(stt(out=yb, in0=yt2, scalar=1.0, in1=yb, op0=ALU.add, op1=ALU.mult))
                settle()
                yv = yb.rearrange("p (t s k) -> p t s k", t=2, s=4)
                for a in range(4):
                    for j in range(4):
                        dst = qrt(yg, a)[:, :, 0:TP].rearrange("p t (k j) -> p t k j", j=SL)[:, :, :, j]
                        step(ts(dst, qrt(yv, j)[:, :, a, NS:], 0.5, None, ALU.mult))
                    step(ts(qrt(yg, a)[:, :, TP:TT], qrt(yv, 0)[:, :, a, 0:NS], 0.5, None, ALU.mult),
                         yg_ready if a == 3 else None)

            def s5_mix(layer):
                dve.wait_ge(glu_tanh, layer + 1)
                step(stt(out=glu[:, :, :], in0=glu[:, :, :], scalar=1.0, in1=yg[:, :, :], op0=ALU.add, op1=ALU.mult))
                settle()
                for t in range(2):
                    step(stt(out=zs[:, t, :], in0=glu[:, t, :], scalar=0.5, in1=zs[:, t, :], op0=ALU.mult, op1=ALU.mult), mix_ready)

            def center(layer):
                for t in range(2):
                    dve.wait_ge(mean_done, layer * 2 + t + 1)
                    step(tt(o[:, 4 + t, :], o[:, 4 + t, :], ring_bank(layer, NCH + t)[:, 0:TT], ALU.subtract), mean_used)

            def head_mix(layer):
                dve.wait_ge(ors_ready, layer * 7 + 7)
                for t in range(6):
                    step(stt(out=o[:, t, :], in0=o[:, t, :], scalar=par(Q_HEADG + layer * 6 + t), in1=rs[:, t, :],
                             op0=ALU.mult, op1=ALU.mult))
                settle()
                for t in range(6):
                    step(tt(zs[:, 2 + t, :], zs[:, 2 + t, :], o[:, t, :], ALU.mult), mix_ready)
                lower_parts(2 * layer + 1)

            def residual(layer, m):
                dve.wait_ge(out_done, layer * KT + m + 1)
                step(tt(x[:, m, :], x[:, m, :], ring_bank(layer, NCH + 8 + m)[:, 0:TT], ALU.add), out_used)

            step(nc.vector.memset(ones_d[:, :], 1.0 / D), zero_ready)
            step(nc.vector.memset(lev[:, :], 0.0))
            step(nc.vector.memset(ub[:, :, :], 0.0))
            step(nc.vector.memset(us0[:, :, :], 0.0))
            step(nc.vector.memset(tmat[:, :, :], 0.0))
            step(nc.vector.memset(sr[:, :, NS:NS + 1], 0.0))
            step(nc.vector.memset(si[:, :, NS:NS + 1], 0.0))
            settle()
            dve.wait_ge(par_in, 16)
            dve.wait_ge(cst_in[0], 16)
            s5_phases()
            for layer in range(DEPTH):
                scale_x(layer, Q_NORM + layer * KT, h_ready)
                if layer == 0:
                    lower_bounds()
                    dve.wait_ge(cst_in[1], 16)
                gate(layer)
                level_diff(layer, 0)
                if layer == 0:
                    s5_coefficients()
                dve.wait_ge(chunk_evac, layer * NCH + C_GQ + 1)
                for n in range(2):
                    step(ts(qv[:, 2 + n, :], qraw[:, :], c("m2")[:, n:n + 1], 32 ** -0.5, ALU.mult, ALU.mult),
                         qv_ready if n else None)
                level_diff(layer, 1)
                settle()
                level_operands(layer, 0)
                dve.wait_ge(eb_ready, layer * 2 + 2)
                step(tt(ke[:, :, 0:TP], ke[:, :, 0:TP], k3[:, :, 0:TP], ALU.mult), ke_ready)
                level_operands(layer, 1)
                settle()
                level_diff(layer, 2)
                level_diff(layer, 3)
                if layer == 0:
                    dve.wait_ge(small_in, 48)
                    dve.wait_ge(cst_in[2], 16)
                diagonal_scores(layer)
                for n in range(NL):
                    level_scores(layer, n)
                    if n + 2 < NL:
                        level_operands(layer, n + 2)
                        settle()
                    if n == 0:
                        level_diff(layer, 4)
                rotary(layer)
                s5_b(layer)
                carry(layer)
                s5_chunk_angles(layer)
                s5_relay(layer)
                ret_decay(layer)
                s5_within(layer)
                s5_scan(layer)
                decayed_q(layer)
                sample_states(layer)
                s5_gelu(layer)
                s5_back(layer)
                gather_outputs(layer)
                center(layer)
                s5_mix(layer)
                head_mix(layer)
                for m in range(KT):
                    residual(layer, m)
            scale_x(DEPTH, Q_FINAL, fin_ready)

        @block.gpsimd
        def _(pool):
            step, settle = chain(pool, pool_step)
            tt, cp = nc.gpsimd.tensor_tensor, nc.gpsimd.tensor_copy

            def s5_c(layer, part):
                if part == 0:
                    pool.wait_ge(s5m_in[layer], 16)
                    if layer:
                        pool.wait_ge(y_done, layer * 2)
                        pool.wait_ge(rst_done, layer)
                    else:
                        pool.wait_ge(tab_ready, 1)
                H = slice(2 * part, 2 * part + 2)
                LH = slice(S5T * layer + 2 * part, S5T * layer + 2 * part + 2)
                a_r, a_i = (z[:, LH, :].unsqueeze(3).to_broadcast([P, 2, NPW, 32]) for z in (are, aim))
                c_r, c_i = (s5m_t[:, 2 + n, H, :].unsqueeze(2).to_broadcast([P, 2, NPW, 32]) for n in range(2))
                step(tt(ca_re[:, H], a_r, c_r, ALU.mult))
                step(tt(ca_im[:, H], a_r, c_i, ALU.mult))
                step(tt(ptmp, a_i, c_i, ALU.mult))
                settle()
                step(tt(ca_re[:, H], ca_re[:, H], ptmp, ALU.subtract))
                settle()
                step(tt(ptmp, a_i, c_r, ALU.mult))
                settle()
                step(tt(ca_im[:, H], ca_im[:, H], ptmp, ALU.add))
                settle()
                step(nc.gpsimd.tensor_scalar(ca_im[:, H], ca_im[:, H], -1.0, None, ALU.mult), ca_ready if part == 3 else None)

            def s5_samples(layer):
                L = slice(S5T * layer, S5T * layer + S5T)
                a_r = are[:, L, 1:2].to_broadcast([P, S5T, NS])
                a_i = aim[:, L, 1:2].to_broadcast([P, S5T, NS])
                s_r, s_i = s5i[:, layer, 0, :, :], s5i[:, layer, 1, :, :]
                if layer == 0:
                    pool.wait_ge(small_in, 48)
                step(tt(s5t[:, 0, :, :], s_r, a_r, ALU.mult))
                step(tt(s5t[:, 1, :, :], s_i, a_i, ALU.mult))
                step(tt(s5t[:, 2, :, :], s_r, a_i, ALU.mult))
                step(tt(s5t[:, 3, :, :], s_i, a_r, ALU.mult))
                step(cp(sr[:, :, 0:NS], s_r))
                step(cp(si[:, :, 0:NS], s_i))
                settle()
                step(tt(s5t[:, 0, :, :], s5t[:, 0, :, :], s5t[:, 1, :, :], ALU.subtract))
                step(tt(s5t[:, 2, :, :], s5t[:, 2, :, :], s5t[:, 3, :, :], ALU.add), s5s_part)

            def split_weights(last):
                for j in range(split[0], 2 * min(last + 1, DEPTH * (NCH + KT))):
                    pool.wait_ge(whi_ready, j + 1)
                    half_used(pool, j - WSLOTS)
                    step(tt(w_lo[:, j % WSLOTS, :, :], wring[:, j % RING, :, :],
                            w_hi[:, j % WSLOTS, :, :].bitcast(F32), ALU.subtract), wlo_ready)
                    split[0] = j + 1

            def lower_parts(n):
                for k in A_LO_POOL:
                    pool.wait_ge(ahi_ready, n * KT + k + 1)
                    step(tt(a_lo[:, k, :], zs[:, k, :], a_hi[:, k, :].bitcast(F32), ALU.subtract), alo_pool)

            def sample_v(layer, n):
                pool.wait_ge(chunk_evac, layer * NCH + (C_I1, C_GV1, C_RV1)[n] + 1)
                if n == 0:
                    pool.wait_ge(lvl_done, layer * NL + NL)
                    pool.wait_ge(bb_ready, layer + 1)
                else:
                    pool.wait_ge(vb_done, layer * 3 + n)
                for t in range(2):
                    step(tt(vd[:, t, :].rearrange("p (b c) -> p b c", b=NS),
                            v[:, 2 * n + t, TP:TT].unsqueeze(2).to_broadcast([P, NS, 64]),
                            c("eye64").unsqueeze(1).to_broadcast([P, NS, 64]), ALU.mult), vd_ready if t else None)

            def sample_gates(layer):
                pool.wait_ge(eb_ready, layer * 2 + 1)
                pool.wait_ge(rqm_ready, layer + 1)
                pool.wait_ge(ss_in[layer], 48)
                step(cp(f4[:, 0:3, :], eb[:, :, TP:TT]))
                step(cp(f4[:, 3, :], c("gamma").to_broadcast([P, NS])))
                step(cp(k4[:, 0:3, :], k3[:, :, TP:TT]))
                step(nc.gpsimd.tensor_scalar(k4[:, 3, :], r2[:, 1, TP:TT], 32 ** -0.5, None, ALU.mult))
                step(cp(q4[:, 0:2, :], qv[:, 0:2, TP:TT]))
                step(tt(q4[:, 2, :], qv[:, 2, TP:TT], qv[:, 3, TP:TT], ALU.add))
                step(cp(q4[:, 3, :], r2[:, 0, TP:TT]))
                settle()
                for t in range(2):
                    step(tt(qs_hg[:, t, :, :], q4[:, t, :].unsqueeze(2).to_broadcast([P, NS, 2]),
                            c("m64").unsqueeze(1).to_broadcast([P, NS, 2]), ALU.mult))
                for n in range(2):
                    step(tt(qs_gr[:, n, :, :], q4[:, 2 + n, :].unsqueeze(2).to_broadcast([P, NS, 4]),
                            c("m32").unsqueeze(1).to_broadcast([P, NS, 4]), ALU.mult), q4_ready if n else None)

            def decay_sample_state(layer, n):
                step(tt(ss[:, n, :, :], ss[:, n, :, :], f4[:, n, :].unsqueeze(2).to_broadcast([P, NS, 64]), ALU.mult),
                     fs_ready if n == 3 else None)

            split = [0]
            for layer in range(DEPTH):
                at = layer * (NCH + KT)
                if layer == 0:
                    split_weights(0)
                lower_parts(2 * layer)
                split_weights(at + 1)
                if layer == 0:
                    for n in range(2):
                        pool.wait_ge(cst_in[n], 16)
                else:
                    pool.wait_ge(state_out, 16 * 8 * layer)
                    step(cp(f4[:, 3, 0:1], c("gamma")), stored)
                    pool.wait_ge(so_done, layer)
                    for dst, src in ((ss[:, 0:2, :, :], hg_in), (ss[:, 2, :, :], gla_in), (ss[:, 3, :, :], ret_in)):
                        pool.dma_start(dst, src[layer]).then_inc(ss_in[layer], 16)
                    pool.wait_ge(glu_done, layer)
                    pool.dma_start(wg[:, :, :, :], w_glu[layer]).then_inc(wg_in, 16)
                for part in range(4):
                    split_weights(at + 8 + part)
                    s5_c(layer, part)
                split_weights(at + 12)
                s5_samples(layer)
                split_weights(at + 15)
                sample_gates(layer)
                for n in range(4):
                    split_weights(at + 16 + n)
                    decay_sample_state(layer, n)
                sample_v(layer, 0)
                if layer + 1 < DEPTH:
                    pool.wait_ge(ca_ready, layer + 1)
                    pool.wait_ge(bb_ready, layer + 1)
                    pool.dma_start(s5m_t[:, :, :, :], s5m[layer + 1]).then_inc(s5m_in[layer + 1], 16)
                split_weights(at + 23)
                sample_v(layer, 1)
                split_weights(at + 24)
                sample_v(layer, 2)
                split_weights(at + 26)
                pool.wait_ge(s5f_ready, layer + 1)
                pool.wait_ge(s3_ready, layer + 1)
                pool.wait_ge(ss_ready, layer + 1)
                pool.wait_ge(st_ready, layer + 1)
                for dst, src in ((s5p_out[layer], s5f[:, :, :]), (s5s_out[layer], s5n[:, :, :, :]),
                                 (hgp_out[layer], s3[:, 0:2, NB, :]), (glap_out[layer], s3[:, 2, NB, :]),
                                 (retp_out[layer], retf[:, :]), (hgs_out[layer], ss[:, 0:2, :, :]),
                                 (glas_out[layer], ss[:, 2, :, :]), (rets_out[layer], ss[:, 3, :, :])):
                    pool.dma_start(dst, src).then_inc(state_out, 16)
                lower_parts(2 * layer + 1)
                split_weights(at + NCH + KT + 1)
            pool.wait_ge(state_out, 16 * 8 * DEPTH)


_OUTS = [("y", (P, KT, TT)), ("s5p", (DEPTH, P, 2, S5T)), ("hgp", (DEPTH, P, 2, 64)), ("glap", (DEPTH, P, 64)),
         ("retp", (DEPTH, P, 64)), ("s5s", (DEPTH, P, 2, S5T, NS)), ("hgs", (DEPTH, P, 2, NS, 64)),
         ("glas", (DEPTH, P, NS, 64)), ("rets", (DEPTH, P, NS, 64))]


def layouts(d):
    f = {k: np.ascontiguousarray(a) for k, a in d.items()}
    L = DEPTH
    out = {}
    xa = np.concatenate([f["x_prompt"][0], f["x_sample"][:, 0]], 0)
    out["xt"] = xa.reshape(TT, KT, P).transpose(2, 1, 0)
    w = f["w_in"]
    wi = np.zeros((L, NCH, P, KT, P), np.float32)
    for i, col in enumerate(CHUNKS):
        n = 16 if i == C_LR else P
        wi[:, i, :, :, 0:n] = w[:, :, col:col + n].reshape(L, KT, P, n).transpose(0, 2, 1, 3)
    out["w_in"] = wi
    out["w_out"] = f["w_out"].reshape(L, KT, P, KT, P).transpose(0, 3, 2, 1, 4)

    def tiles(a, n):
        return a.reshape(-1, P).T

    def s5(a):
        return a.reshape(L * S5T, P).T

    heads = np.stack([f["hgrn_norm_w"].reshape(L, 2, P), f["gla_norm_w"].reshape(L, 2, P),
                      f["ret_norm_w"].reshape(L, 2, P)], 1)
    skip = np.tile(f["s5_d"].reshape(L, S5T, 1, 32), (1, 1, 4, 1))
    step = np.repeat(f["s5_log_step"][:, :, None], 64, 2)
    out["par"] = np.concatenate([
        tiles(f["norm_w"], KT), tiles(f["final_norm_w"], KT), tiles(f["hgrn_lb_logits"], 2), tiles(f["gla_b_gate"], 1),
        tiles(heads, 6), tiles(skip, 8), s5(f["s5_lam_re"]), s5(f["s5_lam_im"]), s5(step)], 1)
    m = np.zeros((L, P, 4, S5T, 32), np.float32)
    for i, name in enumerate(("s5_b_re", "s5_b_im", "s5_c_re", "s5_c_im")):
        a = f[name] if i < 2 else f[name].transpose(0, 1, 3, 2)
        a = a.reshape(L, S5T, 2, 64, 16)
        for g in range(2):
            m[:, 64 * g:64 * g + 64, i, :, 16 * g:16 * g + 16] = a[:, :, g].transpose(0, 2, 1, 3)
    out["s5m"] = m
    out["w_glu"] = f["s5_w_glu"].reshape(L, 2, P, 2, P).transpose(0, 2, 1, 3, 4)
    out["w_up"] = f["gla_w_gate_up"].transpose(1, 0, 2)
    s5s = np.stack([f["state_s5_re"], f["state_s5_im"]], 1).reshape(L, 2, NS, S5T, P)
    out["s5_in"] = s5s.transpose(4, 0, 1, 3, 2)
    out["hg_in"] = f["state_hgrn"].reshape(L, NS, 2, P, 64).transpose(0, 3, 2, 1, 4)
    out["gla_in"] = f["state_gla"].reshape(L, NS, P, 64).transpose(0, 2, 1, 3)
    out["ret_in"] = f["state_ret"].reshape(L, NS, P, 64).transpose(0, 2, 1, 3)
    out["cst"], out["msk"] = constants()
    return {k: np.ascontiguousarray(a) for k, a in out.items()}


def kernel(**inputs):
    import concourse.bacc as bacc
    from concourse.bass_utils import run_bass_kernel_spmd

    nc = bacc.Bacc("TRN2", target_bir_lowering=False, num_devices=1)
    arrays = {"in_" + k: a for k, a in layouts(inputs).items()}
    args = [nc.dram_tensor(k, a.shape, mybir.dt.from_np(a.dtype), kind="ExternalInput").ap() for k, a in arrays.items()]
    args += [nc.dram_tensor("out_" + k, shape, F32, kind="ExternalOutput").ap() for k, shape in _OUTS]
    build(nc, *args)
    r = run_bass_kernel_spmd(nc, [arrays], core_ids=[0]).results[0]
    r = {k: np.asarray(r["out_" + k]) for k, _ in _OUTS}
    L = DEPTH
    y = r["y"].transpose(2, 1, 0).reshape(TT, D)
    s5p = r["s5p"].transpose(0, 2, 3, 1).reshape(L, 2, 1, 16, 64)
    s5s = r["s5s"].transpose(0, 2, 4, 3, 1).reshape(L, 2, NS, 16, 64)
    return (y[0:TP].reshape(1, TP, D), y[TP:].reshape(NS, 1, D),
            s5p[:, 0], s5p[:, 1],
            r["hgp"].transpose(0, 2, 1, 3).reshape(L, 1, 4, 64, 64),
            r["glap"].reshape(L, 1, 4, 32, 64), r["retp"].reshape(L, 1, 4, 32, 64),
            s5s[:, 0], s5s[:, 1],
            r["hgs"].transpose(0, 3, 2, 1, 4).reshape(L, NS, 4, 64, 64),
            r["glas"].transpose(0, 2, 1, 3).reshape(L, NS, 4, 32, 64),
            r["rets"].transpose(0, 2, 1, 3).reshape(L, NS, 4, 32, 64))
```

```python
from contextlib import ExitStack
from math import factorial

import numpy as np

import concourse.bass as bass
from concourse import mybir

F32 = mybir.dt.float32
I32 = mybir.dt.int32
F32R = mybir.dt.float32r
ALU = mybir.AluOpType
ACT = mybir.ActivationFunctionType

P = 128
DEPTH = 2
D = 1024
KT = D // P
TP = 256
NS = 8
TT = TP + NS
NCH = 25
NZ = 8
NP = NCH - NZ
BL = 32
NB = TP // BL
NL = 5
SL = 4
SC = TP // SL
S5T = 8
NPW = SL + 1
KH = KT // 2
RING = 7
WSLOTS = 4
A_LO_POOL = (0, 1, 2, 4)
A_LO_DVE = (3, 5, 6, 7)
EPS = 1e-6
LN2_HI, LN2_LO = 0.693359375, -2.12194440e-4
MAGIC = 12582912.0
TWO_PI = 6.283185
GELU_A, GELU_C = 0.044715, 0.7978845608028654

(C_LR, C_F0, C_F1, C_Q0, C_Q1, C_GQ, C_GK, C_I0, C_I1, C_GV0, C_GV1,
 C_RQ, C_RK, C_RV0, C_RV1, C_U0, C_U1) = range(NP)
CHUNKS = [2048, 768, 896, 512, 640, 1536, 1664, 1024, 1152, 1792, 1920, 2320, 2448, 2576, 2704, 0, 128,
          256, 384, 1280, 1408, 2064, 2192, 2832, 2960]

(Q_NORM, Q_FINAL, Q_LOGIT, Q_GLAB, Q_HEADG, Q_S5D, Q_LR, Q_LI, Q_LS, Q_END) = np.cumsum(
    [0, DEPTH * KT, KT, DEPTH * 2, DEPTH, DEPTH * 6, DEPTH * S5T, DEPTH * S5T, DEPTH * S5T,
     DEPTH * S5T]).tolist()
_CW = [("m64", 2), ("m32", 4), ("m32q", 4), ("m2", 2), ("gamma", 1), ("mult", NPW + SC),
       ("reset", TT), ("ident", P), ("rot", P),
       ("cos", TT), ("sin", TT), ("kdec", TP), ("decay", 4 * TP),
       ("pair", P), ("sel_a", P), ("sel_b", P), ("mean64", P), ("rev", P), ("eye64", 64)]
CST_PARTS = ("m64", "reset", "cos", "decay")
CW = {}
_at = 0
for _n, _w in _CW:
    CW[_n] = (_at, _at + _w)
    _at += _w
CN = _at
CST_AT = [CW[_n][0] for _n in CST_PARTS] + [CN]


def constants():
    p = np.arange(P)
    t = {}
    t["ident"] = np.eye(P)
    same64 = (p[:, None] // 64 == p[None, :] // 64)
    t["mean64"] = same64 / 64.0
    t["sel_a"] = (p[:, None] // 64 == p[None, :] // 32) / 64.0
    t["sel_b"] = (p[:, None] // 64 + 2 == p[None, :] // 32) / 64.0
    t["pair"] = (p[:, None] // 32 % 2 == p[None, :] // 64) * 1.0
    t["rev"] = ((p[:, None] % 32 == p[None, :] % 32) & (3 - p[:, None] // 32 == p[None, :] // 32)) * 1.0
    half = 16
    rot = np.zeros((P, P))
    for i in p:
        if i % 32 < half:
            rot[i + half, i] = -1.0
        else:
            rot[i - half, i] = 1.0
    t["rot"] = rot
    t["eye64"] = (p[:, None] % 64 == np.arange(64)[None, :]) * 64.0
    t["m64"] = (p[:, None] // 64 == np.arange(2)[None, :]) * 1.0
    t["m32"] = (p[:, None] // 32 == np.arange(4)[None, :]) * 1.0
    t["m32q"] = t["m32"] * 32 ** -0.5
    t["m2"] = ((p[:, None] // 32) % 2 == np.arange(2)[None, :]) * 1.0
    log_gamma = np.log1p(-np.exp2(-5.0 - np.arange(4)))
    lg = log_gamma[p // 32]
    t["gamma"] = np.exp(lg)[:, None]
    t["mult"] = np.tile(np.concatenate([np.arange(NPW), np.arange(SC)])[None, :], (P, 1))
    pos = np.arange(TT)
    t["reset"] = np.tile(np.where(pos < TP, pos % BL != 0, 0)[None, :], (P, 1))
    pos = np.where(pos < TP, pos, 2048).astype(np.float32)
    inv = (np.float32(10000.0) ** (-np.arange(half, dtype=np.float32) / np.float32(half))).astype(np.float32)
    ang = (pos[None, :] * inv[p % 32 % half][:, None]).astype(np.float32).astype(np.float64)
    t["cos"] = np.cos(ang)
    t["sin"] = np.sin(ang)
    t["kdec"] = np.exp((TP - 1 - np.arange(TP))[None, :] * lg[:, None]) * 32 ** -0.5
    rel = np.arange(TP)[None, :] - p[:, None]
    t["decay"] = np.concatenate([np.where(rel >= 0, np.exp(np.maximum(rel, 0) * g) * 32 ** -0.5, 0.0)
                                 for g in log_gamma], 1)
    big = np.concatenate([t[n] for n, _ in _CW], 1).astype(np.float32)
    mask = np.zeros((P, NL, 64), np.int32)
    for lev in range(NL):
        h = 1 << lev
        right = np.array([x for x in range(P) if (x // h) % 2 == 1])
        mask[:, lev, :] = (p[:, None] // (2 * h) == right[None, :] // (2 * h)) & ((p[:, None] // h) % 2 == 0)
    return big, mask


def build(nc, xt, w_in, w_out, par_d, s5m, w_glu, w_up, s5_in, hg_in, gla_in, ret_in, cst, msk,
          y_out, s5p_out, hgp_out, glap_out, retp_out, s5s_out, hgs_out, glas_out, rets_out):
    with ExitStack() as ctx:
        def sb(name, *shape, dt=F32):
            return ctx.enter_context(nc.sbuf_tensor(name, [P, *shape], dt))

        def sem(name):
            return ctx.enter_context(nc.semaphore(name))

        x = sb("x", KT, TT)
        a_hi, a_lo = sb("a_hi", KT, TT, dt=F32R), sb("a_lo", KT, TT, dt=F32R)
        w_hi, w_lo = sb("w_hi", WSLOTS, KH, P, dt=F32R), sb("w_lo", WSLOTS, KH, P, dt=F32R)
        wring = sb("wring", RING, KH, P)
        zs = sb("zs", KT, TT)
        h = zs
        parm = sb("parm", Q_END)
        cs = sb("cs", CN)
        masks = sb("masks", NL, 64, dt=I32)
        ones_d = sb("ones_d", P)
        qv = sb("qv", 8, TT)
        q3, qk = zs[:, 0:3, :], zs[:, 3:6, :]
        gates = sb("gates", 6, TT)
        x3, tl = gates[:, 0:3, :], gates[:, 3:6, :]
        k3 = sb("k3", 3, TT)
        eb = sb("eb", 3, TT)
        ke = sb("ke", 3, TT)
        u = sb("u", 2, TT)
        lr_t, rstd = u[:, 0, :], u[:, 1, :]
        v = sb("v", 6, TT)
        o = v
        r2 = ke[:, 0:2, :]
        rqm = sb("rqm", 2, TT)
        kd = sb("kd", TP)
        krt = sb("krt", 2, P)
        qm = sb("qm", 8, TP)
        flat_qm = qm[:, :, :].rearrange("p a t -> p (a t)")
        rs = flat_qm[:, 0:6 * TT].rearrange("p (a t) -> p a t", a=6)
        lev = sb("lev", 3 * 3 * TP + 2 * 8 * P)
        dl = [lev[:, 768 * i:768 * i + 768].rearrange("p (g t) -> p g t", g=3) for i in range(3)]
        ql = [lev[:, 2304 + 1024 * i:3328 + 1024 * i].rearrange("p (g t) -> p g t", g=8) for i in range(2)]
        kvb = lev[:, 0:2048]
        vd = lev[:, 2048:3072].rearrange("p (g n) -> p g n", g=2)
        osq = lev[:, 2048:2048 + 6 * TT].rearrange("p (g t) -> p g t", g=6)
        att = sb("att", 2, 8, P)
        attr = gates[:, :, :].rearrange("p a t -> p (a t)")[:, 0:4 * 384].rearrange("p (a t) -> p a t", a=4)
        rt1, rt2 = gates[:, 0:2, :], gates[:, 2:4, :]
        tok = sb("tok", 18 * P)
        vt = tok[:, 0:12 * P].rearrange("p (b t c) -> p b t c", b=2, t=6)
        ket = tok[:, 12 * P:18 * P].rearrange("p (b t c) -> p b t c", b=2, t=3)
        s3 = sb("s3", 3, NB + 1, 64)
        retf = sb("retf", 64)
        ss = sb("ss", 4, NS, 64)
        f4 = sb("f4", 4, NS)
        k4 = sb("k4", 4, NS)
        qs_hg = sb("qs_hg", 2, NS, 2)
        qs_gr = sb("qs_gr", 2, NS, 4)
        lbc = sb("lbc", 2, 2, 3)
        lbt = sb("lbt", 2, 4)
        s5m_t = sb("s5m_t", 4, S5T, 32)
        LS = DEPTH * S5T
        sw = sb("sw", 12, LS)
        turn4 = sb("turn4", LS)
        sincos = sb("sincos", 2, LS, NPW)
        sinp, cosp = sincos[:, 0, :, :], sincos[:, 1, :, :]
        sinc, cosc = sb("sinc", S5T, SC), sb("cosc", S5T, SC)
        turns, turnr = (lev[:, 3072 + i * S5T * SC:3072 + (i + 1) * S5T * SC] for i in range(2))
        mag = sb("mag", LS, NPW)
        are = sb("are", LS, NPW)
        aim = sb("aim", LS, NPW)
        mtmp = sb("mtmp", LS, NPW)
        gre = sb("gre", LS, SL)
        gim = sb("gim", LS, SL)
        gt1 = sb("gt1", LS, SL)
        gt2 = sb("gt2", LS, SL)
        m4 = lev[:, 3072:3072 + S5T * SC].rearrange("p (s k) -> p s k", s=S5T)
        bb_re, bb_im, bb_t = (lev[:, i * 1024:i * 1024 + 1024].rearrange("p (s j c) -> p s j c", s=S5T, j=SL) for i in range(3))
        ca_re = sb("ca_re", S5T, NPW, 32)
        ca_im = sb("ca_im", S5T, NPW, 32)
        gtr = qm[:, :, :].rearrange("p a t -> p (a t)").rearrange("p (n s m) -> p n s m", n=2, s=S5T)
        tmat = sb("tmat", S5T, P)
        ub = sb("ub", S5T, NS + SC + NS)
        sr = sb("sr", S5T, SC + NS)
        si = sb("si", S5T, SC + NS)
        s5i = sb("s5i", DEPTH, 2, S5T, NS)
        s5n = sb("s5n", 2, S5T, NS)
        s5t = sb("s5t", 4, S5T, NS)
        s5f = sb("s5f", 2, S5T)
        sv = [lev[:, 512 * i:512 * i + 512] for i in range(4)]
        NY = S5T * (NS + SC)
        yb, yt2 = lev[:, 3072:3072 + NY], lev[:, 3072 + NY:3072 + 2 * NY]
        yg = u
        wg = s5m_t[:, 0:2, :, :].rearrange("p a s c -> p (a s c)").rearrange("p (k m c) -> p k m c", k=2, m=2)
        wup = sb("wup", DEPTH, P)
        glu = rqm

        pr = [ctx.enter_context(nc.psum_tensor(f"pr{i}", [P, 512], F32)) for i in range(3)]
        wk = ctx.enter_context(nc.psum_tensor("wk", [P, 5, 512], F32))

        def c(name):
            return cs[:, CW[name][0]:CW[name][1]]

        x_in = [sem(f"x_in{i}") for i in range(2)]
        par_in, small_in = sem("par_in"), sem("small_in")
        cst_in = [sem(f"cst_in{i}") for i in range(4)]
        w_in_sem = [sem(f"w_slot{i}") for i in range(RING)]
        wup_in, angles_ready = sem("wup_in"), sem("angles_ready")
        wg_in = sem("wg_in")
        s5m_in = sem("s5m_in")
        state_out = sem("state_out")
        s5f_ready, r2_used = (sem(n) for n in ("s5f_ready", "r2_used"))
        ss_in = sem("ss_in")
        out_sem = sem("out_sem")
        sum_ready, diag_used = sem("sum_ready"), sem("diag_used")
        whi_ready, wlo_ready, half_done = (sem(n) for n in ("whi_ready", "wlo_ready", "half_done"))
        ahi_ready, alo_pool, alo_dve = sem("ahi_ready"), sem("alo_pool"), sem("alo_dve")
        ms_done, proj_done, lrup_done, s5v_done, diag_done, lvl_done, tr_done, kv_done = (
            sem(n) for n in ("ms_done", "proj_done", "lrup_done", "s5v_done", "diag_done", "lvl_done", "tr_done", "kv_done"))
        rot_done, rsc_done, y_done, vb_done, o_done, rst_done, so_done, glu_done = (
            sem(n) for n in ("rot_done", "rsc_done", "y_done", "vb_done", "o_done", "rst_done", "so_done", "glu_done"))
        mean_done, var_done, out_done, gtr_done, kt_done = (
            sem(n) for n in ("mean_done", "var_done", "out_done", "gtr_done", "kt_done"))
        act_step, sq_ready, rstd_ready, chunk_evac, l_ready, k3_ready, eb_ready, lexp_ready, tr_evac = (
            sem(n) for n in ("act_step", "sq_ready", "rstd_ready", "chunk_evac", "l_ready", "k3_ready", "eb_ready", "lexp_ready", "tr_evac"))
        gtr_evac, sin_ready, y_evac, tanh_ready, glu_tanh, osq_ready, ors_ready, lb_act, lb2_act = (
            sem(n) for n in ("gtr_evac", "sin_ready", "y_evac", "tanh_ready", "glu_tanh", "osq_ready", "ors_ready", "lb_act", "lb2_act"))
        dve_step, h_ready, t_ready, ls_ready, b_ready, de_ready, ld_ready, ql_ready, lvl_used = (
            sem(n) for n in ("dve_step", "h_ready", "t_ready", "ls_ready", "b_ready", "de_ready", "ld_ready", "ql_ready", "lvl_used"))
        lb_ready, tab_ready, tmat_ready, u_ready, s5v_used, s_ready, ke_ready, qv_ready = (
            sem(n) for n in ("lb_ready", "tab_ready", "tmat_ready", "u_ready", "s5v_used", "s_ready", "ke_ready", "qv_ready"))
        s3_ready, rqm_ready, attr_ready, ss_ready, tin_ready, yg_ready, qm_ready, vb_used = (
            sem(n) for n in ("s3_ready", "rqm_ready", "attr_ready", "ss_ready", "tin_ready", "yg_ready", "qm_ready", "vb_used"))
        o_ready, mean_used, mix_ready, out_used, fin_ready, st_ready, zero_ready = (
            sem(n) for n in ("o_ready", "mean_used", "mix_ready", "out_used", "fin_ready", "st_ready", "zero_ready"))
        pool_step, bb_ready, ca_ready, fs_ready, vd_ready, q4_ready, s5s_part, set_ready = (
            sem(n) for n in ("pool_step", "bb_ready", "ca_ready", "fs_ready", "vd_ready", "q4_ready", "s5s_part", "set_ready"))

        def chain(eng, steps):
            last = [None, {}]

            def step(ins, signal=None):
                s = signal if signal is not None else steps
                n = last[1].get(s.name, 0) + 1
                last[1][s.name] = n
                ins.then_inc(s, 1)
                last[0] = (s, n)

            def settle():
                eng.wait_ge(*last[0])
            return step, settle

        def par(col, n=1):
            return parm[:, col:col + n]

        def qrt(ap, q):
            return ap[32 * q:32 * q + 32]

        USES = NCH + 2 + 6 + KT

        def ring_free(eng, layer, i):
            i -= 3
            if i < 0:
                layer, i = layer - 1, i + USES
            if layer < 0:
                return
            if i < NCH:
                eng.wait_ge(chunk_evac, layer * NCH + i + 1)
            elif i < NCH + 2:
                eng.wait_ge(mean_used, layer * 2 + i - NCH + 1)
            elif i < NCH + 8:
                t = i - NCH - 2
                eng.wait_ge(ors_ready, layer * 8 + t + (1 if t < 4 else 2))
            else:
                eng.wait_ge(out_used, layer * KT + i - NCH - 8 + 1)

        def half_used(eng, j):
            if j < 0:
                return
            before, i = divmod(j // 2, NCH + KT)
            if j % 2 == 0:
                eng.wait_ge(half_done, j // 2 + 1)
            elif i < NCH:
                eng.wait_ge(proj_done, before * NCH + i + 1)
            else:
                eng.wait_ge(out_done, before * KT + i - NCH + 1)

        def part_ready(eng, n, k):
            if k in A_LO_DVE:
                eng.wait_ge(alo_dve, n * len(A_LO_DVE) + A_LO_DVE.index(k) + 1)
            else:
                eng.wait_ge(alo_pool, n * len(A_LO_POOL) + A_LO_POOL.index(k) + 1)

        def ring_bank(layer, i):
            return pr[(layer * USES + i) % 3]

        block = ctx.enter_context(nc.Block())

        @block.sync
        def _(sp):
            def const(i):
                part = slice(CST_AT[i], CST_AT[i + 1])
                sp.dma_start(cs[:, part], cst[:, part]).then_inc(cst_in[i], 16)

            for i in range(2):
                half = slice(KT // 2 * i, KT // 2 * (i + 1))
                sp.dma_start(x[:, half, :], xt[:, half, :]).then_inc(x_in[i], 16)
            use = 0

            def chunk(src):
                nonlocal use
                for half in (slice(0, KH), slice(KH, KT)):
                    if use >= RING:
                        sp.wait_ge(wlo_ready, use - RING + 1)
                    sp.dma_start(wring[:, use % RING, :, :], src[:, half]).then_inc(w_in_sem[use % RING], 16)
                    use += 1

            for layer in range(DEPTH):
                for i in range(NCH):
                    chunk(w_in[layer, i])
                    if layer == 0 and i == 1:
                        sp.dma_start(wup[0:16, :, :], w_up).then_inc(wup_in, 16)
                        sp.dma_start(s5m_t[:, :, :, :], s5m[0]).then_inc(s5m_in, 16)
                    if layer == 0 and i == 3:
                        const(1)
                    if layer == 0 and i == 5:
                        sp.dma_start(s5i[:, :, :, :, :], s5_in).then_inc(small_in, 16)
                        sp.dma_start(masks[:, :, :], msk).then_inc(small_in, 16)
                    if layer == 0 and i in (7, 9):
                        const(2 if i == 7 else 3)
                    if i == 11:
                        if layer:
                            sp.wait_ge(state_out, 16 * 8 * layer)
                            sp.wait_ge(so_done, layer)
                        sp.dma_start(ss[:, 0:2, :, :], hg_in[layer]).then_inc(ss_in, 16)
                        sp.dma_start(ss[:, 2, :, :], gla_in[layer]).then_inc(ss_in, 16)
                        sp.dma_start(ss[:, 3, :, :], ret_in[layer]).then_inc(ss_in, 16)
                    if i == NCH - 3:
                        sp.wait_ge(bb_ready, layer + 1)
                        sp.wait_ge(ca_ready, layer + 1)
                        sp.dma_start(wg, w_glu[layer]).then_inc(wg_in, 16)
                for i in range(KT):
                    chunk(w_out[layer, i])
                    if i == 3 and layer + 1 < DEPTH:
                        sp.wait_ge(glu_done, layer + 1)
                        sp.dma_start(s5m_t[:, :, :, :], s5m[layer + 1]).then_inc(s5m_in, 16)
                    if i == 4:
                        sp.wait_ge(s5f_ready, layer + 1)
                        sp.wait_ge(s3_ready, layer + 1)
                        sp.wait_ge(ss_ready, layer + 1)
                        sp.wait_ge(st_ready, layer + 1)
                    if i >= 4:
                        states = ((s5p_out[layer], s5f[:, :, :]), (s5s_out[layer], s5n[:, :, :, :]),
                                  (hgp_out[layer], s3[:, 0:2, NB, :]), (glap_out[layer], s3[:, 2, NB, :]),
                                  (retp_out[layer], retf[:, :]), (hgs_out[layer], ss[:, 0:2, :, :]),
                                  (glas_out[layer], ss[:, 2, :, :]), (rets_out[layer], ss[:, 3, :, :]))
                        for dst, src in states[2 * (i - 4):2 * (i - 4) + 2]:
                            sp.dma_start(dst, src).then_inc(state_out, 16)
            sp.wait_ge(state_out, 16 * 8 * DEPTH)
            for k in range(0, KT, 2):
                sp.wait_ge(fin_ready, k + 2)
                sp.dma_start(y_out[:, k:k + 2, :], h[:, k:k + 2, :]).then_inc(out_sem, 16)
            sp.wait_ge(out_sem, 16 * KT // 2)

        @block.tensor
        def _(pe):
            use = [0]

            def product(layer, i, done, operand):
                ring_free(pe, layer, i)
                for half in range(2):
                    slot = use[0] % WSLOTS
                    use[0] += 1
                    pe.wait_ge(wlo_ready, use[0])
                    for n in range(KH):
                        k = KH * half + n
                        if operand is not None:
                            part_ready(pe, operand, k)
                        for p, (w, a) in enumerate(((w_hi, a_hi), (w_hi, a_lo), (w_lo, a_hi))):
                            mm = nc.tensor.matmul(ring_bank(layer, i)[:, 0:TT], w[:, slot, n, :], a[:, k, :],
                                                  start=(k == 0 and p == 0), stop=(k == KT - 1 and p == 2))
                    mm.then_inc(done if half else half_done, 1)

            def mean_square(n):
                if n:
                    pe.wait_ge(sum_ready, n)
                    nc.tensor.matmul(wk[:, 0, 0:TT], ones_d[:, :], h[:, 0, :], start=True, stop=False)
                    pe.wait_ge(sq_ready, n * KT + KT)
                    nc.tensor.matmul(wk[:, 0, 0:TT], ones_d[:, :], h[:, KT - 1, :], start=False, stop=True).then_inc(ms_done, 1)
                    return
                for k in range(KT):
                    pe.wait_ge(sq_ready, k + 1)
                    mm = nc.tensor.matmul(wk[:, 0, 0:TT], ones_d[:, :], h[:, k, :], start=(k == 0), stop=(k == KT - 1))
                mm.then_inc(ms_done, 1)

            def project(layer, i):
                product(layer, i, proj_done, 2 * layer if i == 0 else None)

            def low_rank(layer):
                pe.wait_ge(chunk_evac, layer * NCH + C_LR + 1)
                if layer == 0:
                    pe.wait_ge(wup_in, 16)
                nc.tensor.matmul(wk[:, 1, 0:TT], wup[0:16, layer, :], lr_t[0:16, :], start=True, stop=True)\
                    .then_inc(lrup_done, 1)

            def s5_turn(layer):
                pe.wait_ge(bb_ready, layer + 1)
                pe.wait_ge(attr_ready, layer + 1)
                for r in range(4):
                    for n in range(4):
                        src = (bb_re, bb_im)[r // 2][:, 4 * (r % 2) + n, :, :]
                        mm = nc.tensor.transpose(wk[:, r, P * n:P * n + P], src.rearrange("p j c -> p (j c)"), c("ident"))
                    mm.then_inc(gtr_done, 1)

            def s5_response(layer):
                pe.wait_ge(ca_ready, layer + 1)
                pe.wait_ge(tr_evac, layer * 6 + 6)
                for s in range(S5T):
                    for n, (b, ca) in enumerate(((bb_re, ca_re), (bb_im, ca_im))):
                        mm = nc.tensor.matmul(wk[32 * (s // 4):32 * (s // 4) + 32, 4, P * (s % 4):P * (s % 4) + P], b[:, s, 0, :],
                                              ca[:, s, 0:SL, :].rearrange("p j c -> p (j c)"),
                                              start=(n == 0), stop=(n == 1))
                mm.then_inc(kt_done, 1)

            def s5_inputs(layer):
                pe.wait_ge(u_ready, layer + 1)
                pe.wait_ge(gtr_evac, layer * 4 + 4)
                for n in range(2):
                    for s in range(S5T):
                        a = (NS + SC) * (s % 4)
                        mm = nc.tensor.matmul(wk[:, 2 * n + s // 4, a:a + NS + SC], gtr[:, n, s, :], ub[:, s, 0:NS + SC],
                                              start=True, stop=True)
                mm.then_inc(s5v_done, 1)

            def s5_outputs(layer, n):
                if n == 0:
                    pe.wait_ge(s_ready, layer + 1)
                if n == 0:
                    pe.wait_ge(tmat_ready, layer + 1)
                if n:
                    pe.wait_ge(y_evac, layer * 2 + 1)
                for s in range(4 * n, 4 * n + 4):
                    dst = wk[:, 4, 72 * (s - 4 * n):72 * (s - 4 * n) + 72]
                    nc.tensor.matmul(dst, tmat[:, s, :], ub[:, s, NS:], start=True, stop=False)
                    nc.tensor.matmul(dst, ca_re[:, s, 1:NPW, :].rearrange("p j c -> p (j c)"), sr[:, s, :],
                                     start=False, stop=False)
                    mm = nc.tensor.matmul(dst, ca_im[:, s, 1:NPW, :].rearrange("p j c -> p (j c)"), si[:, s, :],
                                          start=False, stop=True)
                mm.then_inc(y_done, 1)

            def diagonal(layer):
                pe.wait_ge(qv_ready, layer + 1)
                pe.wait_ge(lvl_used, layer * NL + NL)
                if layer == 0:
                    pe.wait_ge(cst_in[3], 16)
                for t in range(2):
                    nc.tensor.matmul(wk[:, t, 0:TP], c("mean64"), qk[:, t, 0:TP], start=True, stop=True)
                    mm = nc.tensor.matmul(wk[:, t, TP:2 * TP], c("pair")[64 * t:64 * t + 64, :], qk[64 * t:64 * t + 64, 2, 0:TP], start=True, stop=True)
                mm.then_inc(diag_done, 1)

            def level(layer, n):
                pe.wait_ge(ql_ready, layer * NL + n + 1)
                if n >= 2:
                    pe.wait_ge(lvl_used, layer * NL + n - 1)
                bank = 2 * (n % 2)
                for blk in range(2):
                    S, T = slice(P * blk, P * blk + P), slice(64 * blk, 64 * blk + 64)
                    for t in range(2):
                        a = P * (2 * t + blk)
                        nc.tensor.matmul(wk[:, bank, a:a + P], dl[n % 3][:, t, S], ql[n % 2][:, 2 * t:2 * t + 2, T],
                                         start=True, stop=True)
                    mm = nc.tensor.matmul(wk[:, bank + 1, TP * blk:TP * blk + TP], dl[n % 3][:, 2, S], ql[n % 2][:, 4:8, T],
                                          start=True, stop=True)
                mm.then_inc(lvl_done, 1)

            def turn(layer, r, tiles):
                if r:
                    pe.wait_ge(tr_evac, layer * 6 + r)
                else:
                    if layer:
                        pe.wait_ge(o_ready, layer * 4)
                for n, t in enumerate(tiles):
                    mm = nc.tensor.transpose(wk[:, 4, P * n:P * n + P], t, c("ident"))
                mm.then_inc(tr_done, 1)

            def block_states(layer):
                pe.wait_ge(tr_evac, layer * 6 + 4)
                pe.wait_ge(r2_used, layer + 1)
                pe.wait_ge(diag_used, layer + 1)
                pe.wait_ge(lvl_used, layer * NL + NL)
                for blk in range(2):
                    for j in range(4):
                        rows = slice(32 * j, 32 * j + 32)
                        for hd in range(4):
                            t, hh = hd // 2, hd % 2
                            nc.tensor.matmul(wk[64 * hh:64 * hh + 64, j, (3 * blk + t) * 64:(3 * blk + t) * 64 + 64],
                                             ket[rows, blk, t, 64 * hh:64 * hh + 64],
                                             vt[rows, blk, t, 64 * hh:64 * hh + 64], start=True, stop=True)
                        for hd in range(4):
                            mm = nc.tensor.matmul(wk[32 * hd:32 * hd + 32, j, (3 * blk + 2) * 64:(3 * blk + 2) * 64 + 64],
                                                  ket[rows, blk, 2, 32 * hd:32 * hd + 32],
                                                  vt[rows, blk, 2 + hd // 2, 64 * (hd % 2):64 * (hd % 2) + 64],
                                                  start=True, stop=True)
                mm.then_inc(kv_done, 1)

            def rotate(layer):
                pe.wait_ge(chunk_evac, layer * NCH + C_RK + 1)
                pe.wait_ge(lvl_used, layer * NL + 4)
                for n in range(2):
                    mm = nc.tensor.matmul(wk[:, 2 + n, 0:TT], c("rot"), r2[:, n, :], start=True, stop=True)
                mm.then_inc(rot_done, 1)

            def ret_scores(layer):
                pe.wait_ge(rqm_ready, layer + 1)
                pe.wait_ge(s3_ready, layer + 1)
                for hd in range(4):
                    rows = slice(64 * (hd // 2), 64 * (hd // 2) + 64)
                    nc.tensor.matmul(wk[:, hd, 0:TP], r2[rows, 1, 0:P], rqm[rows, hd % 2, 0:TP], start=True, stop=True)
                    mm = nc.tensor.matmul(wk[:, hd, TP:384], r2[rows, 1, P:TP], rqm[rows, hd % 2, P:TP], start=True, stop=True)
                mm.then_inc(rsc_done, 1)

            def sample_v(layer, n):
                pe.wait_ge(vd_ready, layer * 3 + n + 1)
                if n == 0:
                    pe.wait_ge(s5v_used, layer + 1)
                    for t in range(2):
                        mm = nc.tensor.matmul(wk[:, t, :], c("mean64"), vd[:, t, :], start=True, stop=True)
                else:
                    for t in range(2):
                        mm = nc.tensor.matmul(wk[:, 1 + n, :], c(("sel_a", "sel_b")[t]), vd[:, t, :],
                                              start=(t == 0), stop=(t == 1))
                mm.then_inc(vb_done, 1)

            def gated_outputs(layer, kind):
                pe.wait_ge(vb_used, layer + 1)
                pe.wait_ge(lvl_used, layer * NL + NL)
                pe.wait_ge(qm_ready, layer + 1)
                pe.wait_ge(tr_evac, layer * 6 + 6)
                for t in range(2):
                    for hh in range(2):
                        rows = slice(64 * hh, 64 * hh + 64)
                        vtile = 2 * kind + t
                        for blk in range(2):
                            nc.tensor.matmul(wk[rows, kind, TP * t + P * blk:TP * t + P * blk + P],
                                             vt[:, blk, vtile, rows],
                                             att[:, kind, 4 * t + 2 * blk + hh if kind == 0 else 4 * blk + 2 * t + hh, :],
                                             start=(t == 0 and blk == 0), stop=False, skip_group_check=True)
                        for b in range(1, NB):
                            st = s3[:, t if kind == 0 else 2, b, :]
                            q = qm[:, 4 * kind + 2 * t + hh, BL * b:BL * b + BL]
                            mm = nc.tensor.matmul(wk[rows, kind, TP * t + BL * b:TP * t + BL * b + BL], st, q,
                                                  start=False, stop=(t == 1 and b == NB - 1), skip_group_check=True)
                mm.then_inc(o_done, 1)

            def ret_outputs(layer):
                for t in range(2):
                    for hh in range(2):
                        rows = slice(64 * hh, 64 * hh + 64)
                        nc.tensor.matmul(wk[rows, 2, TP * t:TP * t + TP], vt[:, 0, 4 + t, rows], attr[:, 2 * t + hh, 0:TP],
                                         start=(t == 0), stop=False, skip_group_check=True)
                        mm = nc.tensor.matmul(wk[rows, 2, TP * t + P:TP * t + TP], vt[:, 1, 4 + t, rows],
                                              attr[:, 2 * t + hh, TP:384], start=False, stop=(t == 1), skip_group_check=True)
                mm.then_inc(o_done, 1)
                for blk in range(2):
                    mm = nc.tensor.matmul(wk[:, 3, 0:TP], krt[:, blk, :],
                                          vt[:, blk, 4:6, :].rearrange("p a c -> p (a c)"), start=(blk == 0), stop=(blk == 1))
                mm.then_inc(rst_done, 1)

            def sample_outputs(layer, part):
                pe.wait_ge(ss_ready, layer + 1)
                pe.wait_ge(q4_ready, layer + 1)
                pe.wait_ge(y_evac, layer * 2 + 2)
                if part == 0:
                    for t in range(2):
                        for b in range(NS):
                            a = 2 * (NS * t + b)
                            nc.tensor.matmul(wk[0:64, 4, a:a + 2], ss[:, t, b, :], qs_hg[:, t, b, :], start=True, stop=True)
                else:
                    for n in range(2):
                        for b in range(NS):
                            a = 32 + 4 * (NS * n + b)
                            mm = nc.tensor.matmul(wk[0:64, 4, a:a + 4], ss[:, 2 + n, b, :], qs_gr[:, n, b, :],
                                                  start=True, stop=True)
                    mm.then_inc(so_done, 1)

            def glu_gate(layer):
                pe.wait_ge(yg_ready, layer + 1)
                pe.wait_ge(wg_in, 16 * (layer + 1))
                pe.wait_ge(o_ready, layer * 4 + 2)
                for m in range(2):
                    for k in range(2):
                        mm = nc.tensor.matmul(wk[:, m, 0:TT], wg[:, k, m, :], yg[:, k, :],
                                              start=(k == 0), stop=(k == 1))
                mm.then_inc(glu_done, 1)

            def ret_means(layer):
                pe.wait_ge(o_ready, layer * 4 + 4)
                for t in range(2):
                    i = NCH + t
                    ring_free(pe, layer, i)
                    nc.tensor.matmul(ring_bank(layer, i)[:, 0:TT], c("mean64"), o[:, 4 + t, :], start=True, stop=True)\
                        .then_inc(mean_done, 1)

            def head_norms(layer):
                for t in range(6):
                    i = NCH + 2 + t
                    ring_free(pe, layer, i)
                    pe.wait_ge(osq_ready, layer * 2 + (1 if t < 4 else 2))
                    nc.tensor.matmul(ring_bank(layer, i)[:, 0:TT], c("mean64"), osq[:, t, :], start=True, stop=True)\
                        .then_inc(var_done, 1)

            def project_out(layer, m):
                product(layer, NCH + 8 + m, out_done, 2 * layer + 1 if m == 0 else None)

            pe.wait_ge(zero_ready, 1)
            for layer in range(DEPTH):
                mean_square(layer)
                for i in range(NCH - 1):
                    project(layer, i)
                    if i == C_F0:
                        low_rank(layer)
                    if C_I1 <= i < C_I1 + NL:
                        level(layer, i - C_I1)
                    if i == C_GV0:
                        pe.wait_ge(ke_ready, layer + 1)
                        if layer == 0:
                            pe.wait_ge(cst_in[1], 16)
                        turn(layer, 0, [ke[:, t, 0:P] for t in range(3)])
                    if i == C_GV1:
                        turn(layer, 1, [ke[:, t, P:TP] for t in range(3)])
                    if i == C_RQ:
                        turn(layer, 2, [v[:, t, P * b:P * b + P] for b in range(2) for t in range(2)])
                    if i == C_RK:
                        turn(layer, 3, [v[:, 2 + t, P * b:P * b + P] for b in range(2) for t in range(2)])
                    if i == C_RV0:
                        rotate(layer)
                        diagonal(layer)
                    if i == C_RV1:
                        block_states(layer)
                    if i == C_U0:
                        pe.wait_ge(chunk_evac, layer * NCH + C_RV1 + 1)
                        turn(layer, 4, [v[:, 4 + t, P * b:P * b + P] for b in range(2) for t in range(2)])
                    if i == C_U1:
                        pe.wait_ge(rqm_ready, layer + 1)
                        turn(layer, 5, [kd[:, P * b:P * b + P] for b in range(2)])
                    if i == NP:
                        ret_scores(layer)
                    if i == NP + 1:
                        s5_turn(layer)
                        s5_response(layer)
                    if i == NP + 2:
                        s5_inputs(layer)
                    if i == NP + 4:
                        sample_v(layer, 0)
                    if i == NP + 5:
                        sample_v(layer, 1)
                    if i == NP + 6:
                        sample_v(layer, 2)
                s5_outputs(layer, 0)
                gated_outputs(layer, 0)
                s5_outputs(layer, 1)
                gated_outputs(layer, 1)
                ret_outputs(layer)
                sample_outputs(layer, 0)
                project(layer, NCH - 1)
                sample_outputs(layer, 1)
                ret_means(layer)
                glu_gate(layer)
                head_norms(layer)
                for m in range(KT):
                    project_out(layer, m)
            mean_square(DEPTH)

        @block.scalar
        def _(act):
            step, settle = chain(act, act_step)
            fn = nc.scalar.activation

            def use_logs():
                nc.scalar.preload_act_table_set("natural_log_exp_and_others")

            def use_silu():
                nc.scalar.preload_act_table_set("silu_and_others")

            def rsqrt_of(src, dst, signal):
                step(fn(dst, src, ACT.Ln, bias=EPS))
                settle()
                step(fn(dst, dst, ACT.Exp, scale=-0.5), signal)

            def norm(n):
                for k in range(KT):
                    if n == 0 and k % (KT // 2) == 0:
                        act.wait_ge(x_in[2 * k // KT], 16)
                    if n:
                        if k < KT - 1:
                            split_weights((n - 1) * (NCH + KT) + NCH + k + 2)
                        act.wait_ge(out_used, (n - 1) * KT + k + 1)
                    step(fn(h[:, k, :], x[:, k, :], ACT.Square), sq_ready)
                act.wait_ge(ms_done, n + 1)
                if n:
                    act.wait_ge(h_ready, n * KT)
                rsqrt_of(wk[:, 0, 0:TT], rstd, rstd_ready)

            def split_weights(chunk, halves=range(2)):
                if chunk >= DEPTH * (NCH + KT):
                    return
                for j in (2 * chunk + n for n in halves):
                    act.wait_ge(w_in_sem[j % RING], 16 * (j // RING + 1))
                    half_used(act, j - WSLOTS)
                    step(fn(w_hi[:, j % WSLOTS, :, :], wring[:, j % RING, :, :], ACT.Copy), whi_ready)

            def split_operand(n, tiles=range(KT)):
                for k in tiles:
                    if n % 2 == 0:
                        act.wait_ge(h_ready, n // 2 * KT + k + 1)
                        if n and k == 0:
                            act.wait_ge(out_done, n // 2 * KT)
                    else:
                        act.wait_ge(mix_ready, n // 2 * KT + k + 1)
                        if k == 0:
                            act.wait_ge(proj_done, (n // 2 + 1) * NCH)
                    step(fn(a_hi[:, k, :], zs[:, k, :], ACT.Copy), ahi_ready)

            def evac(layer, i, dst):
                split_weights(layer * (NCH + KT) + i + 2, [0])
                act.wait_ge(proj_done, layer * NCH + i + 1)
                m = dst.shape[0]
                step(fn(dst, ring_bank(layer, i)[0:m, 0:TT], ACT.Copy), chunk_evac)
                split_weights(layer * (NCH + KT) + i + 2, [1])

            def sines(s, c):
                step(fn(s[:, :, :], s[:, :, :], ACT.Sin, scale=TWO_PI))
                step(fn(c[:, :, :], c[:, :, :], ACT.Sin, scale=TWO_PI), sin_ready)

            def evac_heads(layer, i, t, heads, masks):
                split_weights(layer * (NCH + KT) + i + 2, [0])
                act.wait_ge(proj_done, layer * NCH + i + 1)
                for n in range(heads.shape[1]):
                    step(fn(heads[:, n, :], ring_bank(layer, i)[:, 0:TT], ACT.Copy, scale=c(masks)[:, n:n + 1]))
                step(fn(q3[:, t, :], ring_bank(layer, i)[:, 0:TT], ACT.Copy, scale=64.0 if t < 2 else 32 ** -0.5), chunk_evac)
                split_weights(layer * (NCH + KT) + i + 2, [1])

            def lower_bounds():
                act.wait_ge(lb_ready, 1)
                step(fn(lbt[:, :, 1], lbt[:, :, 0], ACT.Abs))
                settle()
                step(fn(lbt[:, :, 1], lbt[:, :, 1], ACT.Exp, scale=-1.0))
                settle()
                step(fn(lbt[:, :, 1], lbt[:, :, 1], ACT.Ln, bias=1.0), lb_act)

            def gate_logs(layer):
                act.wait_ge(lrup_done, layer + 1)
                if layer:
                    act.wait_ge(b_ready, layer)
                step(fn(x3[:, 2, :], wk[:, 1, 0:TT], ACT.Identity, bias=par(Q_GLAB + layer)))
                settle()
                step(fn(tl, x3, ACT.Abs))
                settle()
                step(fn(tl, tl, ACT.Exp, scale=-1.0))
                settle()
                step(fn(tl, tl, ACT.Ln, bias=1.0), l_ready)

            def keys(layer):
                act.wait_ge(t_ready, layer + 1)
                for t in range(2):
                    step(fn(k3[:, t, :], k3[:, t, :], ACT.Exp, scale=-1.0, bias=lbc[:, layer, t, 1:2]),
                         k3_ready if t == 1 else None)
                if layer:
                    act.wait_ge(ls_ready, layer + 1)
                    for t in range(2):
                        step(fn(eb[:, t, :], x3[:, t, :], ACT.Abs, bias=lbc[:, layer, t, 2:3]))
                    settle()
                    step(fn(eb[:, 0:2, :], eb[:, 0:2, :], ACT.Exp, scale=-1.0))
                    settle()
                    step(fn(eb[:, 0:2, :], eb[:, 0:2, :], ACT.Ln, bias=1.0), lb2_act)

            def decays(layer):
                act.wait_ge(b_ready, layer + 1)
                step(fn(eb[:, :, :], tl, ACT.Exp), eb_ready)
                act.wait_ge(de_ready, layer + 1)
                step(fn(ke[:, :, 0:TP], ke[:, :, 0:TP], ACT.Exp), eb_ready)

            def level_exp(layer, n):
                act.wait_ge(ld_ready, layer * NL + n + 1)
                step(fn(dl[n % 3], dl[n % 3], ACT.Exp), lexp_ready)

            def turned(layer, r, dst):
                act.wait_ge(tr_done, layer * 6 + r + 1)
                n = dst.free_size()
                step(fn(dst, wk[:, 4, 0:n] if len(dst.shape) == 2 else
                        wk[:, 4, 0:n].rearrange("p (a b) -> p a b", a=dst.shape[1]) if len(dst.shape) == 3 else
                        wk[:, 4, 0:n].rearrange("p (a b c) -> p a b c", a=dst.shape[1], b=dst.shape[2]), ACT.Copy), tr_evac)

            def s5_turned(layer, rounds):
                for r in rounds:
                    act.wait_ge(gtr_done, layer * 4 + r + 1)
                    step(fn(gtr[:, r // 2, 4 * (r % 2):4 * (r % 2) + 4, :].rearrange("p s m -> p (s m)"),
                            wk[:, r, :], ACT.Copy), gtr_evac)

            def silu(layer, i):
                split_weights(layer * (NCH + KT) + i + 2, [0])
                act.wait_ge(proj_done, layer * NCH + i + 1)
                step(fn(zs[:, i - NP, :], ring_bank(layer, i)[:, 0:TT], ACT.Silu), chunk_evac)
                split_weights(layer * (NCH + KT) + i + 2, [1])

            def s5_evac(layer, n):
                act.wait_ge(y_done, layer * 2 + n + 1)
                step(fn(yb[:, NY // 2 * n:NY // 2 * n + NY // 2], wk[:, 4, 0:NY // 2], ACT.Copy), y_evac)

            act.dma_start(parm[:, :], par_d).then_inc(par_in, 16)
            act.dma_start(cs[:, 0:CST_AT[1]], cst[:, 0:CST_AT[1]]).then_inc(cst_in[0], 16)
            use_logs()
            for layer in range(DEPTH):
                if layer == 0:
                    split_weights(0)
                norm(layer)
                split_operand(2 * layer)
                split_weights(layer * (NCH + KT) + 1)
                if layer == 0:
                    act.wait_ge(par_in, 16)
                    act.wait_ge(cst_in[0], 16)
                    lower_bounds()
                evac(layer, C_LR, lr_t[0:16, :])
                evac(layer, C_F0, x3[:, 0, :])
                evac(layer, C_F1, x3[:, 1, :])
                gate_logs(layer)
                evac_heads(layer, C_Q0, 0, qv[:, 0:2, :], "m64")
                if layer:
                    keys(layer)
                evac_heads(layer, C_Q1, 1, qv[:, 2:4, :], "m64")
                if layer == 0:
                    keys(layer)
                evac_heads(layer, C_GQ, 2, qv[:, 4:8, :], "m32q")
                evac(layer, C_GK, k3[:, 2, :])
                decays(layer)
                level_exp(layer, 0)
                evac(layer, C_I0, v[:, 0, :])
                level_exp(layer, 1)
                evac(layer, C_I1, v[:, 1, :])
                level_exp(layer, 2)
                evac(layer, C_GV0, v[:, 2, :])
                turned(layer, 0, ket[:, 0, :, :])
                level_exp(layer, 3)
                evac(layer, C_GV1, v[:, 3, :])
                turned(layer, 1, ket[:, 1, :, :])
                evac(layer, C_RQ, r2[:, 0, :])
                turned(layer, 2, vt[:, :, 0:2, :])
                level_exp(layer, 4)
                evac(layer, C_RK, r2[:, 1, :])
                turned(layer, 3, vt[:, :, 2:4, :])
                evac(layer, C_RV0, v[:, 4, :])
                evac(layer, C_RV1, v[:, 5, :])
                evac(layer, C_U0, u[:, 0, :])
                use_silu()
                turned(layer, 4, vt[:, :, 4:6, :])
                evac(layer, C_U1, u[:, 1, :])
                turned(layer, 5, krt[:, :, :])
                for i in range(NP, NCH):
                    if i == NCH - 1:
                        for n in range(2):
                            s5_evac(layer, n)
                        act.wait_ge(tin_ready, layer + 1)
                        step(fn(yt2, yt2, ACT.Tanh, scale=GELU_C), tanh_ready)
                    silu(layer, i)
                    if i == NP + 1:
                        act.wait_ge(angles_ready, layer + 1)
                        sines(sinc, cosc)
                        s5_turned(layer, range(4))
                act.wait_ge(glu_done, layer + 1)
                step(fn(glu[:, :, :], wk[:, 0:2, 0:TT], ACT.Tanh, scale=0.5), glu_tanh)
                use_logs()
                for tiles in (range(0, 4), range(4, 6)):
                    for t in tiles:
                        act.wait_ge(var_done, layer * 6 + t + 1)
                        step(fn(rs[:, t, :], ring_bank(layer, NCH + 2 + t)[:, 0:TT], ACT.Ln, bias=EPS), ors_ready)
                    settle()
                    part = rs[:, tiles.start:tiles.stop, :]
                    step(fn(part, part, ACT.Exp, scale=-0.5), ors_ready)
                    split_operand(2 * layer + 1, range(0, 2) if tiles.start == 0 else range(2, KT))
            norm(DEPTH)

        @block.vector
        def _(dve):
            step, settle = chain(dve, dve_step)
            tt, ts, stt, cp = (nc.vector.tensor_tensor, nc.vector.tensor_scalar,
                               nc.vector.scalar_tensor_tensor, nc.vector.tensor_copy)

            def scale_x(n, weights, signal):
                dve.wait_ge(rstd_ready, n + 1)
                for k in range(KT):
                    step(stt(out=h[:, k, :], in0=x[:, k, :], scalar=par(weights + k), in1=rstd,
                             op0=ALU.mult, op1=ALU.mult), signal)
                if n < DEPTH:
                    lower_parts(2 * n)

            def lower_parts(n):
                for k in A_LO_DVE:
                    dve.wait_ge(ahi_ready, n * KT + k + 1)
                    step(tt(a_lo[:, k, :], zs[:, k, :], a_hi[:, k, :].bitcast(F32), ALU.subtract), alo_dve)

            def lower_bounds():
                step(tt(lbt[:, :, 0], par(Q_LOGIT + 2, 2), par(Q_LOGIT, 2), ALU.subtract), lb_ready)
                step(nc.vector.memset(lbc[:, 0, :, :], 0.0))
                dve.wait_ge(lb_act, 1)
                step(ts(lbt[:, :, 2], lbt[:, :, 0], 0.0, None, ALU.min))
                step(ts(lbt[:, :, 3], lbt[:, :, 0], 0.0, None, ALU.max))
                settle()
                step(tt(lbc[:, 1, :, 0], lbt[:, :, 2], lbt[:, :, 1], ALU.subtract))
                step(stt(out=lbc[:, 1, :, 1], in0=lbt[:, :, 3], scalar=-1.0, in1=lbt[:, :, 1], op0=ALU.mult, op1=ALU.subtract))
                settle()
                step(tt(lbc[:, 1, :, 2], lbc[:, 1, :, 1], lbc[:, 1, :, 0], ALU.subtract))
                settle()

            def accurate_exp(dst, src, tmp):
                r, k, q = tmp
                step(ts(r, src, -87.0, 88.0, ALU.max, ALU.min))
                settle()
                step(ts(k, r, 1.4426950408889634, MAGIC, ALU.mult, ALU.add))
                settle()
                step(ts(k, k, MAGIC, None, ALU.subtract))
                settle()
                for part in (LN2_HI, LN2_LO):
                    step(stt(out=r, in0=k, scalar=-part, in1=r, op0=ALU.mult, op1=ALU.add))
                    settle()
                step(ts(q, r, 1.0 / 5040, None, ALU.mult))
                for n in (720, 120, 24, 6, 2, 1):
                    settle()
                    step(stt(out=q, in0=q, scalar=1.0 / n, in1=r, op0=ALU.add, op1=ALU.mult))
                step(ts(k.bitcast(I32), k, 127.0, None, ALU.add))
                settle()
                step(ts(k.bitcast(I32), k.bitcast(I32), 23, None, ALU.logical_shift_left))
                settle()
                step(stt(out=dst, in0=q, scalar=1.0, in1=k, op0=ALU.add, op1=ALU.mult))
                settle()

            def s5_phases():
                lr, li = par(Q_LR, LS), par(Q_LI, LS)
                accurate_exp(sw[:, 0, :], par(Q_LS, LS), [sw[:, n, :] for n in (1, 2, 3)])
                step(tt(sw[:, 1, :], lr, sw[:, 0, :], ALU.mult))
                step(tt(sw[:, 2, :], li, sw[:, 0, :], ALU.mult))
                settle()
                step(tt(mag[:, :, :], sw[:, 1, :].unsqueeze(2).to_broadcast([P, LS, NPW]),
                        c("mult")[:, 0:NPW].unsqueeze(1).to_broadcast([P, LS, NPW]), ALU.mult))
                settle()
                flat = mag[:, :, :].rearrange("p s m -> p (s m)")
                accurate_exp(flat, flat, [z[:, :, :].rearrange("p s m -> p (s m)") for z in (are, aim, mtmp)])
                step(ts(sw[:, 2, :], sw[:, 2, :], 1.0 / (2 * np.pi), None, ALU.mult))
                settle()
                step(ts(sw[:, 3, :], sw[:, 2, :], MAGIC, MAGIC, ALU.add, ALU.subtract))
                settle()
                step(tt(sw[:, 2, :], sw[:, 2, :], sw[:, 3, :], ALU.subtract))
                settle()
                step(ts(sw[:, 3, :], sw[:, 2, :], float(SL), None, ALU.mult))
                settle()
                step(ts(sw[:, 4, :], sw[:, 3, :], MAGIC, MAGIC, ALU.add, ALU.subtract))
                settle()
                step(tt(turn4[:, :], sw[:, 3, :], sw[:, 4, :], ALU.subtract))
                settle()
                s5_turns(sw[:, 2, :], c("mult")[:, 0:NPW], sinp, cosp, None)

            def accurate_sines():
                x1 = sincos[:, :, :, :].rearrange("p a s m -> p (a s m)")
                x2, q = (z[:, 0:x1.free_size()] for z in (turns, turnr))
                step(ts(x1, x1, 2 * np.pi, None, ALU.mult))
                settle()
                step(tt(x2, x1, x1, ALU.mult))
                settle()
                series = [(-1.0) ** (k // 2) / factorial(k) for k in range(19, 1, -2)]
                step(ts(q, x2, series[0], None, ALU.mult))
                for term in series[1:]:
                    settle()
                    step(stt(out=q, in0=q, scalar=term, in1=x2, op0=ALU.add, op1=ALU.mult))
                settle()
                step(stt(out=x1, in0=q, scalar=1.0, in1=x1, op0=ALU.add, op1=ALU.mult))
                settle()

            def s5_turns(turn, mult, dst_sin, dst_cos, signal):
                n, m = turn.free_size(), mult.free_size()
                t, r = (z[:, 0:n * m].rearrange("p (s m) -> p s m", s=n) for z in (turns, turnr))
                step(tt(t, turn.unsqueeze(2).to_broadcast([P, n, m]), mult.unsqueeze(1).to_broadcast([P, n, m]), ALU.mult))
                settle()
                step(ts(r, t, MAGIC, MAGIC, ALU.add, ALU.subtract))
                settle()
                step(tt(dst_sin[:, :, :], t, r, ALU.subtract))
                step(ts(t, t, 0.25, None, ALU.add))
                settle()
                step(ts(r, t, MAGIC, MAGIC, ALU.add, ALU.subtract))
                settle()
                step(tt(dst_cos[:, :, :], t, r, ALU.subtract), signal)

            def s5_chunk_angles(layer):
                if layer:
                    settle()
                s5_turns(turn4[:, S5T * layer:S5T * layer + S5T], c("mult")[:, NPW:], sinc, cosc, angles_ready)

            def s5_coefficients():
                lr, li = par(Q_LR, LS), par(Q_LI, LS)
                step(tt(are[:, :, :], mag[:, :, :], cosp[:, :, :], ALU.mult))
                step(tt(aim[:, :, :], mag[:, :, :], sinp[:, :, :], ALU.mult))
                step(tt(sw[:, 3, :], lr, lr, ALU.mult))
                step(tt(sw[:, 4, :], li, li, ALU.mult))
                settle()
                step(tt(sw[:, 3, :], sw[:, 3, :], sw[:, 4, :], ALU.add))
                step(ts(sw[:, 5, :], are[:, :, 1], -1.0, None, ALU.add))
                settle()
                step(nc.vector.reciprocal(sw[:, 4, :], sw[:, 3, :]))
                step(tt(sw[:, 6, :], sw[:, 5, :], lr, ALU.mult))
                step(tt(sw[:, 7, :], aim[:, :, 1], li, ALU.mult))
                step(tt(sw[:, 8, :], aim[:, :, 1], lr, ALU.mult))
                step(tt(sw[:, 9, :], sw[:, 5, :], li, ALU.mult))
                settle()
                step(tt(sw[:, 6, :], sw[:, 6, :], sw[:, 7, :], ALU.add))
                step(tt(sw[:, 8, :], sw[:, 8, :], sw[:, 9, :], ALU.subtract))
                settle()
                step(tt(sw[:, 10, :], sw[:, 6, :], sw[:, 4, :], ALU.mult))
                step(tt(sw[:, 11, :], sw[:, 8, :], sw[:, 4, :], ALU.mult))
                settle()
                fr = sw[:, 10, :].unsqueeze(2).to_broadcast([P, LS, SL])
                fi = sw[:, 11, :].unsqueeze(2).to_broadcast([P, LS, SL])
                step(tt(gre[:, :, :], are[:, :, 0:SL], fr, ALU.mult))
                step(tt(gt1[:, :, :], aim[:, :, 0:SL], fi, ALU.mult))
                step(tt(gim[:, :, :], are[:, :, 0:SL], fi, ALU.mult))
                step(tt(gt2[:, :, :], aim[:, :, 0:SL], fr, ALU.mult))
                settle()
                step(tt(gre[:, :, :], gre[:, :, :], gt1[:, :, :], ALU.subtract))
                step(tt(gim[:, :, :], gim[:, :, :], gt2[:, :, :], ALU.add), tab_ready)

            def s5_c(layer, part):
                L = slice(S5T * layer, S5T * layer + S5T)
                dve.wait_ge(s5m_in, 16 * (layer + 1))
                if layer:
                    dve.wait_ge(y_done, layer * 2)
                settle()
                a_r, a_i = (z[:, L, :].unsqueeze(3).to_broadcast([P, S5T, NPW, 32]) for z in (are, aim))
                c_r, c_i = (s5m_t[:, 2 + n, :, :].unsqueeze(2).to_broadcast([P, S5T, NPW, 32]) for n in range(2))
                t = flat_qm[:, 0:S5T * NPW * 32].rearrange("p (s n c) -> p s n c", s=S5T, n=NPW)
                if part == 0:
                    step(tt(ca_re[:, :, :, :], a_r, c_r, ALU.mult))
                    step(tt(t, a_i, c_i, ALU.mult))
                    settle()
                    step(tt(ca_re[:, :, :, :], ca_re[:, :, :, :], t, ALU.subtract))
                else:
                    step(tt(ca_im[:, :, :, :], a_r, c_i, ALU.mult))
                    step(tt(t, a_i, c_r, ALU.mult))
                    settle()
                    step(stt(out=ca_im[:, :, :, :], in0=ca_im[:, :, :, :], scalar=-1.0, in1=t, op0=ALU.mult, op1=ALU.subtract),
                         ca_ready)

            def s5_b(layer):
                L = slice(S5T * layer, S5T * layer + S5T)
                dve.wait_ge(s5m_in, 16 * (layer + 1))
                dve.wait_ge(lvl_done, layer * NL + NL)
                settle()
                g_r, g_i = (z[:, L, :].unsqueeze(3).to_broadcast([P, S5T, SL, 32]) for z in (gre, gim))
                b_r, b_i = (s5m_t[:, n, :, :].unsqueeze(2).to_broadcast([P, S5T, SL, 32]) for n in range(2))
                step(tt(bb_re, g_r, b_r, ALU.mult))
                step(tt(bb_t, g_i, b_i, ALU.mult))
                step(tt(bb_im, g_r, b_i, ALU.mult))
                settle()
                step(tt(bb_re, bb_re, bb_t, ALU.subtract))
                settle()
                step(tt(bb_t, g_i, b_r, ALU.mult))
                settle()
                step(tt(bb_im, bb_im, bb_t, ALU.add), bb_ready)

            def s5_within(layer):
                settle()
                if layer:
                    dve.wait_ge(y_done, layer * 2)
                step(cp(m4[:, :, :], mag[:, S5T * layer:S5T * layer + S5T, SL:SL + 1].to_broadcast([P, S5T, SC])))
                settle()
                step(nc.vector.memset(m4[:, :, 0:1], 0.0))
                dve.wait_ge(kt_done, layer + 1)
                for q in range(4):
                    for half in range(2):
                        src = wk[32 * half:32 * half + 32, 4, :].rearrange("p (s m) -> p s m", s=4)[:, :, 0:32 * (q + 1)]
                        step(cp(qrt(tmat, q)[:, 4 * half:4 * half + 4, 32 * (3 - q):P], src))
                settle()
                for s in range(S5T):
                    step(stt(out=tmat[:, s, :], in0=c("rev"), scalar=par(Q_S5D + layer * S5T + s), in1=tmat[:, s, :],
                             op0=ALU.mult, op1=ALU.add), tmat_ready if s == S5T - 1 else None)

            def s5_relay(layer):
                dve.wait_ge(chunk_evac, layer * NCH + C_U1 + 1)
                if layer:
                    dve.wait_ge(y_done, layer * 2)
                for a in range(4):
                    src = qrt(u, a)[:, :, 0:TP].rearrange("p t (k j) -> p t k j", j=SL)
                    for q in range(4):
                        dst = qrt(ub, q)[:, :, NS:NS + SC].rearrange("p (t s) k -> p t s k", t=2)[:, :, a, :]
                        step(cp(dst, src[:, :, :, 3 - q]))
                    for n, dst in enumerate((qrt(ub, 3)[:, :, NS + SC:], qrt(ub, 0)[:, :, 0:NS])):
                        step(cp(dst.rearrange("p (t s) k -> p t s k", t=2)[:, :, a, :], qrt(u, a)[:, :, TP:TT]),
                             u_ready if a == 3 and n == 1 else None)

            def s5_scan(layer):
                co, sn = cosc[:, :, :], sinc[:, :, :]
                inputs = [wk[:, 2 * n:2 * n + 2, 0:4 * (NS + SC)].rearrange("p a (s k) -> p a s k", s=4) for n in range(2)]
                vr, vi = (z[:, :, :, NS:] for z in inputs)
                t = [z.rearrange("p (s k) -> p s k", s=S5T) for z in sv]
                t4 = [z.rearrange("p (a s k) -> p a s k", a=2, s=4) for z in sv]
                co4, sn4 = (z[:, :, :].rearrange("p (a s) k -> p a s k", a=2) for z in (cosc, sinc))
                dve.wait_ge(s5v_done, layer + 1)
                dve.wait_ge(sin_ready, layer + 1)
                if layer:
                    dve.wait_ge(state_out, 16 * 8 * layer)
                step(tt(t4[0], vr, co4, ALU.mult))
                step(tt(t4[1], vi, sn4, ALU.mult))
                step(tt(t4[2], vi, co4, ALU.mult))
                step(tt(t4[3], vr, sn4, ALU.mult))
                dve.wait_ge(s5s_part, layer + 1)
                for n in range(2):
                    step(tt(s5n[:, n, :, :].rearrange("p (a s) b -> p a s b", a=2),
                            s5t[:, 2 * n, :, :].rearrange("p (a s) b -> p a s b", a=2),
                            inputs[n][:, :, :, 0:NS], ALU.add), s5v_used if n else None)
                settle()
                step(tt(t[0], t[0], t[1], ALU.add))
                step(tt(t[2], t[2], t[3], ALU.subtract))
                settle()
                m = m4[:, :, :].rearrange("p s k -> p (s k)")
                step(nc.vector.tensor_tensor_scan(sv[1], m, sv[0], 0.0, ALU.mult, ALU.add))
                step(nc.vector.tensor_tensor_scan(sv[3], m, sv[2], 0.0, ALU.mult, ALU.add))
                settle()
                step(tt(t[0], t[1], co, ALU.mult))
                step(tt(t[2], t[3], sn, ALU.mult))
                settle()
                step(tt(sr[:, :, 1:SC], t[0][:, :, 0:SC - 1], t[2][:, :, 0:SC - 1], ALU.subtract))
                step(tt(s5f[:, 0, :], t[0][:, :, SC - 1], t[2][:, :, SC - 1], ALU.subtract))
                settle()
                step(tt(t[0], t[1], sn, ALU.mult))
                step(tt(t[2], t[3], co, ALU.mult))
                settle()
                step(tt(si[:, :, 1:SC], t[0][:, :, 0:SC - 1], t[2][:, :, 0:SC - 1], ALU.add), s_ready)
                step(tt(s5f[:, 1, :], t[0][:, :, SC - 1], t[2][:, :, SC - 1], ALU.add), s5f_ready)
                settle()

            def gate(layer):
                dve.wait_ge(l_ready, layer + 1)
                step(stt(out=k3[:, 0:2, :], in0=x3[:, 0:2, :], scalar=0.0, in1=tl[:, 0:2, :], op0=ALU.max, op1=ALU.add), t_ready)
                settle()
                step(stt(out=x3, in0=x3, scalar=0.0, in1=tl, op0=ALU.min, op1=ALU.subtract), ls_ready)
                settle()
                step(ts(x3[:, 2, :], x3[:, 2, :], 1.0 / 16.0, None, ALU.mult))
                if layer:
                    for t in range(2):
                        step(ts(tl[:, t, :], x3[:, t, :], lbc[:, layer, t, 1:2], lbc[:, layer, t, 0:1], ALU.add, ALU.max))
                    dve.wait_ge(lb2_act, layer)
                    settle()
                    step(tt(x3[:, 0:2, :], tl[:, 0:2, :], eb[:, 0:2, :], ALU.add))
                settle()
                for t in range(3):
                    step(nc.vector.tensor_tensor_scan(tl[:, t, :], c("reset"), x3[:, t, :], 0.0, ALU.mult, ALU.add),
                         b_ready if t == 2 else None)
                settle()
                bb = tl[:, :, 0:TP].rearrange("p a (b t) -> p a b t", t=BL)
                step(tt(ke[:, :, 0:TP].rearrange("p a (b t) -> p a b t", t=BL),
                        bb[:, :, :, BL - 1:BL].to_broadcast([P, 3, NB, BL]), bb, ALU.subtract), de_ready)

            def halves(ap, n):
                return ap.rearrange("p g (n w h) -> p g n w h", w=2, h=1 << n)

            def level_diff(layer, n):
                if n >= 3:
                    dve.wait_ge(lvl_done, layer * NL + n - 2)
                b = halves(tl[:, :, 0:TP], n)
                d = halves(dl[n % 3], n)
                hh = 1 << n
                mid = b[:, :, :, 0, hh - 1:hh].to_broadcast([P, 3, TP // (2 * hh), hh])
                step(tt(d[:, :, :, 1, :], b[:, :, :, 1, :], mid, ALU.subtract))
                step(tt(d[:, :, :, 0, :], mid, b[:, :, :, 0, :], ALU.subtract), ld_ready)

            def level_operands(layer, n):
                dve.wait_ge(lexp_ready, layer * NL + n + 1)
                if n >= 2:
                    dve.wait_ge(lvl_done, layer * NL + n - 1)
                d, kk = halves(dl[n % 3], n), halves(k3[:, :, 0:TP], n)
                qq = halves(qv[:, :, 0:TP], n)
                dst = ql[n % 2].rearrange("p g (n h) -> p g n h", h=1 << n)
                step(tt(d[:, :, :, 0, :], kk[:, :, :, 0, :], d[:, :, :, 0, :], ALU.mult))
                for t, G in enumerate((slice(0, 2), slice(2, 4), slice(4, 8))):
                    step(tt(dst[:, G], qq[:, G, :, 1, :],
                            d[:, t:t + 1, :, 1, :].to_broadcast([P, G.stop - G.start, TP >> (n + 1), 1 << n]), ALU.mult),
                         ql_ready if t == 2 else None)

            def level_scores(layer, n):
                dve.wait_ge(lvl_done, layer * NL + n + 1)
                settle()
                for g in range(2):
                    out = halves(att[:, g], n)[:, :, :, 1, :]
                    data = wk[:, 2 * (n % 2) + g, :].rearrange("p (g n h) -> p g n h", g=8, h=1 << n)
                    mk = masks[:, n, :].rearrange("p (n h) -> p n h", h=1 << n).unsqueeze(1).to_broadcast([P, 8, 64 >> n, 1 << n])
                    step(nc.vector.copy_predicated(out, mk, data), lvl_used if g else None)

            def decayed_q(layer):
                if layer:
                    dve.wait_ge(ors_ready, layer * 8)
                for t, G in enumerate((slice(0, 2), slice(2, 4), slice(4, 8))):
                    step(tt(qm[:, G, :], qv[:, G, 0:TP], eb[:, t:t + 1, 0:TP].to_broadcast([P, G.stop - G.start, TP]), ALU.mult),
                         qm_ready if t == 2 else None)

            def diagonal(layer):
                dve.wait_ge(diag_done, layer + 1)
                dve.wait_ge(tr_evac, layer * 6 + 4)
                for kind in range(2):
                    dst = v[:, 2 * kind:2 * kind + 2, 0:TP]
                    step(tt(dst, dst, wk[:, 0:2, TP * kind:TP * kind + TP], ALU.mult), diag_used if kind else None)

            def carry(layer):
                dve.wait_ge(kv_done, layer + 1)
                if layer:
                    dve.wait_ge(state_out, 16 * 8 * layer)
                dve.wait_ge(tr_evac, layer * 6 + 4)
                dec = eb[:, :, 0:TP].rearrange("p a (b t) -> p a b t", t=BL)
                for b in range(NB):
                    kv = wk[:, b % 4, 192 * (b // 4):192 * (b // 4) + 192].rearrange("p (a c) -> p a c", a=3)
                    if b:
                        settle()
                        for t in range(3):
                            step(stt(out=s3[:, t, b + 1, :], in0=s3[:, t, b, :], scalar=dec[:, t, b, BL - 1:BL],
                                     in1=kv[:, t, :], op0=ALU.mult, op1=ALU.add), s3_ready if b == NB - 1 and t == 2 else None)
                    else:
                        step(cp(s3[:, :, 1, :], kv))

            def rotary(layer):
                dve.wait_ge(rot_done, layer + 1)
                if layer == 0:
                    dve.wait_ge(cst_in[2], 16)
                    dve.wait_ge(cst_in[3], 16)
                step(tt(rt1, r2[:, :, :], c("cos").unsqueeze(1).to_broadcast([P, 2, TT]), ALU.mult))
                step(tt(rt2, wk[:, 2:4, 0:TT], c("sin").unsqueeze(1).to_broadcast([P, 2, TT]), ALU.mult), r2_used)
                settle()
                step(tt(r2[:, :, :], rt1, rt2, ALU.add))
                settle()
                for n in range(2):
                    step(ts(rqm[:, n, :], r2[:, 0, :], c("m2")[:, n:n + 1], None, ALU.mult))
                step(tt(kd[:, :], r2[:, 1, 0:TP], c("kdec"), ALU.mult), rqm_ready)

            def ret_decay(layer):
                dve.wait_ge(rsc_done, layer + 1)
                dec = c("decay").rearrange("p (a t) -> p a t", a=4)
                step(tt(attr[:, :, 0:TP], wk[:, 0:4, 0:TP], dec, ALU.mult))
                step(tt(attr[:, :, TP:384], wk[:, 0:4, TP:384], dec[:, :, 0:P], ALU.mult), attr_ready)

            def sample_states(layer):
                dve.wait_ge(q4_ready, layer + 1)
                for n in range(3):
                    dve.wait_ge(vb_done, layer * 3 + n + 1)
                    if n == 0:
                        a, m = 0, 2
                    else:
                        a, m = 1 + n, 1
                    for t in range(a, a + m):
                        step(tt(kvb[:, 512 * t:512 * t + 512].rearrange("p (b c) -> p b c", b=NS),
                                wk[:, t, :].rearrange("p (b c) -> p b c", b=NS),
                                k4[:, t, :].unsqueeze(2).to_broadcast([P, NS, 64]), ALU.mult),
                             vb_used if n == 2 else None)
                settle()
                dve.wait_ge(fs_ready, layer + 1)
                fl = ss[:, :, :, :].rearrange("p a b c -> p (a b c)")
                step(tt(fl, fl, kvb, ALU.add), ss_ready)

            def gather_outputs(layer):
                dve.wait_ge(vd_ready, layer * 3 + 3)
                for kind in range(3):
                    dve.wait_ge(o_done, layer * 3 + kind + 1)
                    dst, src = o[:, 2 * kind:2 * kind + 2, 0:TP], wk[:, kind, :].rearrange("p (t n) -> p t n", t=2)
                    step(tt(dst, src, dst, ALU.add) if kind < 2 else cp(dst, src), o_ready)
                dve.wait_ge(rst_done, layer + 1)
                if layer:
                    dve.wait_ge(state_out, 16 * 8 * layer)
                for hd in range(4):
                    step(cp(qrt(retf, hd), qrt(wk, hd)[:, 3, 64 * hd:64 * hd + 64]), st_ready if hd == 3 else None)
                dve.wait_ge(so_done, layer + 1)
                for hh in range(2):
                    rows = slice(64 * hh, 64 * hh + 64)
                    step(cp(o[rows, 0:2, TP:TT], wk[0:64, 4, 0:32].rearrange("p (t b h) -> p t b h", t=2, h=2)[:, :, :, hh]))
                    for n in range(2):
                        src = wk[0:64, 4, 32 + 32 * n:64 + 32 * n].rearrange("p (b t h) -> p t b h", t=2, h=2)[:, :, :, hh]
                        step(cp(o[rows, 2 + 2 * n:4 + 2 * n, TP:TT], src), o_ready if hh and n else None)

            def s5_gelu(layer):
                dve.wait_ge(y_evac, layer * 2 + 2)
                step(tt(yt2, yb, yb, ALU.mult))
                settle()
                step(ts(yt2, yt2, GELU_A, 1.0, ALU.mult, ALU.add))
                settle()
                step(tt(yt2, yt2, yb, ALU.mult), tin_ready)

            def s5_back(layer):
                dve.wait_ge(tanh_ready, layer + 1)
                step(stt(out=yb, in0=yt2, scalar=1.0, in1=yb, op0=ALU.add, op1=ALU.mult))
                settle()
                yv = yb.rearrange("p (t s k) -> p t s k", t=2, s=4)
                for a in range(4):
                    for j in range(4):
                        dst = qrt(yg, a)[:, :, 0:TP].rearrange("p t (k j) -> p t k j", j=SL)[:, :, :, j]
                        step(ts(dst, qrt(yv, j)[:, :, a, 0:SC], 0.5, None, ALU.mult))
                    step(ts(qrt(yg, a)[:, :, TP:TT], qrt(yv, 0)[:, :, a, SC:], 0.5, None, ALU.mult),
                         yg_ready if a == 3 else None)

            def s5_mix(layer):
                dve.wait_ge(glu_tanh, layer + 1)
                step(stt(out=glu[:, :, :], in0=glu[:, :, :], scalar=1.0, in1=yg[:, :, :], op0=ALU.add, op1=ALU.mult))
                settle()
                for t in range(2):
                    step(stt(out=zs[:, t, :], in0=glu[:, t, :], scalar=0.5, in1=zs[:, t, :], op0=ALU.mult, op1=ALU.mult), mix_ready)

            def center(layer):
                for t in range(2):
                    dve.wait_ge(mean_done, layer * 2 + t + 1)
                    step(tt(o[:, 4 + t, :], o[:, 4 + t, :], ring_bank(layer, NCH + t)[:, 0:TT], ALU.subtract), mean_used)

            def square_outputs(layer, part):
                settle()
                step(tt(osq[:, part, :], o[:, part, :], o[:, part, :], ALU.mult), osq_ready)

            def head_gates(layer, tiles):
                dve.wait_ge(chunk_evac, layer * NCH + NP + 2 + tiles.stop)
                settle()
                for t in tiles:
                    step(stt(out=zs[:, 2 + t, :], in0=o[:, t, :], scalar=par(Q_HEADG + layer * 6 + t), in1=zs[:, 2 + t, :],
                             op0=ALU.mult, op1=ALU.mult))

            def head_mix(layer):
                for t in range(6):
                    if t in (0, 4):
                        dve.wait_ge(ors_ready, layer * 8 + (5 if t == 0 else 8))
                        settle()
                    step(tt(zs[:, 2 + t, :], zs[:, 2 + t, :], rs[:, t, :], ALU.mult), mix_ready)
                lower_parts(2 * layer + 1)

            def residual(layer, m):
                dve.wait_ge(out_done, layer * KT + m + 1)
                step(tt(x[:, m, :], x[:, m, :], ring_bank(layer, NCH + 8 + m)[:, 0:TT], ALU.add), out_used)

            def sum_squares(layer, m):
                dve.wait_ge(sq_ready, (layer + 1) * KT + m + 1)
                settle()
                step(tt(h[:, 0, :], h[:, 0, :], h[:, m, :], ALU.add), sum_ready if m == KT - 2 else None)

            step(nc.vector.memset(ones_d[:, :], 1.0 / D), zero_ready)
            step(nc.vector.memset(sr[:, :, 0:1], 0.0))
            step(nc.vector.memset(si[:, :, 0:1], 0.0))
            settle()
            dve.wait_ge(par_in, 16)
            dve.wait_ge(cst_in[0], 16)
            s5_phases()
            for layer in range(DEPTH):
                scale_x(layer, Q_NORM + layer * KT, h_ready)
                if layer == 0:
                    lower_bounds()
                    accurate_sines()
                    s5_coefficients()
                    dve.wait_ge(set_ready, 1)
                s5_c(layer, 0)
                if layer == 0:
                    dve.wait_ge(cst_in[1], 16)
                gate(layer)
                level_diff(layer, 0)
                level_diff(layer, 1)
                dve.wait_ge(k3_ready, layer + 1)
                dve.wait_ge(chunk_evac, layer * NCH + C_GK + 1)
                step(tt(qk[:, :, 0:TP], q3[:, :, 0:TP], k3[:, :, 0:TP], ALU.mult), qv_ready)
                settle()
                level_operands(layer, 0)
                dve.wait_ge(eb_ready, layer * 2 + 2)
                step(tt(ke[:, :, 0:TP], ke[:, :, 0:TP], k3[:, :, 0:TP], ALU.mult), ke_ready)
                level_operands(layer, 1)
                settle()
                level_diff(layer, 2)
                if layer == 0:
                    dve.wait_ge(small_in, 32)
                for n in range(NL):
                    level_scores(layer, n)
                    if n == 2:
                        s5_c(layer, 1)
                    if n + 2 < NL:
                        level_operands(layer, n + 2)
                        settle()
                    if n < 2:
                        level_diff(layer, n + 3)
                rotary(layer)
                diagonal(layer)
                s5_b(layer)
                carry(layer)
                s5_chunk_angles(layer)
                s5_relay(layer)
                ret_decay(layer)
                s5_within(layer)
                s5_scan(layer)
                decayed_q(layer)
                sample_states(layer)
                s5_gelu(layer)
                s5_back(layer)
                gather_outputs(layer)
                square_outputs(layer, slice(0, 4))
                head_gates(layer, range(0, 4))
                center(layer)
                square_outputs(layer, slice(4, 6))
                s5_mix(layer)
                head_gates(layer, range(4, 6))
                head_mix(layer)
                for m in range(KT):
                    if m == KT - 1:
                        sum_squares(layer, m - 1)
                    residual(layer, m)
                    if 1 < m < KT - 1:
                        sum_squares(layer, m - 1)
            scale_x(DEPTH, Q_FINAL, fin_ready)

        @block.gpsimd
        def _(pool):
            step, settle = chain(pool, pool_step)
            tt, cp = nc.gpsimd.tensor_tensor, nc.gpsimd.tensor_copy

            def s5_samples(layer):
                L = slice(S5T * layer, S5T * layer + S5T)
                a_r = are[:, L, 1:2].to_broadcast([P, S5T, NS])
                a_i = aim[:, L, 1:2].to_broadcast([P, S5T, NS])
                s_r, s_i = s5i[:, layer, 0, :, :], s5i[:, layer, 1, :, :]
                if layer == 0:
                    pool.wait_ge(small_in, 32)
                step(tt(s5t[:, 0, :, :], s_r, a_r, ALU.mult))
                step(tt(s5t[:, 1, :, :], s_i, a_i, ALU.mult))
                step(tt(s5t[:, 2, :, :], s_r, a_i, ALU.mult))
                step(tt(s5t[:, 3, :, :], s_i, a_r, ALU.mult))
                step(cp(sr[:, :, SC:], s_r))
                step(cp(si[:, :, SC:], s_i))
                settle()
                step(tt(s5t[:, 0, :, :], s5t[:, 0, :, :], s5t[:, 1, :, :], ALU.subtract))
                step(tt(s5t[:, 2, :, :], s5t[:, 2, :, :], s5t[:, 3, :, :], ALU.add), s5s_part)

            def split_weights(last):
                for j in range(split[0], 2 * min(last + 1, DEPTH * (NCH + KT))):
                    split[0] = j + 1
                    pool.wait_ge(whi_ready, j + 1)
                    half_used(pool, j - WSLOTS)
                    step(tt(w_lo[:, j % WSLOTS, :, :], wring[:, j % RING, :, :],
                            w_hi[:, j % WSLOTS, :, :].bitcast(F32), ALU.subtract), wlo_ready)

            def lower_parts(n):
                for k in A_LO_POOL:
                    pool.wait_ge(ahi_ready, n * KT + k + 1)
                    step(tt(a_lo[:, k, :], zs[:, k, :], a_hi[:, k, :].bitcast(F32), ALU.subtract), alo_pool)

            def sample_v(layer, n):
                pool.wait_ge(chunk_evac, layer * NCH + (C_I1, C_GV1, C_RV1)[n] + 1)
                if n == 0 and layer == 0:
                    pool.wait_ge(cst_in[3], 16)
                if n == 0:
                    pool.wait_ge(lvl_done, layer * NL + NL)
                    pool.wait_ge(bb_ready, layer + 1)
                else:
                    pool.wait_ge(vb_done, layer * 3 + n)
                for t in range(2):
                    step(tt(vd[:, t, :].rearrange("p (b c) -> p b c", b=NS),
                            v[:, 2 * n + t, TP:TT].unsqueeze(2).to_broadcast([P, NS, 64]),
                            c("eye64").unsqueeze(1).to_broadcast([P, NS, 64]), ALU.mult), vd_ready if t else None)

            def sample_gates(layer):
                pool.wait_ge(eb_ready, layer * 2 + 1)
                pool.wait_ge(rqm_ready, layer + 1)
                pool.wait_ge(ss_in, 48 * (layer + 1))
                step(cp(f4[:, 0:3, :], eb[:, :, TP:TT]))
                step(cp(f4[:, 3, :], c("gamma").to_broadcast([P, NS])))
                step(cp(k4[:, 0:3, :], k3[:, :, TP:TT]))
                step(nc.gpsimd.tensor_scalar(k4[:, 3, :], r2[:, 1, TP:TT], 32 ** -0.5, None, ALU.mult))
                for t in range(2):
                    step(cp(qs_hg[:, t, :, :], qv[:, 2 * t:2 * t + 2, TP:TT].rearrange("p h b -> p b h")))
                step(cp(qs_gr[:, 0, :, :], qv[:, 4:8, TP:TT].rearrange("p h b -> p b h")))
                step(tt(qs_gr[:, 1, :, :], r2[:, 0, TP:TT].unsqueeze(2).to_broadcast([P, NS, 4]),
                        c("m32").unsqueeze(1).to_broadcast([P, NS, 4]), ALU.mult), q4_ready)
                settle()

            def decay_sample_state(layer, n):
                step(tt(ss[:, n, :, :], ss[:, n, :, :], f4[:, n, :].unsqueeze(2).to_broadcast([P, NS, 64]), ALU.mult),
                     fs_ready if n == 3 else None)

            step(nc.gpsimd.memset(att[:, :, :], 0.0))
            step(nc.gpsimd.memset(ub[:, :, :], 0.0))
            step(nc.gpsimd.memset(tmat[:, :, :], 0.0), set_ready)
            split = [0]
            for layer in range(DEPTH):
                at = layer * (NCH + KT)
                if layer == 0:
                    split_weights(0)
                lower_parts(2 * layer)
                split_weights(at + 12)
                if layer == 0:
                    for n in range(2):
                        pool.wait_ge(cst_in[n], 16)
                s5_samples(layer)
                split_weights(at + 15)
                sample_gates(layer)
                for n in range(4):
                    split_weights(at + 16 + n)
                    decay_sample_state(layer, n)
                sample_v(layer, 0)
                split_weights(at + 23)
                sample_v(layer, 1)
                split_weights(at + 24)
                sample_v(layer, 2)
                split_weights(at + 26)
                lower_parts(2 * layer + 1)
                split_weights(at + NCH + KT)


_OUTS = [("y", (P, KT, TT)), ("s5p", (DEPTH, P, 2, S5T)), ("hgp", (DEPTH, P, 2, 64)), ("glap", (DEPTH, P, 64)),
         ("retp", (DEPTH, P, 64)), ("s5s", (DEPTH, P, 2, S5T, NS)), ("hgs", (DEPTH, P, 2, NS, 64)),
         ("glas", (DEPTH, P, NS, 64)), ("rets", (DEPTH, P, NS, 64))]


def layouts(d):
    f = {k: np.ascontiguousarray(a) for k, a in d.items()}
    L = DEPTH
    out = {}
    xa = np.concatenate([f["x_prompt"][0], f["x_sample"][:, 0]], 0)
    out["xt"] = xa.reshape(TT, KT, P).transpose(2, 1, 0)
    w = f["w_in"]
    wi = np.zeros((L, NCH, P, KT, P), np.float32)
    for i, col in enumerate(CHUNKS):
        n = 16 if i == C_LR else P
        wi[:, i, :, :, 0:n] = w[:, :, col:col + n].reshape(L, KT, P, n).transpose(0, 2, 1, 3)
    out["w_in"] = wi
    out["w_out"] = f["w_out"].reshape(L, KT, P, KT, P).transpose(0, 3, 2, 1, 4)

    def tiles(a, n):
        return a.reshape(-1, P).T

    def s5(a):
        return a.reshape(L * S5T, P).T

    heads = np.stack([f["hgrn_norm_w"].reshape(L, 2, P), f["gla_norm_w"].reshape(L, 2, P),
                      f["ret_norm_w"].reshape(L, 2, P)], 1)
    skip = np.tile(f["s5_d"].reshape(L, S5T, 1, 32), (1, 1, 4, 1))
    step = np.repeat(f["s5_log_step"][:, :, None], 64, 2)
    out["par"] = np.concatenate([
        tiles(f["norm_w"], KT), tiles(f["final_norm_w"], KT), tiles(f["hgrn_lb_logits"], 2), tiles(f["gla_b_gate"], 1),
        tiles(heads, 6), tiles(skip, 8), s5(f["s5_lam_re"]), s5(f["s5_lam_im"]), s5(step)], 1)
    m = np.zeros((L, P, 4, S5T, 32), np.float32)
    for i, name in enumerate(("s5_b_re", "s5_b_im", "s5_c_re", "s5_c_im")):
        a = f[name] if i < 2 else f[name].transpose(0, 1, 3, 2)
        a = a.reshape(L, S5T, 2, 64, 16)
        for g in range(2):
            m[:, 64 * g:64 * g + 64, i, :, 16 * g:16 * g + 16] = a[:, :, g].transpose(0, 2, 1, 3)
    out["s5m"] = m
    out["w_glu"] = f["s5_w_glu"].reshape(L, 2, P, 2, P).transpose(0, 2, 1, 3, 4)
    out["w_up"] = f["gla_w_gate_up"].transpose(1, 0, 2)
    s5s = np.stack([f["state_s5_re"], f["state_s5_im"]], 1).reshape(L, 2, NS, S5T, P)
    out["s5_in"] = s5s.transpose(4, 0, 1, 3, 2)
    out["hg_in"] = f["state_hgrn"].reshape(L, NS, 2, P, 64).transpose(0, 3, 2, 1, 4)
    out["gla_in"] = f["state_gla"].reshape(L, NS, P, 64).transpose(0, 2, 1, 3)
    out["ret_in"] = f["state_ret"].reshape(L, NS, P, 64).transpose(0, 2, 1, 3)
    out["cst"], out["msk"] = constants()
    return {k: np.ascontiguousarray(a) for k, a in out.items()}


def kernel(**inputs):
    import concourse.bacc as bacc
    from concourse.bass_utils import run_bass_kernel_spmd

    nc = bacc.Bacc("TRN2", target_bir_lowering=False, num_devices=1)
    arrays = {"in_" + k: a for k, a in layouts(inputs).items()}
    args = [nc.dram_tensor(k, a.shape, mybir.dt.from_np(a.dtype), kind="ExternalInput").ap() for k, a in arrays.items()]
    args += [nc.dram_tensor("out_" + k, shape, F32, kind="ExternalOutput").ap() for k, shape in _OUTS]
    build(nc, *args)
    r = run_bass_kernel_spmd(nc, [arrays], core_ids=[0]).results[0]
    r = {k: np.asarray(r["out_" + k]) for k, _ in _OUTS}
    L = DEPTH
    y = r["y"].transpose(2, 1, 0).reshape(TT, D)
    s5p = r["s5p"].transpose(0, 2, 3, 1).reshape(L, 2, 1, 16, 64)
    s5s = r["s5s"].transpose(0, 2, 4, 3, 1).reshape(L, 2, NS, 16, 64)
    return (y[0:TP].reshape(1, TP, D), y[TP:].reshape(NS, 1, D),
            s5p[:, 0], s5p[:, 1],
            r["hgp"].transpose(0, 2, 1, 3).reshape(L, 1, 4, 64, 64),
            r["glap"].reshape(L, 1, 4, 32, 64), r["retp"].reshape(L, 1, 4, 32, 64),
            s5s[:, 0], s5s[:, 1],
            r["hgs"].transpose(0, 3, 2, 1, 4).reshape(L, NS, 4, 64, 64),
            r["glas"].transpose(0, 2, 1, 3).reshape(L, NS, 4, 32, 64),
            r["rets"].transpose(0, 2, 1, 3).reshape(L, NS, 4, 32, 64))
```
